# Optimizing a Trainium2 kernel written in Bass

```python
import jax, jax.numpy as jnp
from jax import lax
import numpy as np

D_MODEL = 1024
BATCH = 1
SEQ = 512
DEPTH = 2
DEC_BATCH = 1
DEC_SEQ = 64
PAST_LEN = 1024

CHUNK = 64
MIX = D_MODEL
A_HEADS = 8
A_KV_HEADS = 2
A_HEAD_DIM = (MIX // 2) // A_HEADS
WINDOW = 128
WINDOW_CHUNKS = WINDOW // CHUNK
ROPE_THETA = 500000.0
ROPE_DIM = A_HEAD_DIM // 4
M_HEADS = 4
M_HEAD_DIM = (MIX // 2) // M_HEADS
D_FF = 4 * D_MODEL
NORM_EPS = 1e-6
NEG = -1e30
A_Q = A_HEADS * A_HEAD_DIM
A_KV = A_KV_HEADS * A_HEAD_DIM
M_W = M_HEADS * M_HEAD_DIM
IN_COLS = A_Q + 2 * A_KV + 4 * M_W + 2 * M_HEADS

kernel_name = 'hymba_mlstm_swa_sink_streaming_step'

def rmsnorm(x, g):
    xf = x.astype(jnp.float32)
    r = lax.rsqrt(jnp.mean(xf * xf, axis=-1, keepdims=True) + NORM_EPS)
    return (xf * r * g.astype(jnp.float32)).astype(x.dtype)

def partial_rotary(x, pos):
    half = ROPE_DIM // 2
    inv = ROPE_THETA ** (-(jnp.arange(half, dtype=jnp.float32) * 2.0 / ROPE_DIM))
    ang = pos[:, None] * inv[None, :]
    cos = jnp.cos(ang)[None, :, None, :]
    sin = jnp.sin(ang)[None, :, None, :]
    xf = x.astype(jnp.float32)
    x1 = xf[..., :half]
    x2 = xf[..., half:ROPE_DIM]
    out = jnp.concatenate([x1 * cos - x2 * sin, x2 * cos + x1 * sin, xf[..., ROPE_DIM:]], axis=-1)
    return out.astype(x.dtype)

def sink_attention(q, k, v, valid, sink):
    B, N, Lq, H, d = q.shape
    G = k.shape[3]
    R = H // G
    qf = q.astype(jnp.float32).reshape(B, N, Lq, G, R, d)
    s = jnp.einsum('bnqgrd,bnkgd->bngrqk', qf, k.astype(jnp.float32)) * (d ** -0.5)
    s = jnp.where(valid[None, :, None, None, None, :], s, NEG)
    sk = sink.astype(jnp.float32).reshape(1, 1, G, R, 1, 1)
    mx = jnp.maximum(jnp.max(s, axis=-1, keepdims=True), sk)
    p = jnp.exp(s - mx)
    p = p / (jnp.sum(p, axis=-1, keepdims=True) + jnp.exp(sk - mx))
    o = jnp.einsum('bngrqk,bnkgd->bnqgrd', p, v.astype(jnp.float32))
    return o.reshape(B, N, Lq, H * d)

def banded_prompt_attention(q, k, v, sink):
    B, T, H, d = q.shape
    NC = T // CHUNK
    P = WINDOW_CHUNKS * CHUNK
    pad = ((0, 0), (P, 0), (0, 0), (0, 0))
    kc = jnp.pad(k, pad).reshape(B, NC + WINDOW_CHUNKS, CHUNK, A_KV_HEADS, d)
    vc = jnp.pad(v, pad).reshape(B, NC + WINDOW_CHUNKS, CHUNK, A_KV_HEADS, d)
    kb = jnp.concatenate([kc[:, j:j + NC] for j in range(WINDOW_CHUNKS + 1)], axis=2)
    vb = jnp.concatenate([vc[:, j:j + NC] for j in range(WINDOW_CHUNKS + 1)], axis=2)
    key_pos = (jnp.arange(NC)[:, None] - WINDOW_CHUNKS) * CHUNK + jnp.arange((WINDOW_CHUNKS + 1) * CHUNK)[None, :]
    valid = key_pos >= 0
    o = sink_attention(q.reshape(B, NC, CHUNK, H, d), kb, vb, valid, sink)
    return o.reshape(B, T, H * d)

def sample_attention(q, k_new, v_new, k_cache, v_cache, sink):
    B, S, H, d = q.shape
    kk = jnp.concatenate([k_cache.astype(k_new.dtype), k_new], axis=1)[:, None]
    vv = jnp.concatenate([v_cache.astype(v_new.dtype), v_new], axis=1)[:, None]
    valid = jnp.ones((1, kk.shape[2]), dtype=bool)
    o = sink_attention(q[:, None], kk, vv, valid, sink)
    return o.reshape(B, S, H * d)

def mlstm_chunkwise(q, k, v, ig, lf, C0, n0, m0, L):
    B, T, H, d = q.shape
    NC = T // L

    def blk(a):
        return a.astype(jnp.float32).reshape(B, NC, L, H, d).transpose(1, 0, 3, 2, 4)

    def gblk(a):
        return a.astype(jnp.float32).reshape(B, NC, L, H).transpose(1, 0, 3, 2)

    causal = jnp.tril(jnp.ones((L, L), dtype=bool))

    def step(carry, xs):
        C, n, m = carry
        qc, kc, vc, ic, fc = xs
        b = jnp.cumsum(fc, axis=-1)
        D = b[..., :, None] - b[..., None, :] + ic[..., None, :]
        D = jnp.where(causal, D, NEG)
        inter = b + m[..., None]
        mt = jnp.maximum(inter, jnp.max(D, axis=-1))
        S = jnp.einsum('bhtd,bhsd->bhts', qc, kc) * jnp.exp(D - mt[..., None])
        w_inter = jnp.exp(inter - mt)
        num = jnp.einsum('bhts,bhsd->bhtd', S, vc) + w_inter[..., None] * jnp.einsum('bhvk,bhtk->bhtv', C, qc)
        den = jnp.sum(S, axis=-1) + w_inter * jnp.einsum('bhk,bhtk->bht', n, qc)
        h = num / jnp.maximum(jnp.abs(den), jnp.exp(-mt))[..., None]
        mL = mt[..., -1]
        ws = jnp.exp(b[..., -1:] - b + ic - mL[..., None])
        decay = jnp.exp(b[..., -1] + m - mL)
        C_new = decay[..., None, None] * C + jnp.einsum('bhs,bhsv,bhsk->bhvk', ws, vc, kc)
        n_new = decay[..., None] * n + jnp.einsum('bhs,bhsk->bhk', ws, kc)
        return (C_new, n_new, mL), h

    carry0 = (C0.astype(jnp.float32), n0.astype(jnp.float32), m0.astype(jnp.float32))
    (C, n, m), hs = lax.scan(step, carry0, (blk(q), blk(k), blk(v), gblk(ig), gblk(lf)))
    h = hs.transpose(1, 0, 3, 2, 4).reshape(B, T, H, d)
    return h, C, n, m

def layer(x, pos, C0, n0, m0, k_cache, v_cache, chunk_len,
          g1, w_in, gate_b, sink, mnorm_g, w_out, g2, w_up, w_down):
    B, T, _ = x.shape
    h = rmsnorm(x, g1)
    z = h @ w_in
    sizes = [A_Q, A_KV, A_KV, M_W, M_W, M_W, M_W, M_HEADS]
    idx = [int(s) for s in np.cumsum(sizes)]
    aq, ak, av, mq, mk, mv, mo, mi, mf = jnp.split(z, idx, axis=-1)
    aq = partial_rotary(aq.reshape(B, T, A_HEADS, A_HEAD_DIM), pos)
    ak = partial_rotary(ak.reshape(B, T, A_KV_HEADS, A_HEAD_DIM), pos)
    av = av.reshape(B, T, A_KV_HEADS, A_HEAD_DIM)
    if k_cache is None:
        attn = banded_prompt_attention(aq, ak, av, sink)
        k_rows = ak[:, -WINDOW:]
        v_rows = av[:, -WINDOW:]
    else:
        attn = sample_attention(aq, ak, av, k_cache, v_cache, sink)
        k_rows = ak
        v_rows = av
    gb = gate_b.astype(jnp.float32)
    ig = mi.astype(jnp.float32) + gb[:M_HEADS]
    lf = jax.nn.log_sigmoid(mf.astype(jnp.float32) + gb[M_HEADS:])
    hm, C, n, m = mlstm_chunkwise(
        mq.reshape(B, T, M_HEADS, M_HEAD_DIM),
        mk.reshape(B, T, M_HEADS, M_HEAD_DIM) * (M_HEAD_DIM ** -0.5),
        mv.reshape(B, T, M_HEADS, M_HEAD_DIM),
        ig, lf, C0, n0, m0, chunk_len)
    hm = rmsnorm(hm, mnorm_g.reshape(M_HEADS, M_HEAD_DIM)).reshape(B, T, M_W)
    hm = hm * jax.nn.sigmoid(mo.astype(jnp.float32))
    mix = jnp.concatenate([attn.astype(x.dtype), hm.astype(x.dtype)], axis=-1)
    x = x + mix @ w_out
    u = rmsnorm(x, g2) @ w_up
    x = x + jnp.square(jax.nn.relu(u)) @ w_down
    return x, k_rows, v_rows, C, n, m

def setup_inputs(seed: int = 0) -> dict:
    key = jax.random.key(seed)
    ks = jax.random.split(key, 20)
    f32 = jnp.float32
    nrm = lambda k, s: jax.random.normal(k, s, dtype=f32)
    gate_b = jnp.concatenate([
        0.1 * nrm(ks[9], (DEPTH, M_HEADS)),
        jnp.linspace(3.0, 6.0, M_HEADS, dtype=f32)[None, :] + 0.1 * nrm(ks[10], (DEPTH, M_HEADS))], axis=-1)
    return {
        'x_prompt': nrm(ks[0], (BATCH, SEQ, D_MODEL)),
        'x_sample': nrm(ks[1], (DEC_BATCH, DEC_SEQ, D_MODEL)),
        'cache_k': nrm(ks[2], (DEPTH, DEC_BATCH, WINDOW, A_KV_HEADS, A_HEAD_DIM)),
        'cache_v': nrm(ks[3], (DEPTH, DEC_BATCH, WINDOW, A_KV_HEADS, A_HEAD_DIM)),
        'state_C': 0.1 * nrm(ks[4], (DEPTH, DEC_BATCH, M_HEADS, M_HEAD_DIM, M_HEAD_DIM)),
        'state_n': 0.1 * nrm(ks[5], (DEPTH, DEC_BATCH, M_HEADS, M_HEAD_DIM)),
        'state_m': 0.5 * nrm(ks[6], (DEPTH, DEC_BATCH, M_HEADS)),
        'norm1_g': 1.0 + 0.02 * nrm(ks[7], (DEPTH, D_MODEL)),
        'w_in': nrm(ks[8], (DEPTH, D_MODEL, IN_COLS)) * D_MODEL ** -0.5,
        'gate_b': gate_b,
        'attn_sink': 0.5 * nrm(ks[11], (DEPTH, A_HEADS)),
        'mnorm_g': 1.0 + 0.02 * nrm(ks[12], (DEPTH, M_W)),
        'w_out': nrm(ks[13], (DEPTH, MIX, D_MODEL)) * MIX ** -0.5,
        'norm2_g': 1.0 + 0.02 * nrm(ks[14], (DEPTH, D_MODEL)),
        'w_up': nrm(ks[15], (DEPTH, D_MODEL, D_FF)) * D_MODEL ** -0.5,
        'w_down': nrm(ks[16], (DEPTH, D_FF, D_MODEL)) * D_FF ** -0.5,
        'final_g': 1.0 + 0.02 * nrm(ks[17], (D_MODEL,)),
    }

def reference(x_prompt, x_sample, cache_k, cache_v, state_C, state_n, state_m,
              norm1_g, w_in, gate_b, attn_sink, mnorm_g, w_out, norm2_g, w_up, w_down, final_g):
    Bp, T, _ = x_prompt.shape
    Bs, S, _ = x_sample.shape
    pos_p = jnp.arange(T, dtype=jnp.float32)
    pos_s = jnp.arange(S, dtype=jnp.float32) + float(PAST_LEN)
    zC = jnp.zeros((Bp, M_HEADS, M_HEAD_DIM, M_HEAD_DIM), jnp.float32)
    zn = jnp.zeros((Bp, M_HEADS, M_HEAD_DIM), jnp.float32)
    zm = jnp.zeros((Bp, M_HEADS), jnp.float32)
    yp, ys = x_prompt, x_sample
    pk, pv, pC, pn, pm = [], [], [], [], []
    sk, sv, sC, sn, sm = [], [], [], [], []
    for l in range(DEPTH):
        w = (norm1_g[l], w_in[l], gate_b[l], attn_sink[l], mnorm_g[l], w_out[l], norm2_g[l], w_up[l], w_down[l])
        yp, k_r, v_r, C, n, m = layer(yp, pos_p, zC, zn, zm, None, None, CHUNK, *w)
        pk.append(k_r); pv.append(v_r); pC.append(C); pn.append(n); pm.append(m)
        ys, k_r, v_r, C, n, m = layer(ys, pos_s, state_C[l], state_n[l], state_m[l], cache_k[l], cache_v[l], S, *w)
        sk.append(k_r); sv.append(v_r); sC.append(C); sn.append(n); sm.append(m)
    y_prompt = rmsnorm(yp, final_g)
    y_sample = rmsnorm(ys, final_g)
    return (y_prompt, y_sample,
            jnp.stack(pk), jnp.stack(pv), jnp.stack(pC), jnp.stack(pn), jnp.stack(pm),
            jnp.stack(sk), jnp.stack(sv), jnp.stack(sC), jnp.stack(sn), jnp.stack(sm))


_drawn_inputs = setup_inputs


def setup_inputs(seed=0):
    import zlib

    import numpy as np

    out = dict(_drawn_inputs(seed))
    spreads = {}
    factors = {'attn_sink': 8.0, 'mnorm_g': 5.29, 'final_g': 8.245, 'norm2_g': 2.972}
    for name, (base, spread) in spreads.items():
        noise = np.random.default_rng([zlib.crc32(name.encode()), seed]).standard_normal(out[name].shape)
        drawn = base * np.exp(spread * noise) if base else spread * noise
        out[name] = __import__('jax').numpy.asarray(drawn.astype(out[name].dtype))
    for name, factor in factors.items():
        out[name] = (out[name] * factor).astype(out[name].dtype)
    return out
```

```python
from contextlib import ExitStack

import concourse.bass as bass
from concourse import mybir

F32 = mybir.dt.float32
F32R = mybir.dt.float32r
ALU = mybir.AluOpType
ACT = mybir.ActivationFunctionType
AX = mybir.AxisListType

P = 128
DM = 1024
KT = DM // P
SEQ, DEC = 512, 64
T = SEQ + DEC
HALF = T // 2
DEPTH = 2
L = 64
NC = T // L
SAMPLE = NC - 1
WIN = 128
AH, AG, AD = 8, 2, 64
AJ = AH // AG
MH, MD = 4, 128
AQ, AKV, MW = AH * AD, AG * AD, MH * MD
COL_K, COL_V = AQ, AQ + AKV
COL_MQ = AQ + 2 * AKV
COL_MK, COL_MV, COL_MO = COL_MQ + MW, COL_MQ + 2 * MW, COL_MQ + 3 * MW
COL_GATE = COL_MQ + 4 * MW
FF = 4 * DM
GROUPS = FF // DM
EPS = 1e-6
A_SCALE = float(AD) ** -0.5
K_SCALE = float(MD) ** -0.5
ROPE_DIM = AD // 4
PAST = 1024

S_GATE = 0
S_AK, S_AV = 1, 2
S_AQ = 3
S_MK, S_MQ, S_MV, S_MO = 7, 11, 15, 19
S_WOA, S_WOM = 23, 27
S_MLP = 31
SLOTS = S_MLP + GROUPS * 2 * KT
TILES = SLOTS + 8
PAIRS = 1 + (SLOTS - 1) // 2

C_ID, C_ONE, C_COS, C_SIN = 0, 128, 256, 832
C_R = 1408
R_SEL, R_ROW, R_NEG, R_ID = 0, 1024, 1280, 1536
R_COLS = 1664


def constants():
    import numpy as np
    c = np.zeros((P, C_R + R_COLS), np.float32)
    c[:, C_ID:C_ID + P] = np.eye(P)
    c[:, C_ONE:C_ONE + P] = 1.0
    half = ROPE_DIM // 2
    inv = np.float32(500000.0) ** (-(np.arange(half, dtype=np.float32) * np.float32(2.0) / np.float32(ROPE_DIM)))
    pos = np.concatenate([np.arange(SEQ), np.arange(DEC) + PAST]).astype(np.float32)
    ang = inv.astype(np.float32)[:, None] * pos[None, :]
    c[:, C_COS:C_COS + T] = 1.0
    for g in range(AG):
        a = g * AD
        c[a:a + half, C_COS:C_COS + T] = np.cos(ang)
        c[a + half:a + 2 * half, C_COS:C_COS + T] = np.cos(ang)
        c[a:a + half, C_SIN:C_SIN + T] = -np.sin(ang)
        c[a + half:a + 2 * half, C_SIN:C_SIN + T] = np.sin(ang)
    r = c[:, C_R:]
    for h in range(MH):
        for which, base in ((h, 0), (MH + h, 64)):
            r[base + h, R_SEL + which * P:R_SEL + (which + 1) * P] = 1.0
            r[base + 32 + h, R_SEL + which * P:R_SEL + (which + 1) * P] = 1.0
        r[h, R_ROW + h * L:R_ROW + (h + 1) * L] = 1.0
        r[32 + h, R_ROW + h * L:R_ROW + (h + 1) * L] = 1.0
        r[:L, R_NEG + h * L:R_NEG + (h + 1) * L] = np.tril(np.full((L, L), -1e30, np.float32), -1)
    r[:L, R_ID:R_ID + L] = np.eye(L)
    return c


A_FILL = (8, 3, 3)
M_FILL = (1, 1, 1, 1)


def hymba_step(nc, inputs, outs):
    (x_prompt, x_sample, cache_k, cache_v, state_C, state_n, state_m, norm1_g, w_in, gate_b,
     attn_sink, mnorm_g, w_out, norm2_g, w_up, w_down, final_g, const) = inputs
    (y_prompt, y_sample, p_k, p_v, p_C, p_n, p_m, s_k, s_v, s_C, s_n, s_m) = outs

    with ExitStack() as ctx:
        def sem(name):
            return ctx.enter_context(nc.semaphore(name))

        base = (nc.sbuf_base + 63) // 64 * 64
        top = [base]

        def place(name, shape, dt=F32, where=None):
            size = 4
            for n in shape[1:]:
                size *= n
            off = top[0] if where is None else where
            if where is None:
                top[0] += (size + 31) // 32 * 32
                assert top[0] <= nc.sbuf_usable_end, (name, top[0] - nc.sbuf_usable_end)
            return nc.alloc_sbuf_tensor_at(name, shape, dt, offset=off)

        x = place("x", [P, KT, T])
        xh = place("xh", [P, KT, T], F32R)
        xl = place("xl", [P, KT, T], F32R)
        hh_off = top[0]
        hid_h = place("hid_h", [P, KT, T], F32R)
        hl_off = top[0]
        hid_l = place("hid_l", [P, KT, T], F32R)
        upper = 4 * T * 4
        qbd = [place("qbd_a", [P, 2, NC, AG, L], where=hh_off + upper),
               place("qbd_b", [P, 2, NC, AG, L], where=hl_off + upper)]
        z = place("z", [P, 4 * MH, T])
        kT = place("kT", [P, T])
        vT = place("vT", [P, T])
        rms = place("rms", [P, T])
        ssum = place("ssum", [P, T])
        tmp = [place(f"tmp{i}", [P, T]) for i in range(3)]
        sqr = tmp[2]
        stage = place("stage", [P, 2, KT * 2 * P])
        w_hi = place("w_hi", [P, 2, KT * P], F32R)
        w_lo = place("w_lo", [P, 2, KT * P], F32R)
        io = place("io", [P, 2 * P])
        ident, ones = io[:, 0:P], io[:, P:2 * P]
        rconst = place("rconst", [P, R_COLS], F32R)
        bcr = place("bcr", [P, T], F32R)
        ncr = place("ncr", [P, T], F32R)
        acl = place("acl", [P, T + L], F32R)
        gains = place("gains", [P, 56])
        cst = place("cst", [P, 2, MH, MD])
        nst = place("nst", [P, 2, MH])
        g9 = place("g9", [P, 6 * 16])
        gT = place("gT", [P, 2, NC * MH])
        small = place("small", [P, 64])
        kout = place("kout", [P, 2, P])
        arena = top[0]
        vwin = place("vwin", [P, NC, P])
        kcT = place("kcT", [P, WIN])
        kraw = place("kraw", [P, WIN])
        vcache = place("vcache", [P, WIN])
        prob = place("prob", [P, AJ, WIN + L])
        pT1 = place("pT1", [P, AJ * P])
        pT2 = place("pT2", [L, AJ * P])
        end = top[0]
        top[0] = arena
        ktok = place("ktok", [L, MH, MD])
        vtok = place("vtok", [L, MH, MD])
        wsv = place("wsv", [L, MH, MD])
        eexp = place("eexp", [L, MH, L])
        sw = place("sw", [L, MH, L])
        qw = place("qw", [P, MH, L])
        nq = place("nq", [P, MH, L])
        dena = place("dena", [P, MH, L])
        hsq = place("hsq", [P, MH, L])
        rstd = place("rstd", [P, MH, L])
        top[0] = max(top[0], end)
        cout = place("cout", [P, 2, MH * MD], where=arena)

        def row(i, q=0):
            return z[32 * q:32 * q + MH, 8 + i, :]

        eps_col = small[:, 0:1]
        sink_c = [small[:, 8 + AJ * l:8 + AJ * (l + 1)] for l in range(DEPTH)]
        nsink_c = [small[:, 16 + AJ * l:16 + AJ * (l + 1)] for l in range(DEPTH)]
        bi_c = [small[0:MH, 24 + l:25 + l] for l in range(DEPTH)]
        ms_c = [small[0:MH, 26 + l:27 + l] for l in range(DEPTH)]
        bf_c = [small[32:32 + MH, 24 + l:25 + l] for l in range(DEPTH)]
        att_s = small[:, 32:64]

        def gain(n, k):
            r = 2 * DEPTH if n == 2 * DEPTH else n // 2 + (DEPTH if n % 2 else 0)
            return gains[:, r * KT + k:r * KT + k + 1]

        psum = ctx.enter_context(nc.psum_tensor("psum", [P, 8, 512], F32))
        acc = [psum[:, 2 * i:2 * i + 2, 0:HALF] for i in range(2)]
        two = lambda ap: ap.rearrange("p (a t) -> p a t", a=2)

        s_par, s_xin, s_const = sem("s_par"), sem("s_xin"), sem("s_const")
        s_ld = [sem("s_ld0"), sem("s_ld1")]
        s_hi, s_lo = sem("s_hi"), sem("s_lo")
        s_gz = sem("s_gz")
        s_tile = sem("s_tile")
        s_evac = sem("s_evac")
        s_x0, s_xs = sem("s_x0"), sem("s_xs")
        s_gain, s_rcon = sem("s_gain"), sem("s_rcon")
        s_xT = sem("s_xT")
        s_xh, s_xl = sem("s_xh"), sem("s_xl")
        s_sum, s_ss, s_rms = sem("s_sum"), sem("s_ss"), sem("s_rms")
        s_hh, s_hidh, s_hid = sem("s_hh"), sem("s_hidh"), sem("s_hid")
        s_dve, s_act, s_pool = sem("s_dve"), sem("s_act"), sem("s_pool")
        s_rot = sem("s_rot")
        s_tab = sem("s_tab")
        s_gf, s_g1, s_g2, s_g3, s_g4 = sem("s_gf"), sem("s_g1"), sem("s_g2"), sem("s_g3"), sem("s_g4")
        s_moz, s_moe = sem("s_moz"), sem("s_moe")
        s_cl = sem("s_cl")
        s_set, s_seta, s_setd, s_set2 = sem("s_set"), sem("s_seta"), sem("s_setd"), sem("s_set2")
        s_setd2 = sem("s_setd2")
        s_sc, s_neg, s_sn, s_p, s_pn = sem("s_sc"), sem("s_neg"), sem("s_sn"), sem("s_p"), sem("s_pn")
        s_T, s_pt1, s_pt2, s_pv = sem("s_T"), sem("s_pt1"), sem("s_pt2"), sem("s_pv")
        s_aoh, s_ao = sem("s_aoh"), sem("s_ao")
        s_tk, s_swp, s_e, s_kev, s_ex = sem("s_tk"), sem("s_swp"), sem("s_e"), sem("s_kev"), sem("s_ex")
        s_tv, s_vev, s_sw, s_wv, s_nd = sem("s_tv"), sem("s_vev"), sem("s_sw"), sem("s_wv"), sem("s_nd")
        s_abs, s_h, s_u, s_st, s_hsq = sem("s_abs"), sem("s_h"), sem("s_u"), sem("s_st"), sem("s_hsq")
        s_ssm, s_rs, s_hm, s_hmh, s_hmd = sem("s_ssm"), sem("s_rs"), sem("s_hm"), sem("s_hmh"), sem("s_hmd")
        s_ct, s_co = sem("s_ct"), sem("s_co")
        s_y, s_yt, s_ye = sem("s_y"), sem("s_yt"), sem("s_ye")
        s_kvo, s_mo, s_cno, s_yo = sem("s_kvo"), sem("s_mo"), sem("s_cno"), sem("s_yo")

        def tile_of(s):
            return s if s < S_WOA else (S_WOA + 2 * (s - S_WOA) if s < S_MLP else s + 8)

        def end_tile(g):
            return TILES * (g // SLOTS) + tile_of(g % SLOTS + 1)

        landed, got = {}, [0, 0]
        for n in range(PAIRS * DEPTH):
            got[n % 2] += 16 * {2: 4, 3: 4, 12: 2, 13: 2}.get(n % PAIRS, 1)
            landed[n] = got[n % 2]

        fills = {}

        def plan_fills(kind, first, last, counts):
            u = first
            for c in range(NC):
                for i, n in enumerate(counts):
                    fills[kind, c, i] = (u, min(u + n, last))
                    u = min(u + n, last)
            fills[kind, NC, 0] = (u, last)

        plan_fills("a", 8 * S_MK, 8 * S_WOA, A_FILL)
        plan_fills("m", 8 * S_WOA, 8 * S_WOM, M_FILL)

        def slots_done(kind, c, i):
            a, b = fills[kind, c, i]
            return range(-(-(a + 1) // 8) - 1, b // 8) if b > a else range(0)

        def x_ready(n, k):
            if n == 0:
                return s_x0, k + 1
            l, second = (n - 1) // 2, n % 2
            return s_evac, TILES * l + (S_WOA + 8 if second else TILES - 8) + k + 1

        def keys(c):
            return WIN + L if c >= 2 else (c + 1) * L

        def n_pt1(l, c):
            return (NC - 1) * l + max(c - 1, 0)

        def n_pt2(l, c):
            return (NC - 1) * l + (c if c < 2 else c - 1)

        block = ctx.enter_context(nc.Block())

        @block.sync
        def _(sp):
            sp.dma_start(io[:], const[:, C_ID:C_ID + 2 * P]).then_inc(s_const, 16)
            zf = z[:, :, :].rearrange("p a t -> p (a t)")
            for t in range(SEQ // P):
                sp.dma_start(zf[:, t * DM:(t + 1) * DM], x_prompt[0, t * P:(t + 1) * P, :]).then_inc(s_xin, 16)
            sp.dma_start(zf[0:DEC, 4 * DM:5 * DM], x_sample[0]).then_inc(s_xin, 16)
            for l in range(DEPTH):
                for p in range(S_MLP // 2 + 1):
                    n = PAIRS * l + p
                    if n >= 2:
                        sp.wait_ge(s_lo, SLOTS * ((n - 2) // PAIRS) + 2 * ((n - 2) % PAIRS) + 1)
                    dst = stage[:, n % 2, :]
                    if p == 0:
                        sp.dma_start(dst[:, 0:8 * KT].rearrange("p (k c) -> p k c", k=KT),
                                     w_in[l, :, COL_GATE:].rearrange("(k p) c -> p k c", p=P)).then_inc(s_ld[n % 2], 16)
                    elif p in (2, 3):
                        d5 = dst.rearrange("p (k q g c) -> p k q g c", k=KT, q=2, g=AG)
                        for q in range(2):
                            for g in range(AG):
                                col = g * AJ * AD + (2 * (p - 2) + q) * AD
                                sp.dma_start(d5[:, :, q, g, :], w_in[l, :, col:col + AD].rearrange(
                                    "(k p) c -> p k c", p=P)).then_inc(s_ld[n % 2], 16)
                    elif p < 12:
                        col = COL_K if p == 1 else (COL_MK, COL_MQ, COL_MV, COL_MO)[(p - 4) // 2] + (p % 2) * 2 * P
                        sp.dma_start(dst.rearrange("p (k c) -> p k c", k=KT),
                                     w_in[l, :, col:col + 2 * P].rearrange("(k p) c -> p k c", p=P)).then_inc(s_ld[n % 2], 16)
                    else:
                        cols = slice((p % 2) * 4 * P, (p % 2 + 1) * 4 * P)
                        d3 = dst.rearrange("p (k c) -> p k c", k=AJ)
                        if p < 14:
                            for g in range(AG):
                                sp.dma_start(d3[g * AD:(g + 1) * AD], w_out[l, g * AJ * AD:(g + 1) * AJ * AD, cols].rearrange(
                                    "(j p) c -> p j c", p=AD)).then_inc(s_ld[n % 2], 16)
                        else:
                            sp.dma_start(d3, w_out[l, AQ:, cols].rearrange("(k p) c -> p k c", p=P)).then_inc(s_ld[n % 2], 16)
                free0 = SLOTS * l + S_MLP - 2
                with sp.Fori(0, GROUPS) as g:
                    with sp.Fori(0, 2) as i:
                        for q in range(2):
                            sp.wait_ge(s_lo, free0 + 16 * g + 4 * i + 2 * q)
                            sp.dma_start(stage[:, q, :].rearrange("p (k c) -> p k c", k=KT),
                                         w_up[l, :, bass.ds(g * DM + i * 4 * P + q * 2 * P, 2 * P)].rearrange(
                                             "(k p) c -> p k c", p=P)).then_inc(s_ld[q], 16)
                    with sp.Fori(0, 2) as i:
                        for q in range(2):
                            sp.wait_ge(s_lo, free0 + 8 + 16 * g + 4 * i + 2 * q)
                            sp.dma_start(stage[:, q, :].rearrange("p (k c) -> p k c", k=KT),
                                         w_down[l, bass.ds(g * DM, DM), bass.ds(i * 4 * P + q * 2 * P, 2 * P)].rearrange(
                                             "(k p) c -> p k c", p=P)).then_inc(s_ld[q], 16)

        @block.gpsimd
        def _(pool):
            chain = [0]

            def link(ins):
                chain[0] += 1
                ins.then_inc(s_pool, 1)
                pool.wait_ge(s_pool, chain[0])

            def squares(n):
                if n:
                    pool.wait_ge(s_ss, n)
                for k in range(KT):
                    pool.wait_ge(*x_ready(n, k))
                    if k == 0:
                        link(nc.gpsimd.tensor_tensor(ssum[:], x[:, k, :], x[:, k, :], ALU.mult))
                    else:
                        link(nc.gpsimd.tensor_tensor(sqr[:], x[:, k, :], x[:, k, :], ALU.mult))
                        last = nc.gpsimd.tensor_tensor(ssum[:], ssum[:], sqr[:], ALU.add)
                        if k < KT - 1:
                            link(last)
                last.then_inc(s_sum, 1)

            squares(0)
            for l in range(DEPTH):
                for c in range(NC):
                    pool.wait_ge(s_vev, NC * l + c + 1)
                    w = gT[0:L, 0, c * MH:(c + 1) * MH].rearrange("p (h o) -> p h o", o=1).to_broadcast([L, MH, MD])
                    nc.gpsimd.tensor_tensor(wsv[:], vtok[:], w, ALU.mult).then_inc(s_wv, 1)
                squares(2 * l + 1)
                squares(2 * l + 2)

        @block.scalar
        def _(act):
            chain = [0]

            def link(ins):
                chain[0] += 1
                ins.then_inc(s_act, 1)
                act.wait_ge(s_act, chain[0])

            A = nc.scalar.activation
            zf = z[:, :, :].rearrange("p a t -> p (a t)")

            def split(g):
                if g >= SLOTS * DEPTH:
                    return
                l, s = g // SLOTS, g % SLOTS
                n = PAIRS * l + (s + 1) // 2
                act.wait_ge(s_ld[n % 2], landed[n])
                if g >= 2:
                    act.wait_ge(s_tile, end_tile(g - 2))
                if s == 0:
                    act.wait_ge(s_gz, 2)
                    A(w_hi[:, g % 2, :].rearrange("p (k a b) -> p k a b", k=KT, b=32)[:, :, 0:2, 0:MH],
                      stage[:, n % 2, 0:8 * KT].rearrange("p (k a c) -> p k a c", k=KT, a=2), ACT.Copy).then_inc(s_hi, 1)
                    return
                k = KT if s < S_WOA or s >= S_MLP else 4
                A(w_hi[:, g % 2, :].rearrange("p (k c) -> p k c", k=k),
                  stage[:, n % 2, :].rearrange("p (k q c) -> p k q c", k=k, q=2)[:, :, (s + 1) % 2, :],
                  ACT.Copy).then_inc(s_hi, 1)

            def norm_tile(n, k):
                act.wait_ge(*x_ready(n, k))
                A(xh[:, k, :], x[:, k, :], ACT.Copy, scale=gain(n, k)).then_inc(s_xh, 1)

            def rms_of(n):
                act.wait_ge(s_ss, n + 1)
                link(A(two(rms[:]), psum[:, 4:6, 0:HALF], ACT.Ln, bias=eps_col, scale=1.0 / DM))
                A(rms[:], rms[:], ACT.Exp, scale=-0.5).then_inc(s_rms, 1)

            graw = zf[0:56, 5 * DM + R_COLS:5 * DM + R_COLS + P]
            act.dma_start(graw[0:16], norm_rows(norm1_g)).then_inc(s_par, 16)
            act.dma_start(graw[16:32], norm_rows(norm2_g)).then_inc(s_par, 16)
            act.dma_start(graw[32:40], final_g.rearrange("(k p) -> k p", p=P)).then_inc(s_par, 16)
            act.dma_start(graw[40:48], norm_rows(mnorm_g)).then_inc(s_par, 16)
            act.dma_start(graw[48:56], state_n.rearrange("l b h k -> (l b h) k")).then_inc(s_par, 16)
            act.dma_start(zf[:, 5 * DM:5 * DM + R_COLS], const[:, C_R:C_R + R_COLS]).then_inc(s_par, 16)
            with nc.allow_non_contiguous_dma(reason="a few bytes"):
                for g in range(AG):
                    act.dma_start(small[g * AD:(g + 1) * AD, 8:8 + DEPTH * AJ].rearrange("p (l j) -> p l j", l=DEPTH),
                                  attn_sink[:, g * AJ:(g + 1) * AJ].rearrange("(o l) j -> o l j", o=1).to_broadcast(
                                      [AD, DEPTH, AJ])).then_inc(s_par, 16)
                act.dma_start(small[0:MH, 24:24 + DEPTH], gate_b[:, 0:MH].rearrange("l h -> h l")).then_inc(s_par, 16)
                act.dma_start(small[32:32 + MH, 24:24 + DEPTH], gate_b[:, MH:].rearrange("l h -> h l")).then_inc(s_par, 16)
                act.dma_start(small[0:MH, 26:26 + DEPTH], state_m.rearrange("l b h -> (b h) l")).then_inc(s_par, 16)
            act.wait_ge(s_par, 11 * 16)
            A(rconst[:], zf[:, 5 * DM:5 * DM + R_COLS], ACT.Copy).then_inc(s_rcon, 1)
            act.wait_ge(s_gain, 2)
            for k in range(KT):
                norm_tile(0, k)
            split(0)
            split(1)

            for l in range(DEPTH):
                g0 = SLOTS * l

                def load_side():
                    if l == 0:
                        act.wait_ge(s_x0, KT)
                    act.dma_start(z[:, 0:2, :].rearrange("p a t -> p (a t)"), const[:, C_COS:C_COS + 2 * T]).then_inc(s_tab, 16)
                    if l:
                        act.wait_ge(s_cno, 16 * 4 * l)
                    act.dma_start(kraw[:], cache_k[l, 0].rearrange("t g d -> t (g d)")).then_inc(s_cl, 16)
                    act.dma_start(vcache[:], cache_v[l, 0].rearrange("t g d -> t (g d)")).then_inc(s_cl, 16)
                    act.dma_start(pT1[:].rearrange("p (h k) -> p h k", h=MH), state_C[l, 0].rearrange("h v k -> v h k")).then_inc(s_cl, 16)

                load_side()
                rms_of(2 * l)
                split(g0 + 2)
                act.wait_ge(s_gf, l + 1)
                link(A(row(2, 1), row(1, 1), ACT.Abs, bias=bf_c[l]))
                link(A(row(2, 1), row(2, 1), ACT.Exp, scale=-1.0))
                A(row(3, 1), row(2, 1), ACT.Ln, bias=1.0).then_inc(s_g1, 1)
                split(g0 + 3)
                split(g0 + 4)
                split(g0 + 5)
                act.wait_ge(s_g2, l + 1)
                A(row(7), row(7), ACT.Exp)
                A(row(1, 2), row(1, 2), ACT.Exp, scale=-1.0)
                A(row(5), row(5), ACT.Exp)
                A(g9[0:MH, 32:32 + NC], g9[0:MH, 32:32 + NC], ACT.Exp).then_inc(s_g3, 1)
                split(g0 + 6)
                split(g0 + 7)
                split(g0 + 8)
                act.wait_ge(s_set, l + 1)
                A(vwin[:, 0:4, :], psum[:, 4, :].rearrange("p (n c) -> p n c", n=4), ACT.Copy)
                A(vwin[:, 4:8, :], psum[:, 6, :].rearrange("p (n c) -> p n c", n=4), ACT.Copy).then_inc(s_seta, 1)
                act.wait_ge(s_setd, l + 1)
                act.wait_ge(s_seta, l + 1)
                act.dma_start(p_k[l, 0].rearrange("t g d -> t (g d)"), kout[:, 0, :]).then_inc(s_kvo, 16)
                act.dma_start(s_k[l, 0].rearrange("t g d -> t (g d)"), kout[0:DEC, 1, :]).then_inc(s_kvo, 16)
                act.dma_start(p_v[l, 0].rearrange("t g d -> t (g d)"), vwin[:, SAMPLE - 2, :]).then_inc(s_kvo, 16)
                act.dma_start(s_v[l, 0].rearrange("t g d -> t (g d)"), vwin[0:DEC, SAMPLE, :]).then_inc(s_kvo, 16)
                with nc.allow_non_contiguous_dma(reason="four values"):
                    act.dma_start(p_m[l].rearrange("b h -> h b"), g9[0:MH, NC - 2:NC - 1]).then_inc(s_kvo, 16)
                    act.dma_start(s_m[l].rearrange("b h -> h b"), g9[0:MH, NC - 1:NC]).then_inc(s_kvo, 16)

                def fill(kind, c, i):
                    for s in slots_done(kind, c, i):
                        split(g0 + s + 2)
                        if S_MO <= s < S_WOA:
                            act.wait_ge(s_evac, TILES * l + s + 1)
                            A(z[:, 12 + s - S_MO, :], z[:, 12 + s - S_MO, :], ACT.Exp, scale=-1.0).then_inc(s_moe, 1)

                for c in range(NC):
                    a, nk = NC * l + c, keys(c)
                    act.wait_ge(s_neg, a + 1)
                    if c or l:
                        act.wait_ge(s_T, a)
                    for j in range(AJ):
                        A(prob[:, j, 0:nk], psum[:, 4 + j // 2, (j % 2) * (WIN + L):(j % 2) * (WIN + L) + nk], ACT.Exp,
                          bias=att_s[:, 4 + j:5 + j], scale=A_SCALE, accum_out=att_s[:, 8 + j:9 + j])
                    act.wait_ge(s_sn, a + 1)
                    A(att_s[:, 16:16 + AJ], att_s[:, 12:12 + AJ], ACT.Exp).then_inc(s_p, 1)
                    fill("a", c, 0)
                    act.wait_ge(s_T, a + 1)
                    if nk > L:
                        A(pT1[:], psum[:, 6, :], ACT.Copy).then_inc(s_pt1, 1)
                    fill("a", c, 1)
                    act.wait_ge(s_pv, a + 1)
                    o4 = psum[:, 4, :].rearrange("p (j g q) -> p j g q", j=AJ, g=AG)
                    A(hid_h[0:AD, 0:AJ, c * L:(c + 1) * L], o4[0:AD, :, 0, :], ACT.Copy)
                    A(hid_h[AD:P, 0:AJ, c * L:(c + 1) * L], o4[AD:P, :, 1, :], ACT.Copy).then_inc(s_aoh, 1)
                    fill("a", c, 2)
                fill("a", NC, 0)

                act.wait_ge(s_kvo, 16 * 6 * (l + 1))

                def finish(c):
                    act.wait_ge(s_hm, NC * l + c + 1)
                    A(hid_h[:, MH:2 * MH, c * L:(c + 1) * L],
                      tmp[2][:, 256:512].rearrange("p (h t) -> p h t", h=MH), ACT.Copy).then_inc(s_hmh, 1)

                for c in range(NC):
                    a = NC * l + c
                    act.wait_ge(s_tk, a + 1)
                    A(ktok[:], psum[0:L, 7, :].rearrange("p (h d) -> p h d", h=MH), ACT.Copy).then_inc(s_kev, 1)
                    act.wait_ge(s_e, a + 1)
                    A(eexp[:], psum[0:L, 5, 0:MH * L].rearrange("p (h t) -> p h t", h=MH), ACT.Exp).then_inc(s_ex, 1)
                    fill("m", c, 0)
                    act.wait_ge(s_tv, a + 1)
                    A(vtok[:], psum[0:L, 7, :].rearrange("p (h d) -> p h d", h=MH), ACT.Copy).then_inc(s_vev, 1)
                    if c:
                        finish(c - 1)
                    fill("m", c, 1)
                    act.wait_ge(s_nd, a + 1)
                    A(dena[:], psum[:, 6, MH * L:2 * MH * L].rearrange("p (h t) -> p h t", h=MH), ACT.Abs).then_inc(s_abs, 1)
                    fill("m", c, 2)
                    act.wait_ge(s_h, a + 1)
                    A(hsq[:], z[:, 4:8, c * L:(c + 1) * L], ACT.Square).then_inc(s_hsq, 1)
                    act.wait_ge(s_ssm, a + 1)
                    link(A(rstd[:], psum[:, 5, MH * L:2 * MH * L].rearrange("p (h t) -> p h t", h=MH), ACT.Ln,
                           bias=eps_col, scale=1.0 / MD))
                    A(rstd[:], rstd[:], ACT.Exp, scale=-0.5).then_inc(s_rs, 1)
                    fill("m", c, 3)
                finish(NC - 1)
                fill("m", NC, 0)
                act.wait_ge(s_co, 2 * (l + 1))
                for w, (co, no) in enumerate(((p_C, p_n), (s_C, s_n))):
                    act.dma_start(co[l, 0].rearrange("h v k -> v h k"),
                                  cout[:, w, :].rearrange("p (h k) -> p h k", h=MH)).then_inc(s_cno, 16)
                    act.dma_start(no[l, 0], kout[0:MH, w, :]).then_inc(s_cno, 16)
                for s in range(S_WOM, S_MLP):
                    split(g0 + s + 2)
                    for k in range(2):
                        norm_tile(2 * l + 1, 2 * (s - S_WOM) + k)
                rms_of(2 * l + 1)

                tile_m = TILES * l + S_MLP + 8
                def mlp_split(j, q, m):
                    r = ((q + 2) % 4) // 2
                    act.wait_ge(s_ld[r], landed[PAIRS * l + 16 + r] + 16 * m)
                    act.wait_ge(s_tile, tile_m + j + 1)
                    A(w_hi[:, (g0 + S_MLP + q) % 2, :].rearrange("p (k c) -> p k c", k=KT),
                      stage[:, r, :].rearrange("p (k q c) -> p k q c", k=KT, q=2)[:, :, q % 2, :],
                      ACT.Copy).then_inc(s_hi, 1)

                def up_step(g, i, q):
                    mlp_split(16 * g + 4 * i + q, q, 4 * g + i + (q + 2) // 4)
                    act.wait_ge(s_hh, 8 * GROUPS * l + 8 * g + 4 * i + q + 1)
                    A(hid_h[:, bass.ds(4 * i + q, 1), :], tmp[1][:].rearrange("p (o t) -> p o t", o=1), ACT.Copy).then_inc(s_hidh, 1)

                with act.Fori(0, GROUPS - 1) as g:
                    with act.Fori(0, 2) as i:
                        for q in range(4):
                            up_step(g, i, q)
                    with act.Fori(0, 2) as i:
                        for q in range(4):
                            mlp_split(16 * g + 8 + 4 * i + q, q, 4 * g + 2 + i + (q + 2) // 4)
                with act.Fori(0, 2) as i:
                    for q in range(4):
                        up_step(GROUPS - 1, i, q)
                for k in range(KT):
                    split(g0 + SLOTS - KT + k + 2)
                    norm_tile(2 * l + 2, k)
            rms_of(2 * DEPTH)
            for t in range(5):
                act.wait_ge(s_ye, 2 * t + 2)
                dst = y_prompt[0, t * P:(t + 1) * P, :] if t < 4 else y_sample[0]
                n = P if t < 4 else DEC
                act.dma_start(dst, zf[0:n, t * DM:(t + 1) * DM]).then_inc(s_yo, 16)
            act.wait_ge(s_yo, 5 * 16)
            act.wait_ge(s_cno, 16 * 4 * DEPTH)
            act.wait_ge(s_kvo, 16 * 6 * DEPTH)

        @block.vector
        def _(dve):
            chain = [0]

            def link(ins):
                chain[0] += 1
                ins.then_inc(s_dve, 1)
                dve.wait_ge(s_dve, chain[0])

            V = nc.vector
            f = lambda ap: ap.bitcast(F32)

            def split(g):
                if g >= SLOTS * DEPTH:
                    return
                l, s = g // SLOTS, g % SLOTS
                n = PAIRS * l + (s + 1) // 2
                dve.wait_ge(s_hi, g + 1)
                if s == 0:
                    pick = lambda w: w[:, g % 2, :].rearrange("p (k a b) -> p k a b", k=KT, b=32)[:, :, 0:2, 0:MH]
                    src = stage[:, n % 2, 0:8 * KT].rearrange("p (k a c) -> p k a c", k=KT, a=2)
                else:
                    k = KT if s < S_WOA or s >= S_MLP else 4
                    pick = lambda w: w[:, g % 2, :].rearrange("p (k c) -> p k c", k=k)
                    src = stage[:, n % 2, :].rearrange("p (k q c) -> p k q c", k=k, q=2)[:, :, (s + 1) % 2, :]
                V.tensor_tensor(pick(w_lo), src, f(pick(w_hi)), ALU.subtract).then_inc(s_lo, 1)

            def norm_tile(n, k):
                dve.wait_ge(s_xh, KT * n + k + 1)
                V.scalar_tensor_tensor(xl[:, k, :], x[:, k, :], gain(n, k), f(xh[:, k, :]),
                                       ALU.mult, ALU.subtract).then_inc(s_xl, 1)

            V.memset(eps_col, EPS).then_inc(s_gain, 1)
            V.memset(f(w_hi[:, 0, :]), 0.0).then_inc(s_gz, 1)
            V.memset(f(w_lo[:, 0, :]), 0.0).then_inc(s_gz, 1)
            for b in (bcr, ncr, acl):
                link(V.memset(f(b[:]), 0.0))
            dve.wait_ge(s_par, 11 * 16)
            link(V.tensor_scalar(small[:, 16:24], small[:, 8:16], -1.0, None, ALU.mult))
            dve.wait_ge(s_xT, 1)
            V.tensor_copy(gains[:], psum[:, 4, 0:56]).then_inc(s_gain, 1)
            dve.wait_ge(s_xT, 2)
            V.tensor_copy(x[:, :, SEQ:T], psum[:, 7, :].rearrange("p (k t) -> p k t", k=KT)).then_inc(s_xs, 1)
            dve.wait_ge(s_xs, 1)
            for k in range(KT):
                dve.wait_ge(s_xT, 3 + k)
                V.tensor_copy(x[:, k, 0:SEQ], psum[:, k % 4, :]).then_inc(s_x0, 1)
            for k in range(KT):
                norm_tile(0, k)
            dve.wait_ge(s_gz, 2)
            split(0)
            split(1)

            rotated = [0]

            def rotary(l, s, writes):
                t = TILES * l + tile_of(s)
                src = acc[t % 2]
                dve.wait_ge(s_tile, t + 1)
                if rotated[0]:
                    dve.wait_ge(s_rot, rotated[0])
                rotated[0] += 1
                mask = list(range(32))
                for i in range(ROPE_DIM // 2):
                    mask[i], mask[i + ROPE_DIM // 2] = i + ROPE_DIM // 2, i
                link(V.stream_shuffle(two(tmp[0][:]), src, mask))
                V.tensor_tensor(two(tmp[1][:]), src, two(z[:, 0, :]), ALU.mult).then_inc(s_evac, 1)
                link(V.tensor_tensor(tmp[0][:], tmp[0][:], z[:, 1, :], ALU.mult))
                dve.wait_ge(s_evac, t + 1)
                for n, (out, sl) in enumerate(writes):
                    t0, t1 = tmp[0][sl, :], tmp[1][sl, :]
                    if len(out.shape) == 3:
                        t0, t1 = (v.rearrange("p (c q) -> p c q", c=NC) for v in (t0, t1))
                    ins = V.tensor_tensor(out, t0, t1, ALU.add)
                ins.then_inc(s_rot, 1)

            for l in range(DEPTH):
                g0, t0 = SLOTS * l, TILES * l

                def plain(s, out, scale=None):
                    t = t0 + tile_of(s)
                    dve.wait_ge(s_tile, t + 1)
                    if scale is None:
                        return V.tensor_tensor(two(out), acc[t % 2], two(rms[:]), ALU.mult).then_inc(s_evac, 1)
                    return V.scalar_tensor_tensor(two(out), acc[t % 2], scale, two(rms[:]), ALU.mult, ALU.mult).then_inc(s_evac, 1)

                def add_x(t, m):
                    dve.wait_ge(s_tile, t + 1)
                    V.tensor_tensor(two(x[:, m, :]), two(x[:, m, :]), acc[t % 2], ALU.add).then_inc(s_evac, 1)

                for b in qbd:
                    V.memset(b[0:AD, :, :, 1, :].rearrange("p j c q -> p (j c) q"), 0.0)
                    link(V.memset(b[AD:P, :, :, 0, :].rearrange("p j c q -> p (j c) q"), 0.0))
                dve.wait_ge(s_rms, 2 * l + 1)
                dve.wait_ge(s_tab, 16 * (l + 1))
                V.tensor_tensor(z[:, 0, :], z[:, 0, :], rms[:], ALU.mult)
                link(V.tensor_tensor(z[:, 1, :], z[:, 1, :], rms[:], ALU.mult))
                dve.wait_ge(s_tile, t0 + 1)
                a0 = acc[t0 % 2]
                V.tensor_tensor(two(row(0)), a0[0:MH], two(rms[0:MH, :]), ALU.mult)
                link(V.tensor_tensor(two(row(1, 1)), a0[32:32 + MH], two(rms[32:32 + MH, :]), ALU.mult))
                link(V.tensor_scalar(row(4, 1), row(1, 1), bf_c[l], 0.0, ALU.add, ALU.min))
                V.tensor_scalar(row(0), row(0), bi_c[l], None, ALU.add).then_inc(s_evac, 1)
                V.memset(row(5), 1.0).then_inc(s_gf, 1)
                split(g0 + 2)
                rotary(l, S_AK, [(kT[:], slice(0, P))])
                split(g0 + 3)
                plain(S_AV, vT[:])
                split(g0 + 4)
                dve.wait_ge(s_gf, l + 1)
                link(V.memset(row(5).rearrange("p (c t) -> p c t", c=NC)[:, :, 0:1], 0.0))
                dve.wait_ge(s_g1, l + 1)
                link(V.tensor_tensor(row(1), row(4, 1), row(3, 1), ALU.subtract))
                link(V.tensor_tensor_scan(row(2), row(5), row(1), 0.0, ALU.mult, ALU.add))
                link(V.tensor_tensor(row(3), row(0), row(2), ALU.subtract))
                last_of = lambda r, c0, c1: r.rearrange("p (c t) -> p c t", c=NC)[:, c0:c1, L - 1:L]
                first_of = lambda r, c0, c1: r.rearrange("p (c t) -> p c t", c=NC)[:, c0:c1, 0:1]
                link(V.memset(row(4), 0.0))
                link(V.tensor_copy(first_of(row(4), 1, SAMPLE), last_of(row(2), 0, SAMPLE - 1)))
                link(V.tensor_tensor_scan(row(6)[:, 0:SEQ], row(4)[:, 0:SEQ], row(3)[:, 0:SEQ], 0.0, ALU.add, ALU.max))
                link(V.tensor_tensor_scan(row(6)[:, SEQ:T], row(4)[:, SEQ:T], row(3)[:, SEQ:T], ms_c[l], ALU.add, ALU.max))
                rotary(l, S_AQ, [(qbd[0][0:AD, 0, :, 0, :], slice(0, AD)), (qbd[0][AD:P, 0, :, 1, :], slice(AD, P))])
                split(g0 + 5)
                col = lambda i: g9[0:MH, 16 * i:16 * i + NC].rearrange("p (c o) -> p c o", o=1)
                if l:
                    dve.wait_ge(s_kvo, 16 * 6 * l)
                link(V.tensor_tensor(col(0), last_of(row(6), 0, NC), last_of(row(2), 0, NC), ALU.add))
                V.memset(g9[0:MH, 16:17], 0.0)
                V.tensor_copy(g9[0:MH, 17:17 + SAMPLE - 1], g9[0:MH, 0:SAMPLE - 1])
                link(V.tensor_copy(g9[0:MH, 16 + SAMPLE:17 + SAMPLE], ms_c[l]))
                chunks = lambda r: r.rearrange("p (c t) -> p c t", c=NC)
                V.tensor_tensor(chunks(row(7)), col(1).to_broadcast([MH, NC, L]), chunks(row(6)), ALU.subtract)
                V.tensor_tensor(row(1, 2), row(2), row(6), ALU.add)
                V.tensor_tensor(chunks(row(5)), chunks(row(3)), last_of(row(6), 0, NC).to_broadcast([MH, NC, L]), ALU.subtract)
                V.tensor_tensor(col(2), col(1), last_of(row(6), 0, NC), ALU.subtract).then_inc(s_g2, 1)
                V.tensor_scalar(ncr[0:MH, :], row(6), -1.0, None, ALU.mult)
                link(V.tensor_copy(acl[0:MH, 0:T], row(3)))
                V.scalar_tensor_tensor(ncr[32:32 + MH, :], row(6), -1.0, f(ncr[0:MH, :]), ALU.mult, ALU.subtract)
                V.tensor_tensor(acl[32:32 + MH, 0:T], row(3), f(acl[0:MH, 0:T]), ALU.subtract)
                rotary(l, S_AQ + 1, [(qbd[0][0:AD, 1, :, 0, :], slice(0, AD)), (qbd[0][AD:P, 1, :, 1, :], slice(AD, P))])
                split(g0 + 6)
                dve.wait_ge(s_g3, l + 1)
                V.tensor_copy(bcr[0:MH, :], row(7))
                link(V.tensor_copy(bcr[64:64 + MH, :], row(1, 2)))
                V.tensor_tensor(bcr[32:32 + MH, :], row(7), f(bcr[0:MH, :]), ALU.subtract)
                V.tensor_tensor(bcr[96:96 + MH, :], row(1, 2), f(bcr[64:64 + MH, :]), ALU.subtract)
                V.tensor_tensor(g9[0:MH, 48:48 + MH * NC].rearrange("p (c h) -> p c h", c=NC), col(2).to_broadcast([MH, NC, MH]),
                                ident[0:MH, 0:MH].rearrange("p (o h) -> p o h", o=1).to_broadcast([MH, NC, MH]),
                                ALU.mult).then_inc(s_g4, 1)
                for j in range(2, AJ):
                    rotary(l, S_AQ + j, [(qbd[1][0:AD, j - 2, :, 0, :], slice(0, AD)), (qbd[1][AD:P, j - 2, :, 1, :], slice(AD, P))])
                    split(g0 + S_AQ + j + 2)
                if l:
                    dve.wait_ge(s_cno, 16 * 4 * l)
                dve.wait_ge(s_set, l + 1)
                V.tensor_copy(cst[:, 1], psum[:, 5, :].rearrange("p (h v) -> p h v", h=MH))
                V.tensor_copy(vwin[0:L, SAMPLE, :], psum[0:L, 7, 0:P])
                V.tensor_copy(gT[0:L, 0, :], psum[0:L, 7, P:P + NC * MH])
                V.tensor_copy(gT[:, 1, :], psum[:, 7, 164:164 + NC * MH])
                V.tensor_copy(nst[:, 1, :], gains[:, 48 + MH * l:52 + MH * l])
                V.tensor_copy(kout[:, 0, :], psum[:, 7, 200:200 + P])
                V.tensor_copy(kout[0:DEC, 1, :], psum[0:DEC, 7, 328:328 + P]).then_inc(s_setd, 1)
                dve.wait_ge(s_set2, l + 1)
                V.tensor_copy(kcT[:], psum[:, 4, 0:P]).then_inc(s_setd2, 1)

                def gate_of(h):
                    zz = z[:, 12 + h, :]
                    dve.wait_ge(s_moe, MH * l + h + 1)
                    link(V.tensor_scalar(zz, zz, 1.0, None, ALU.add))
                    link(V.reciprocal(zz, zz))
                    V.tensor_scalar(zz, zz, gains[:, 40 + MH * l + h:41 + MH * l + h], None, ALU.mult).then_inc(s_moz, 1)

                def fill(kind, c, i):
                    for s in slots_done(kind, c, i):
                        if s < S_WOA:
                            i4 = (s - S_MK) // 4
                            plain(s, z[:, s - S_MK, :], K_SCALE if i4 == 0 else None)
                            split(g0 + s + 2)
                            if s > S_MO:
                                gate_of(s - S_MO - 1)
                        else:
                            for m in range(2):
                                add_x(t0 + tile_of(s) + m, 2 * (s - S_WOA) + m)
                            split(g0 + s + 2)

                for c in range(NC):
                    a, nk = NC * l + c, keys(c)
                    dve.wait_ge(s_sc, a + 1)
                    for b in range(2):
                        ins = V.tensor_reduce(att_s[:, 2 * b:2 * b + 2],
                                              psum[:, 4 + b, 0:2 * (WIN + L)].rearrange("p (j k) -> p j k", j=2)[:, :, 0:nk],
                                              AX.X, ALU.max)
                    link(ins)
                    V.scalar_tensor_tensor(att_s[:, 4:8], att_s[:, 0:4], -A_SCALE, nsink_c[l], ALU.mult, ALU.min).then_inc(s_neg, 1)
                    dve.wait_ge(s_neg, a + 1)
                    V.tensor_tensor(att_s[:, 12:16], att_s[:, 4:8], sink_c[l], ALU.add).then_inc(s_sn, 1)
                    dve.wait_ge(s_p, a + 1)
                    link(V.tensor_tensor(att_s[:, 20:24], att_s[:, 8:12], att_s[:, 16:20], ALU.add))
                    link(V.reciprocal(att_s[:, 24:28], att_s[:, 20:24]))
                    for j in range(AJ):
                        ins = V.tensor_scalar(prob[:, j, 0:nk], prob[:, j, 0:nk], att_s[:, 24 + j:25 + j], None, ALU.mult)
                    ins.then_inc(s_pn, 1)
                    fill("a", c, 0)
                    dve.wait_ge(s_T, a + 1)
                    if nk != WIN:
                        V.tensor_copy(pT2[:], psum[0:L, 7, :]).then_inc(s_pt2, 1)
                    fill("a", c, 1)
                    dve.wait_ge(s_aoh, a + 1)
                    o4 = psum[:, 4, :].rearrange("p (j g q) -> p j g q", j=AJ, g=AG)
                    cs = slice(c * L, (c + 1) * L)
                    V.tensor_tensor(hid_l[0:AD, 0:AJ, cs], o4[0:AD, :, 0, :], f(hid_h[0:AD, 0:AJ, cs]), ALU.subtract)
                    V.tensor_tensor(hid_l[AD:P, 0:AJ, cs], o4[AD:P, :, 1, :], f(hid_h[AD:P, 0:AJ, cs]), ALU.subtract).then_inc(s_ao, 1)
                    fill("a", c, 2)
                fill("a", NC, 0)
                gate_of(MH - 1)

                t4 = lambda i: tmp[2][:, 256 * i:256 * (i + 1)].rearrange("p (h t) -> p h t", h=MH)

                def finish(c):
                    cs = slice(c * L, (c + 1) * L)
                    dve.wait_ge(s_rs, NC * l + c + 1)
                    link(V.tensor_tensor(t4(0), z[:, 4:8, cs], rstd[:], ALU.mult))
                    V.tensor_tensor(t4(1), t4(0), z[:, 12:16, cs], ALU.mult).then_inc(s_hm, 1)
                    dve.wait_ge(s_hmh, NC * l + c + 1)
                    V.tensor_tensor(hid_l[:, MH:2 * MH, cs], t4(1), f(hid_h[:, MH:2 * MH, cs]), ALU.subtract).then_inc(s_hmd, 1)

                for c in range(NC):
                    a, w = NC * l + c, int(c == SAMPLE)
                    cs = slice(c * L, (c + 1) * L)
                    dve.wait_ge(s_swp, a + 1)
                    dve.wait_ge(s_ex, a + 1)
                    ins = V.tensor_tensor(sw[:], psum[0:L, 4, 0:MH * L].rearrange("p (h t) -> p h t", h=MH), eexp[:], ALU.mult)
                    if c:
                        link(V.tensor_tensor(qw[:], z[:, 4:8, cs], psum[:, 4, MH * L:2 * MH * L].rearrange("p (h t) -> p h t", h=MH), ALU.mult))
                        if c > 1:
                            dve.wait_ge(s_st, a)
                        ins = V.tensor_tensor(nq[:], qw[:], nst[:, w, :].rearrange("p (h o) -> p h o", o=1).to_broadcast([P, MH, L]), ALU.mult)
                    ins.then_inc(s_sw, 1)
                    fill("m", c, 0)
                    if c:
                        finish(c - 1)
                    fill("m", c, 1)
                    dve.wait_ge(s_abs, a + 1)
                    link(V.tensor_tensor(dena[:], dena[:], psum[:, 5, 0:MH * L].rearrange("p (h t) -> p h t", h=MH), ALU.max))
                    link(V.reciprocal(dena[:], dena[:]))
                    V.tensor_tensor(z[:, 4:8, cs], psum[:, 6, 0:MH * L].rearrange("p (h t) -> p h t", h=MH), dena[:], ALU.mult).then_inc(s_h, 1)
                    dve.wait_ge(s_u, a + 1)
                    if c == 0:
                        V.tensor_copy(cst[:, 0], psum[:, 7, :].rearrange("p (h v) -> p h v", h=MH))
                        V.tensor_copy(nst[:, 0, :], psum[:, 4, 0:MH]).then_inc(s_st, 1)
                    else:
                        for h in range(MH):
                            V.scalar_tensor_tensor(cst[:, w, h], cst[:, w, h], gT[:, 1, c * MH + h:c * MH + h + 1],
                                                   psum[:, 7, h * MD:(h + 1) * MD], ALU.mult, ALU.add)
                        link(V.tensor_tensor(nst[:, w, :], nst[:, w, :], gT[:, 1, c * MH:(c + 1) * MH], ALU.mult))
                        V.tensor_tensor(nst[:, w, :], nst[:, w, :], psum[:, 4, 0:MH], ALU.add).then_inc(s_st, 1)
                    fill("m", c, 2)
                    fill("m", c, 3)
                finish(NC - 1)
                fill("m", NC, 0)
                for w in range(2):
                    dve.wait_ge(s_ct, 2 * (l + 1))
                    V.tensor_copy(cout[:, w, :], psum[:, 6 + w, :])
                    V.tensor_copy(kout[0:MH, w, :], psum[0:MH, 4, w * P:(w + 1) * P]).then_inc(s_co, 1)
                for s in range(S_WOM, S_MLP):
                    for m in range(2):
                        add_x(t0 + tile_of(s) + m, 2 * (s - S_WOM) + m)
                    split(g0 + s + 2)
                    for m in range(2):
                        norm_tile(2 * l + 1, 2 * (s - S_WOM) + m)

                tile_m, slot_m = t0 + S_MLP + 8, g0 + S_MLP
                hid0 = 8 * GROUPS * l
                dve.wait_ge(s_rms, 2 * l + 2)
                
                def mlp_split(j, q):
                    r = ((q + 2) % 4) // 2
                    pick = lambda w: w[:, (slot_m + q) % 2, :].rearrange("p (k c) -> p k c", k=KT)
                    dve.wait_ge(s_hi, slot_m + 3 + j)
                    V.tensor_tensor(pick(w_lo), stage[:, r, :].rearrange("p (k q c) -> p k q c", k=KT, q=2)[:, :, q % 2, :],
                                    f(pick(w_hi)), ALU.subtract).then_inc(s_lo, 1)

                def up_step(g, i, q):
                    j = 16 * g + 4 * i + q
                    n = hid0 + 8 * g + 4 * i + q + 1
                    dve.wait_ge(s_tile, tile_m + 1 + j)
                    V.tensor_tensor(two(tmp[0][:]), acc[(tile_m + q) % 2], two(rms[:]), ALU.mult).then_inc(s_evac, 1)
                    mlp_split(j, q)
                    dve.wait_ge(s_evac, tile_m + 1 + j)
                    V.scalar_tensor_tensor(tmp[1][:], tmp[0][:], 0.0, tmp[0][:], ALU.max, ALU.mult).then_inc(s_hh, 1)
                    dve.wait_ge(s_hidh, n)
                    V.tensor_tensor(hid_l[:, bass.ds(4 * i + q, 1), :], tmp[1][:].rearrange("p (o t) -> p o t", o=1),
                                    f(hid_h[:, bass.ds(4 * i + q, 1), :]), ALU.subtract).then_inc(s_hid, 1)

                with dve.Fori(0, GROUPS - 1) as g:
                    with dve.Fori(0, 2) as i:
                        for q in range(4):
                            up_step(g, i, q)
                    with dve.Fori(0, 2) as i:
                        for q in range(4):
                            j = 16 * g + 8 + 4 * i + q
                            dve.wait_ge(s_tile, tile_m + 1 + j)
                            xt = x[:, bass.ds(4 * i + q, 1), :].rearrange("p o (a t) -> p (o a) t", a=2)
                            V.tensor_tensor(xt, xt, acc[(tile_m + q) % 2], ALU.add).then_inc(s_evac, 1)
                            mlp_split(j, q)
                with dve.Fori(0, 2) as i:
                    for q in range(4):
                        up_step(GROUPS - 1, i, q)
                for k in range(KT):
                    add_x(t0 + TILES - KT + k, k)
                    split(g0 + SLOTS - KT + k + 2)
                    norm_tile(2 * l + 2, k)

            n = 2 * DEPTH
            dve.wait_ge(s_rms, n + 1)
            for k in range(KT):
                V.scalar_tensor_tensor(x[:, k, :], x[:, k, :], gain(n, k), rms[:],
                                       ALU.mult, ALU.mult).then_inc(s_y, 1)
            zf = z[:, :, :].rearrange("p a t -> p (a t)")
            for i in range(10):
                t, half = i // 2, i % 2
                m = P if t < 4 else DEC
                dve.wait_ge(s_yt, i + 1)
                V.tensor_copy(zf[0:m, t * DM + half * 512:t * DM + (half + 1) * 512], psum[0:m, i % 4, :]).then_inc(s_ye, 1)

        @block.tensor
        def _(pe):
            M = nc.tensor.matmul
            TR = nc.tensor.transpose
            zf = z[:, :, :].rearrange("p a t -> p (a t)")

            def products(t, lhs, k, first, last, hi_mov, lo_mov):
                ins = None
                for n, (w, mov) in enumerate(((w_hi, hi_mov), (w_hi, lo_mov), (w_lo, hi_mov))):
                    for a in range(2):
                        ins = M(acc[t % 2][:, a, :], lhs(w), mov[:, k, a * HALF:(a + 1) * HALF],
                                start=first and n == 0, stop=last and n == 2)
                return ins

            def sum_squares(n):
                pe.wait_ge(s_sum, n + 1)
                for a in range(2):
                    ins = M(psum[:, 4 + a, 0:HALF], ones, ssum[:, a * HALF:(a + 1) * HALF], start=True, stop=True)
                ins.then_inc(s_ss, 1)

            def unit(l, u):
                s, e = u // 8, u % 8
                g = SLOTS * l + s
                if e == 0:
                    pe.wait_ge(s_lo, g + 1)
                    if s == S_WOA:
                        pe.wait_ge(s_ao, NC * (l + 1))
                    if s == S_WOM:
                        pe.wait_ge(s_hmd, NC * (l + 1))
                if s < S_WOA:
                    t, k, first, last = TILES * l + s, e, e == 0, e == 7
                    if s == 0:
                        pe.wait_ge(s_xl, KT * 2 * l + k + 1)
                    lhs = lambda w: w[:, g % 2, k * P:(k + 1) * P]
                    mov = (xh, xl)
                    kk = k
                else:
                    m, k = e // 4, e % 4
                    t, first, last = TILES * l + tile_of(s) + m, k == 0, k == 3
                    lhs = lambda w: w[:, g % 2, k * 2 * P + m * P:k * 2 * P + (m + 1) * P]
                    mov = (hid_h, hid_l)
                    kk = k + (4 if s >= S_WOM else 0)
                if first and t >= 2:
                    pe.wait_ge(s_evac, t - 1)
                ins = products(t, lhs, kk, first, last, *mov)
                if last:
                    ins.then_inc(s_tile, 1)

            def fill(l, kind, c, i):
                for u in range(*fills[kind, c, i]):
                    unit(l, u)

            pe.wait_ge(s_const, 16)
            pe.wait_ge(s_par, 11 * 16)
            TR(psum[:, 4, 0:56], zf[0:56, 5 * DM + R_COLS:5 * DM + R_COLS + P], ident[0:56, 0:56]).then_inc(s_xT, 1)
            pe.wait_ge(s_xin, 5 * 16)
            for k in range(KT):
                ins = TR(psum[:, 7, k * DEC:(k + 1) * DEC], zf[0:DEC, 4 * DM + k * P:4 * DM + (k + 1) * P], ident[0:DEC, 0:DEC])
            ins.then_inc(s_xT, 1)
            for k in range(KT):
                if k >= 4:
                    pe.wait_ge(s_x0, k - 3)
                for t in range(4):
                    ins = TR(psum[:, k % 4, t * P:(t + 1) * P], zf[:, t * DM + k * P:t * DM + (k + 1) * P], ident)
                ins.then_inc(s_xT, 1)
            pe.wait_ge(s_rcon, 1)
            pe.wait_ge(s_x0, KT)

            for l in range(DEPTH):
                for u in range(8):
                    unit(l, u)
                sum_squares(2 * l)
                for u in range(8, 8 * S_MK):
                    unit(l, u)
                pe.wait_ge(s_rot, 5 * l + 1)
                pe.wait_ge(s_evac, TILES * l + S_AV + 1)
                pe.wait_ge(s_cl, 16 * 3 * (l + 1))
                pe.wait_ge(s_g4, l + 1)
                pe.wait_ge(s_rms, 2 * l + 1)
                for n in range(8):
                    TR(psum[:, 4 + n // 4 * 2, (n % 4) * P:(n % 4 + 1) * P], vT[:, n * L:n * L + P], ident)
                for h in range(MH):
                    TR(psum[:, 5, h * P:(h + 1) * P], pT1[:, h * P:(h + 1) * P], ident)
                TR(psum[0:L, 7, 0:P], vT[:, SEQ:T], ident)
                for c in range(NC):
                    TR(psum[0:L, 7, P + c * MH:P + (c + 1) * MH], row(5)[:, c * L:(c + 1) * L], ident[0:MH, 0:MH])
                M(psum[:, 7, 164:164 + NC * MH], ones[0:MH, :], g9[0:MH, 48:48 + NC * MH], start=True, stop=True)
                TR(psum[:, 7, 200:200 + P], kT[:, SEQ - WIN:SEQ], ident)
                TR(psum[0:DEC, 7, 328:328 + P], kT[:, SEQ:T], ident).then_inc(s_set, 1)
                pe.wait_ge(s_seta, l + 1)
                TR(psum[:, 4, 0:P], kraw[:], ident).then_inc(s_set2, 1)
                pe.wait_ge(s_setd, l + 1)
                pe.wait_ge(s_setd2, l + 1)
                pe.wait_ge(s_rot, 5 * (l + 1))

                for c in range(NC):
                    a, nk = NC * l + c, keys(c)
                    if a:
                        pe.wait_ge(s_ao, a)
                    for j in range(AJ):
                        out = psum[:, 4 + j // 2, (j % 2) * (WIN + L):(j % 2) * (WIN + L) + nk]
                        q = qbd[j // 2][:, j % 2, c].rearrange("p g q -> p (g q)")
                        if c == SAMPLE:
                            M(out[:, 0:WIN], q, kcT[:], start=True, stop=True)
                            ins = M(out[:, WIN:nk], q, kT[:, SEQ:T], start=True, stop=True)
                        else:
                            ins = M(out, q, kT[:, (c + 1) * L - nk:(c + 1) * L], start=True, stop=True)
                    ins.then_inc(s_sc, 1)
                    fill(l, "a", c, 0)
                    pe.wait_ge(s_pn, a + 1)
                    if n_pt1(l, c):
                        pe.wait_ge(s_pt1, n_pt1(l, c))
                    if n_pt2(l, c):
                        pe.wait_ge(s_pt2, n_pt2(l, c))
                    old = nk // P * P
                    for j in range(AJ):
                        if old:
                            ins = TR(psum[:, 6, j * P:(j + 1) * P], prob[:, j, 0:P], ident)
                        if nk != WIN:
                            ins = TR(psum[0:L, 7, j * P:(j + 1) * P], prob[:, j, old:nk], ident)
                    ins.then_inc(s_T, 1)
                    fill(l, "a", c, 1)
                    if old:
                        pe.wait_ge(s_pt1, n_pt1(l, c) + 1)
                        older = vcache[:] if c == SAMPLE else vwin[:, max(c - 2, 0), :]
                        ins = M(psum[:, 4, :], older, pT1[:], start=True, stop=nk == WIN)
                    if nk != WIN:
                        pe.wait_ge(s_pt2, n_pt2(l, c) + 1)
                        ins = M(psum[:, 4, :], vwin[0:L, c, :], pT2[:], start=not old, stop=True)
                    ins.then_inc(s_pv, 1)
                    fill(l, "a", c, 2)
                fill(l, "a", NC, 0)

                sel = lambda i: rconst[:, R_SEL + i * P:R_SEL + (i + 1) * P]
                pe.wait_ge(s_ao, NC * (l + 1))
                pe.wait_ge(s_evac, TILES * l + S_MO)
                for c in range(NC):
                    a, w = NC * l + c, int(c == SAMPLE)
                    cs = slice(c * L, (c + 1) * L)
                    if c:
                        pe.wait_ge(s_st, a)
                    for h in range(MH):
                        ins = TR(psum[0:L, 7, h * MD:(h + 1) * MD], z[:, h, cs], ident)
                    ins.then_inc(s_tk, 1)
                    if c:
                        pe.wait_ge(s_rs, a)
                    M(psum[:, 5, 0:MH * L], rconst[:, R_ID:R_ID + P], rconst[:, R_NEG:R_NEG + MH * L], start=True, stop=False)
                    M(psum[:, 5, 0:MH * L], acl[:, c * L:c * L + P], rconst[:, R_ROW:R_ROW + MH * L], start=False, stop=False)
                    for h in range(MH):
                        ins = M(psum[:, 5, h * L:(h + 1) * L], sel(h), ncr[:, cs], start=False, stop=h == MH - 1)
                    ins.then_inc(s_e, 1)
                    for h in range(MH):
                        ins = M(psum[0:L, 4, h * L:(h + 1) * L], z[:, h, cs], z[:, 4 + h, cs], start=True, stop=True)
                    if c:
                        for h in range(MH):
                            ins = M(psum[:, 4, (MH + h) * L:(MH + h + 1) * L], sel(h), bcr[:, cs], start=True, stop=True)
                    ins.then_inc(s_swp, 1)
                    fill(l, "m", c, 0)
                    pe.wait_ge(s_kev, a + 1)
                    for h in range(MH):
                        ins = TR(psum[0:L, 7, h * MD:(h + 1) * MD], z[:, 8 + h, cs], ident)
                    ins.then_inc(s_tv, 1)
                    fill(l, "m", c, 1)
                    pe.wait_ge(s_sw, a + 1)
                    pe.wait_ge(s_vev, a + 1)
                    for h in range(MH):
                        M(psum[:, 6, h * L:(h + 1) * L], vtok[:, h], sw[:, h], start=True, stop=c == 0)
                        if c:
                            M(psum[:, 6, h * L:(h + 1) * L], cst[:, w, h], qw[:, h], start=False, stop=True)
                    M(psum[:, 6, MH * L:2 * MH * L], ones[0:L, :], sw[:].rearrange("p h t -> p (h t)"), start=True, stop=c == 0)
                    if c:
                        M(psum[:, 6, MH * L:2 * MH * L], ones, nq[:].rearrange("p h t -> p (h t)"), start=False, stop=True)
                    for h in range(MH):
                        ins = M(psum[:, 5, h * L:(h + 1) * L], sel(MH + h), bcr[:, cs], start=True, stop=True)
                    ins.then_inc(s_nd, 1)
                    fill(l, "m", c, 2)
                    pe.wait_ge(s_wv, a + 1)
                    for h in range(MH):
                        M(psum[:, 7, h * MD:(h + 1) * MD], ktok[:, h], wsv[:, h], start=True, stop=True)
                    for h in range(MH):
                        ins = M(psum[:, 4, h:h + 1], ktok[:, h], gT[0:L, 0, c * MH + h:c * MH + h + 1], start=True, stop=True)
                    ins.then_inc(s_u, 1)
                    fill(l, "m", c, 3)
                    pe.wait_ge(s_hsq, a + 1)
                    M(psum[:, 5, MH * L:2 * MH * L], ones, hsq[:].rearrange("p h t -> p (h t)"), start=True, stop=True).then_inc(s_ssm, 1)
                fill(l, "m", NC, 0)
                pe.wait_ge(s_st, NC * (l + 1))
                pe.wait_ge(s_h, NC * (l + 1))
                for w in range(2):
                    for h in range(MH):
                        TR(psum[:, 6 + w, h * P:(h + 1) * P], cst[:, w, h], ident)
                    TR(psum[0:MH, 4, w * P:(w + 1) * P], nst[:, w, :], ident).then_inc(s_ct, 1)
                for u in range(8 * S_WOM, 8 * S_MLP):
                    unit(l, u)
                pe.wait_ge(s_rs, NC * (l + 1))
                pe.wait_ge(s_co, 2 * (l + 1))

                tile_m, slot_m, hid0 = TILES * l + S_MLP + 8, SLOTS * l + S_MLP, 8 * GROUPS * l

                def mlp_slot(g, down, i, q):
                    j = 16 * g + 8 * down + 4 * i + q
                    pe.wait_ge(s_lo, slot_m + 1 + j)
                    pe.wait_ge(s_evac, tile_m - 1 + j)
                    for k in range(KT):
                        if down and q == 0:
                            pe.wait_ge(s_hid, hid0 + 8 * g + k + 1)
                        lhs = lambda w: w[:, (slot_m + q) % 2, k * P:(k + 1) * P]
                        mov = (hid_h, hid_l) if down else (xh, xl)
                        ins = products(tile_m + q, lhs, k, k == 0, k == KT - 1, *mov)
                    ins.then_inc(s_tile, 1)

                pe.wait_ge(s_xl, KT * (2 * l + 2))
                for j in range(KT):
                    mlp_slot(0, 0, j // 4, j % 4)
                    if j == 0:
                        sum_squares(2 * l + 1)
                with pe.Fori(0, 2) as i:
                    for q in range(4):
                        mlp_slot(0, 1, i, q)
                with pe.Fori(1, GROUPS) as g:
                    for down in range(2):
                        with pe.Fori(0, 2) as i:
                            for q in range(4):
                                mlp_slot(g, down, i, q)

            n = 2 * DEPTH
            sum_squares(n)
            pe.wait_ge(s_y, KT)
            pe.wait_ge(s_evac, TILES * DEPTH)
            for i in range(10):
                t, half = i // 2, i % 2
                m = P if t < 4 else DEC
                if i >= 4:
                    pe.wait_ge(s_ye, i - 3)
                for k in range(4):
                    ins = TR(psum[0:m, i % 4, k * P:(k + 1) * P], x[:, half * 4 + k, t * P:t * P + m], ident)
                ins.then_inc(s_yt, 1)


def norm_rows(g):
    return g.rearrange("l (k p) -> (l k) p", p=P)


_INS = ["x_prompt", "x_sample", "cache_k", "cache_v", "state_C", "state_n", "state_m", "norm1_g", "w_in", "gate_b",
        "attn_sink", "mnorm_g", "w_out", "norm2_g", "w_up", "w_down", "final_g"]
_OUTS = [(1, SEQ, DM), (1, DEC, DM)] + [(DEPTH, 1, WIN, AG, AD)] * 2 + [
    (DEPTH, 1, MH, MD, MD), (DEPTH, 1, MH, MD), (DEPTH, 1, MH)] + [(DEPTH, 1, DEC, AG, AD)] * 2 + [
    (DEPTH, 1, MH, MD, MD), (DEPTH, 1, MH, MD), (DEPTH, 1, MH)]


def kernel(**inputs):
    import numpy as _np
    import concourse.bacc as _bacc
    from concourse.bass_utils import run_bass_kernel_spmd as _run

    nc = _bacc.Bacc("TRN2", target_bir_lowering=False, num_devices=1)
    arrays = {f"in_{name}": _np.ascontiguousarray(inputs[name]) for name in _INS}
    arrays["in_const"] = constants()
    ins = [nc.dram_tensor(name, a.shape, F32, kind="ExternalInput").ap() for name, a in arrays.items()]
    outs = [nc.dram_tensor(f"out_{i}", shape, F32, kind="ExternalOutput").ap() for i, shape in enumerate(_OUTS)]
    hymba_step(nc, ins, outs)
    r = _run(nc, [arrays], core_ids=[0])
    return tuple(r.results[0][f"out_{i}"] for i in range(len(_OUTS)))
```

```python
from contextlib import ExitStack

import concourse.bass as bass
from concourse import mybir

F32 = mybir.dt.float32
F32R = mybir.dt.float32r
ALU = mybir.AluOpType
ACT = mybir.ActivationFunctionType
AX = mybir.AxisListType

P = 128
DM = 1024
KT = DM // P
SEQ, DEC = 512, 64
T = SEQ + DEC
HALF = T // 2
DEPTH = 2
L = 64
NC = T // L
SAMPLE = NC - 1
NP = (NC + 1) // 2
WIN = 128
AH, AG, AD = 8, 2, 64
AJ = AH // AG
MH, MD = 4, 128
AQ, AKV, MW = AH * AD, AG * AD, MH * MD
COL_K, COL_V = AQ, AQ + AKV
COL_MQ = AQ + 2 * AKV
COL_MK, COL_MV, COL_MO = COL_MQ + MW, COL_MQ + 2 * MW, COL_MQ + 3 * MW
COL_GATE = COL_MQ + 4 * MW
FF = 4 * DM
GROUPS = FF // DM
EPS = 1e-6
A_SCALE = float(AD) ** -0.5
K_SCALE = float(MD) ** -0.5
ROPE_DIM = AD // 4
E_TOP, E_LOW = 1e30, 1e-36
PAST = 1024

S_GATE = 0
S_AK, S_AV = 1, 2
S_AQ = 3
S_MK, S_MQ, S_MO, S_MV = 7, 11, 15, 19
S_WOA, S_WOM = 23, 27
S_MLP = 31
SLOTS = S_MLP + GROUPS * 2 * KT
TILES = SLOTS + 8
PAIRS = 1 + (SLOTS - 1) // 2

C_ID, C_ONE, C_COS, C_SIN = 0, 128, 256, 832
C_R = 1408
R_SEL, R_ROW, R_NEG, R_ID = 0, 1024, 1280, 1536
R_COLS = 1664


def constants():
    import numpy as np
    c = np.zeros((P, C_R + R_COLS), np.float32)
    c[:, C_ID:C_ID + P] = np.eye(P)
    c[:, C_ONE:C_ONE + P] = 1.0
    half = ROPE_DIM // 2
    inv = np.float32(500000.0) ** (-(np.arange(half, dtype=np.float32) * np.float32(2.0) / np.float32(ROPE_DIM)))
    pos = np.concatenate([np.arange(SEQ), np.arange(DEC) + PAST]).astype(np.float32)
    ang = inv.astype(np.float32)[:, None] * pos[None, :]
    c[:, C_COS:C_COS + T] = 1.0
    for g in range(AG):
        a = g * AD
        c[a:a + half, C_COS:C_COS + T] = np.cos(ang)
        c[a + half:a + 2 * half, C_COS:C_COS + T] = np.cos(ang)
        c[a:a + half, C_SIN:C_SIN + T] = -np.sin(ang)
        c[a + half:a + 2 * half, C_SIN:C_SIN + T] = np.sin(ang)
    r = c[:, C_R:]
    for h in range(MH):
        for which, base in ((h, 0), (MH + h, 64)):
            r[base + h, R_SEL + which * P:R_SEL + (which + 1) * P] = 1.0
            r[base + 32 + h, R_SEL + which * P:R_SEL + (which + 1) * P] = 1.0
        r[h, R_ROW + h * L:R_ROW + (h + 1) * L] = 1.0
        r[32 + h, R_ROW + h * L:R_ROW + (h + 1) * L] = 1.0
        for q in range(2):
            r[q * L:(q + 1) * L, R_NEG + h * L:R_NEG + (h + 1) * L] = np.tril(np.full((L, L), -1e30, np.float32), -1)
    r[:, R_ID:R_ID + P] = np.eye(P)
    return c


A_FILL = (8, 3, 2)
P_FILL = (2, 2)
M_FILL = (1, 2)


def hymba_step(nc, inputs, outs):
    (x_prompt, x_sample, cache_k, cache_v, state_C, state_n, state_m, norm1_g, w_in, gate_b,
     attn_sink, mnorm_g, w_out, norm2_g, w_up, w_down, final_g, const) = inputs
    (y_prompt, y_sample, p_k, p_v, p_C, p_n, p_m, s_k, s_v, s_C, s_n, s_m) = outs

    with ExitStack() as ctx:
        def sem(name):
            return ctx.enter_context(nc.semaphore(name))

        base = (nc.sbuf_base + 63) // 64 * 64
        top = [base]

        def place(name, shape, dt=F32, where=None):
            size = 4
            for n in shape[1:]:
                size *= n
            off = top[0] if where is None else where
            if where is None:
                top[0] += (size + 31) // 32 * 32
                assert top[0] <= nc.sbuf_usable_end, (name, top[0] - nc.sbuf_usable_end)
            return nc.alloc_sbuf_tensor_at(name, shape, dt, offset=off)

        x = place("x", [P, KT, T])
        xh = place("xh", [P, KT, T], F32R)
        xl = place("xl", [P, KT, T], F32R)
        hh_off = top[0]
        hid_h = place("hid_h", [P, KT, T], F32R)
        hl_off = top[0]
        hid_l = place("hid_l", [P, KT, T], F32R)
        upper = 4 * T * 4
        qbd = [place("qbd_a", [P, 2, NC, AG, L], where=hh_off + upper),
               place("qbd_b", [P, 2, NC, AG, L], where=hl_off + upper)]
        z = place("z", [P, 4 * MH, T])
        kT = place("kT", [P, T])
        vT = place("vT", [P, T])
        rms = place("rms", [P, T])
        ssum = place("ssum", [P, T])
        tmp = [place(f"tmp{i}", [P, T]) for i in range(3)]
        sqr = tmp[2]
        stage = place("stage", [P, 2, KT * 2 * P])
        w_hi = place("w_hi", [P, 2, KT * P], F32R)
        w_lo = place("w_lo", [P, 2, KT * P], F32R)
        io = place("io", [P, 2 * P])
        ident, ones = io[:, 0:P], io[:, P:2 * P]
        rconst = place("rconst", [P, R_COLS], F32R)
        bcr = place("bcr", [P, T], F32R)
        ncr = place("ncr", [P, T], F32R)
        acl = place("acl", [P, T + L], F32R)
        gains = place("gains", [P, 56])
        cst = place("cst", [P, 2, MH, MD + 1])
        g9 = place("g9", [P, 6 * 16])
        gT = place("gT", [P, 2, NC * MH])
        small = place("small", [P, 64])
        kout = place("kout", [P, 2, P])
        arena = top[0]
        vwin = place("vwin", [P, NC, P])
        kcT = place("kcT", [P, WIN])
        kraw = place("kraw", [P, WIN])
        vcache = place("vcache", [P, WIN])
        prob = place("prob", [P, AJ, WIN + L])
        pT1 = place("pT1", [P, AJ * P])
        pT2 = place("pT2", [L, AJ * P])
        end = top[0]
        top[0] = arena
        ktok = place("ktok", [P, MH, MD])
        vtok = place("vtok", [P, MH, MD])
        wsv = place("wsv", [P, MH, MD + 1])
        eexp = place("eexp", [P, MH, L])
        sw = place("sw", [P, MH, L])
        qw = place("qw", [P, MH, L])
        nq = place("nq", [P, MH, L])
        dsq = place("dsq", [P, MH, L])
        hsq = place("hsq", [P, MH, L])
        rstd = place("rstd", [P, MH, L])
        top[0] = max(top[0], end)
        cout = place("cout", [P, 2, MH * MD], where=arena)

        def row(i, q=0):
            return z[32 * q:32 * q + MH, 8 + i, :]

        eps_col = small[:, 0:1]
        sink_c = [small[:, 8 + AJ * l:8 + AJ * (l + 1)] for l in range(DEPTH)]
        nsink_c = [small[:, 16 + AJ * l:16 + AJ * (l + 1)] for l in range(DEPTH)]
        bi_c = [small[0:MH, 24 + l:25 + l] for l in range(DEPTH)]
        ms_c = [small[0:MH, 26 + l:27 + l] for l in range(DEPTH)]
        bf_c = [small[32:32 + MH, 24 + l:25 + l] for l in range(DEPTH)]
        att_s = small[:, 32:64]

        def gain(n, k):
            r = 2 * DEPTH if n == 2 * DEPTH else n // 2 + (DEPTH if n % 2 else 0)
            return gains[:, r * KT + k:r * KT + k + 1]

        psum = ctx.enter_context(nc.psum_tensor("psum", [P, 8, 512], F32))
        acc = [psum[:, 2 * i:2 * i + 2, 0:HALF] for i in range(2)]
        two = lambda ap: ap.rearrange("p (a t) -> p a t", a=2)

        s_par, s_xin, s_const = sem("s_par"), sem("s_xin"), sem("s_const")
        s_ld = [sem("s_ld0"), sem("s_ld1")]
        s_hi, s_lo = sem("s_hi"), sem("s_lo")
        s_gz = sem("s_gz")
        s_tile = sem("s_tile")
        s_evac = sem("s_evac")
        s_x0, s_xs = sem("s_x0"), sem("s_xs")
        s_gain, s_rcon = sem("s_gain"), sem("s_rcon")
        s_xT = sem("s_xT")
        s_xh, s_xl = sem("s_xh"), sem("s_xl")
        s_r0 = sem("s_r0")
        s_sum, s_ss, s_rms = sem("s_sum"), sem("s_ss"), sem("s_rms")
        s_hh, s_hidh, s_hid = sem("s_hh"), sem("s_hidh"), sem("s_hid")
        s_dve, s_act, s_pool = sem("s_dve"), sem("s_act"), sem("s_pool")
        s_rot = sem("s_rot")
        s_tab = sem("s_tab")
        s_gf, s_g1, s_g2, s_g3, s_g4 = sem("s_gf"), sem("s_g1"), sem("s_g2"), sem("s_g3"), sem("s_g4")
        s_moz, s_moe = sem("s_moz"), sem("s_moe")
        s_cl = sem("s_cl")
        s_set, s_seta, s_setd, s_set2 = sem("s_set"), sem("s_seta"), sem("s_setd"), sem("s_set2")
        s_setd2 = sem("s_setd2")
        s_sc, s_neg, s_sn, s_p, s_pn = sem("s_sc"), sem("s_neg"), sem("s_sn"), sem("s_p"), sem("s_pn")
        s_T, s_pt1, s_pt2, s_pv = sem("s_T"), sem("s_pt1"), sem("s_pt2"), sem("s_pv")
        s_aoh, s_ao = sem("s_aoh"), sem("s_ao")
        s_dn = sem("s_dn")
        s_tv, s_vev, s_tk, s_kev, s_wv = sem("s_tv"), sem("s_vev"), sem("s_tk"), sem("s_kev"), sem("s_wv")
        s_e, s_ex, s_swp, s_sw, s_nd = sem("s_e"), sem("s_ex"), sem("s_swp"), sem("s_sw"), sem("s_nd")
        s_dsq, s_hsq, s_em, s_mx = sem("s_dsq"), sem("s_hsq"), sem("s_em"), sem("s_mx")
        s_nu, s_nn, s_u, s_st = sem("s_nu"), sem("s_nn"), sem("s_u"), sem("s_st")
        s_ssm, s_s2, s_rs, s_hm, s_hmh, s_hmd = (sem("s_ssm"), sem("s_s2"), sem("s_rs"), sem("s_hm"), sem("s_hmh"),
                                                 sem("s_hmd"))
        s_ct, s_co = sem("s_ct"), sem("s_co")
        s_y, s_yt, s_ye = sem("s_y"), sem("s_yt"), sem("s_ye")
        s_kvo, s_mo, s_cno, s_yo = sem("s_kvo"), sem("s_mo"), sem("s_cno"), sem("s_yo")

        def tile_of(s):
            return s if s < S_WOA else (S_WOA + 2 * (s - S_WOA) if s < S_MLP else s + 8)

        def end_tile(g):
            return TILES * (g // SLOTS) + tile_of(g % SLOTS + 1)

        landed, got = {}, [0, 0]
        for n in range(PAIRS * DEPTH):
            got[n % 2] += 16 * {2: 4, 3: 4, 12: 2, 13: 2}.get(n % PAIRS, 1)
            landed[n] = got[n % 2]

        fills = {}

        def plan_fills(kind, first, last, counts):
            u = first
            for c in range(NC):
                for i, n in enumerate(counts):
                    fills[kind, c, i] = (u, min(u + n, last))
                    u = min(u + n, last)
            fills[kind, NC, 0] = (u, (u + last) // 2)
            fills[kind, NC, 1] = ((u + last) // 2, last)

        plan_fills("a", 8 * S_MK, 8 * S_WOA, A_FILL)
        fills["p", 0, 0] = (8 * S_WOA, 8 * S_WOA + P_FILL[0])
        fills["p", 0, 1] = (8 * S_WOA + P_FILL[0], 8 * S_WOA + sum(P_FILL))
        plan_fills("m", 8 * S_WOA + sum(P_FILL), 8 * S_WOM, M_FILL)

        def slots_done(kind, c, i):
            a, b = fills[kind, c, i]
            return range(-(-(a + 1) // 8) - 1, b // 8) if b > a else range(0)

        def x_ready(n, k):
            if n == 0:
                return s_x0, k + 1
            l, second = (n - 1) // 2, n % 2
            return s_evac, TILES * l + (S_WOA + 8 if second else TILES - 8) + k + 1

        def keys(c):
            return WIN + L if c >= 2 else (c + 1) * L

        def n_pt1(l, c):
            return (NC - 1) * l + max(c - 1, 0)

        def n_pt2(l, c):
            return (NC - 1) * l + (c if c < 2 else c - 1)

        block = ctx.enter_context(nc.Block())

        @block.sync
        def _(sp):
            sp.dma_start(io[:], const[:, C_ID:C_ID + 2 * P]).then_inc(s_const, 16)
            zf = z[:, :, :].rearrange("p a t -> p (a t)")
            for t in range(SEQ // P):
                sp.dma_start(zf[:, t * DM:(t + 1) * DM], x_prompt[0, t * P:(t + 1) * P, :]).then_inc(s_xin, 16)
            sp.dma_start(zf[0:DEC, 4 * DM:5 * DM], x_sample[0]).then_inc(s_xin, 16)
            for l in range(DEPTH):
                for p in range(S_MLP // 2 + 1):
                    n = PAIRS * l + p
                    if n >= 2:
                        sp.wait_ge(s_lo, SLOTS * ((n - 2) // PAIRS) + 2 * ((n - 2) % PAIRS) + 1)
                    dst = stage[:, n % 2, :]
                    if p == 0:
                        sp.dma_start(dst[:, 0:8 * KT].rearrange("p (k c) -> p k c", k=KT),
                                     w_in[l, :, COL_GATE:].rearrange("(k p) c -> p k c", p=P)).then_inc(s_ld[n % 2], 16)
                    elif p in (2, 3):
                        d5 = dst.rearrange("p (k q g c) -> p k q g c", k=KT, q=2, g=AG)
                        for q in range(2):
                            for g in range(AG):
                                col = g * AJ * AD + (2 * (p - 2) + q) * AD
                                sp.dma_start(d5[:, :, q, g, :], w_in[l, :, col:col + AD].rearrange(
                                    "(k p) c -> p k c", p=P)).then_inc(s_ld[n % 2], 16)
                    elif p < 12:
                        col = COL_K if p == 1 else (COL_MK, COL_MQ, COL_MO, COL_MV)[(p - 4) // 2] + (p % 2) * 2 * P
                        sp.dma_start(dst.rearrange("p (k c) -> p k c", k=KT),
                                     w_in[l, :, col:col + 2 * P].rearrange("(k p) c -> p k c", p=P)).then_inc(s_ld[n % 2], 16)
                    else:
                        cols = slice((p % 2) * 4 * P, (p % 2 + 1) * 4 * P)
                        d3 = dst.rearrange("p (k c) -> p k c", k=AJ)
                        if p < 14:
                            for g in range(AG):
                                sp.dma_start(d3[g * AD:(g + 1) * AD], w_out[l, g * AJ * AD:(g + 1) * AJ * AD, cols].rearrange(
                                    "(j p) c -> p j c", p=AD)).then_inc(s_ld[n % 2], 16)
                        else:
                            sp.dma_start(d3, w_out[l, AQ:, cols].rearrange("(k p) c -> p k c", p=P)).then_inc(s_ld[n % 2], 16)
                free0 = SLOTS * l + S_MLP - 2
                with sp.Fori(0, GROUPS) as g:
                    with sp.Fori(0, 2) as i:
                        for q in range(2):
                            sp.wait_ge(s_lo, free0 + 16 * g + 4 * i + 2 * q)
                            sp.dma_start(stage[:, q, :].rearrange("p (k c) -> p k c", k=KT),
                                         w_up[l, :, bass.ds(g * DM + i * 4 * P + q * 2 * P, 2 * P)].rearrange(
                                             "(k p) c -> p k c", p=P)).then_inc(s_ld[q], 16)
                    with sp.Fori(0, 2) as i:
                        for q in range(2):
                            sp.wait_ge(s_lo, free0 + 8 + 16 * g + 4 * i + 2 * q)
                            sp.dma_start(stage[:, q, :].rearrange("p (k c) -> p k c", k=KT),
                                         w_down[l, bass.ds(g * DM, DM), bass.ds(i * 4 * P + q * 2 * P, 2 * P)].rearrange(
                                             "(k p) c -> p k c", p=P)).then_inc(s_ld[q], 16)

        @block.gpsimd
        def _(pool):
            chain = [0]

            def link(ins):
                chain[0] += 1
                ins.then_inc(s_pool, 1)
                pool.wait_ge(s_pool, chain[0])

            def squares(n):
                if n:
                    pool.wait_ge(s_ss, n)
                for k in range(KT):
                    pool.wait_ge(*x_ready(n, k))
                    if k == 0:
                        link(nc.gpsimd.tensor_tensor(ssum[:], x[:, k, :], x[:, k, :], ALU.mult))
                    else:
                        link(nc.gpsimd.tensor_tensor(sqr[:], x[:, k, :], x[:, k, :], ALU.mult))
                        last = nc.gpsimd.tensor_tensor(ssum[:], ssum[:], sqr[:], ALU.add)
                        if k < KT - 1:
                            link(last)
                last.then_inc(s_sum, 1)

            squares(0)
            for l in range(DEPTH):
                for c in range(NC):
                    if c % 2 == 0:
                        p = c // 2
                        pool.wait_ge(s_vev, NP * l + p + 1)
                        r = L if p == NP - 1 else P
                        w = gT[0:r, 0, p * MH:(p + 1) * MH].rearrange("p (h o) -> p h o", o=1)
                        nc.gpsimd.tensor_copy(wsv[0:r, :, MD:MD + 1], w)
                        nc.gpsimd.tensor_tensor(wsv[0:r, :, 0:MD], vtok[0:r], w.to_broadcast([r, MH, MD]), ALU.mult).then_inc(s_wv, 1)
                    if c:
                        q = slice((c % 2) * L, (c % 2 + 1) * L)
                        pool.wait_ge(s_sw, NC * l + c + 1)
                        nc.gpsimd.tensor_tensor(nq[q], nq[q], sw[q], ALU.add).then_inc(s_dn, 1)
                squares(2 * l + 1)
                squares(2 * l + 2)

        @block.scalar
        def _(act):
            chain = [0]

            def link(ins):
                chain[0] += 1
                ins.then_inc(s_act, 1)
                act.wait_ge(s_act, chain[0])

            A = nc.scalar.activation
            zf = z[:, :, :].rearrange("p a t -> p (a t)")

            def split(g):
                if g >= SLOTS * DEPTH:
                    return
                l, s = g // SLOTS, g % SLOTS
                n = PAIRS * l + (s + 1) // 2
                act.wait_ge(s_ld[n % 2], landed[n])
                if g >= 2:
                    act.wait_ge(s_tile, end_tile(g - 2))
                if s == 0:
                    act.wait_ge(s_gz, 2)
                    A(w_hi[:, g % 2, :].rearrange("p (k a b) -> p k a b", k=KT, b=32)[:, :, 0:2, 0:MH],
                      stage[:, n % 2, 0:8 * KT].rearrange("p (k a c) -> p k a c", k=KT, a=2), ACT.Copy).then_inc(s_hi, 1)
                    return
                k = KT if s < S_WOA or s >= S_MLP else 4
                A(w_hi[:, g % 2, :].rearrange("p (k c) -> p k c", k=k),
                  stage[:, n % 2, :].rearrange("p (k q c) -> p k q c", k=k, q=2)[:, :, (s + 1) % 2, :],
                  ACT.Copy).then_inc(s_hi, 1)

            def norm_tile(n, k):
                act.wait_ge(*x_ready(n, k))
                A(xh[:, k, :], x[:, k, :], ACT.Copy, scale=gain(n, k)).then_inc(s_xh, 1)

            def rms_of(n):
                act.wait_ge(s_ss, n + 1)
                link(A(two(rms[:]), psum[:, 4:6, 0:HALF], ACT.Ln, bias=eps_col, scale=1.0 / DM))
                link(A(rms[:], rms[:], ACT.Exp, scale=-0.5))
                A(tmp[1][:], rms[:], ACT.Square, scale=0.5 ** 0.5)
                A(two(tmp[0][:]), psum[:, 4:6, 0:HALF], ACT.Identity, bias=eps_col, scale=1.0 / DM).then_inc(s_r0, 1)

            nc.scalar.preload_act_table_set("natural_log_exp_and_others")

            graw = zf[0:56, 5 * DM + R_COLS:5 * DM + R_COLS + P]
            act.dma_start(graw[0:16], norm_rows(norm1_g)).then_inc(s_par, 16)
            act.dma_start(graw[16:32], norm_rows(norm2_g)).then_inc(s_par, 16)
            act.dma_start(graw[32:40], final_g.rearrange("(k p) -> k p", p=P)).then_inc(s_par, 16)
            act.dma_start(graw[40:48], norm_rows(mnorm_g)).then_inc(s_par, 16)
            act.dma_start(graw[48:56], state_n.rearrange("l b h k -> (l b h) k")).then_inc(s_par, 16)
            act.dma_start(zf[:, 5 * DM:5 * DM + R_COLS], const[:, C_R:C_R + R_COLS]).then_inc(s_par, 16)
            with nc.allow_non_contiguous_dma(reason="a few bytes"):
                for g in range(AG):
                    act.dma_start(small[g * AD:(g + 1) * AD, 8:8 + DEPTH * AJ].rearrange("p (l j) -> p l j", l=DEPTH),
                                  attn_sink[:, g * AJ:(g + 1) * AJ].rearrange("(o l) j -> o l j", o=1).to_broadcast(
                                      [AD, DEPTH, AJ])).then_inc(s_par, 16)
                act.dma_start(small[0:MH, 24:24 + DEPTH], gate_b[:, 0:MH].rearrange("l h -> h l")).then_inc(s_par, 16)
                act.dma_start(small[32:32 + MH, 24:24 + DEPTH], gate_b[:, MH:].rearrange("l h -> h l")).then_inc(s_par, 16)
                act.dma_start(small[0:MH, 26:26 + DEPTH], state_m.rearrange("l b h -> (b h) l")).then_inc(s_par, 16)
            act.wait_ge(s_par, 11 * 16)
            A(rconst[:], zf[:, 5 * DM:5 * DM + R_COLS], ACT.Copy).then_inc(s_rcon, 1)
            act.wait_ge(s_gain, 2)
            for k in range(KT):
                norm_tile(0, k)
            split(0)
            split(1)

            for l in range(DEPTH):
                g0 = SLOTS * l

                def load_side():
                    if l == 0:
                        act.wait_ge(s_x0, KT)
                    act.dma_start(z[:, 0:2, :].rearrange("p a t -> p (a t)"), const[:, C_COS:C_COS + 2 * T]).then_inc(s_tab, 16)
                    if l:
                        act.wait_ge(s_cno, 16 * 4 * l)
                    act.dma_start(kraw[:], cache_k[l, 0].rearrange("t g d -> t (g d)")).then_inc(s_cl, 16)
                    act.dma_start(vcache[:], cache_v[l, 0].rearrange("t g d -> t (g d)")).then_inc(s_cl, 16)
                    act.dma_start(pT1[:].rearrange("p (h k) -> p h k", h=MH), state_C[l, 0].rearrange("h v k -> v h k")).then_inc(s_cl, 16)

                load_side()
                rms_of(2 * l)
                split(g0 + 2)
                act.wait_ge(s_gf, l + 1)
                link(A(row(2, 1), row(1, 1), ACT.Abs, bias=bf_c[l]))
                link(A(row(2, 1), row(2, 1), ACT.Exp, scale=-1.0))
                nc.scalar.preload_act_table_set("natural_log")
                A(row(3, 1), row(2, 1), ACT.Ln, bias=1.0).then_inc(s_g1, 1)
                nc.scalar.preload_act_table_set("natural_log_exp_and_others")
                split(g0 + 3)
                split(g0 + 4)
                split(g0 + 5)
                act.wait_ge(s_g2, l + 1)
                A(row(7), row(7), ACT.Exp)
                A(row(1, 2), row(1, 2), ACT.Exp, scale=-2.0)
                A(row(5), row(5), ACT.Exp)
                A(g9[0:MH, 32:32 + NC], g9[0:MH, 32:32 + NC], ACT.Exp).then_inc(s_g3, 1)
                split(g0 + 6)
                split(g0 + 7)
                split(g0 + 8)
                act.wait_ge(s_set, l + 1)
                A(vwin[:, 0:4, :], psum[:, 4, :].rearrange("p (n c) -> p n c", n=4), ACT.Copy)
                A(vwin[:, 4:8, :], psum[:, 6, :].rearrange("p (n c) -> p n c", n=4), ACT.Copy).then_inc(s_seta, 1)
                act.wait_ge(s_setd, l + 1)
                act.wait_ge(s_seta, l + 1)
                act.dma_start(p_k[l, 0].rearrange("t g d -> t (g d)"), kout[:, 0, :]).then_inc(s_kvo, 16)
                act.dma_start(s_k[l, 0].rearrange("t g d -> t (g d)"), kout[0:DEC, 1, :]).then_inc(s_kvo, 16)
                act.dma_start(p_v[l, 0].rearrange("t g d -> t (g d)"), vwin[:, SAMPLE - 2, :]).then_inc(s_kvo, 16)
                act.dma_start(s_v[l, 0].rearrange("t g d -> t (g d)"), vwin[0:DEC, SAMPLE, :]).then_inc(s_kvo, 16)
                with nc.allow_non_contiguous_dma(reason="four values"):
                    act.dma_start(p_m[l].rearrange("b h -> h b"), g9[0:MH, NC - 2:NC - 1]).then_inc(s_kvo, 16)
                    act.dma_start(s_m[l].rearrange("b h -> h b"), g9[0:MH, NC - 1:NC]).then_inc(s_kvo, 16)

                def fill(kind, c, i):
                    for s in slots_done(kind, c, i):
                        split(g0 + s + 2)
                        if S_MO <= s < S_MV:
                            act.wait_ge(s_evac, TILES * l + s + 1)
                            A(z[:, 12 + s - S_MO, :], z[:, 12 + s - S_MO, :], ACT.Exp, scale=-1.0).then_inc(s_moe, 1)

                for c in range(NC):
                    a, nk = NC * l + c, keys(c)
                    act.wait_ge(s_neg, a + 1)
                    if c or l:
                        act.wait_ge(s_T, a)
                    for j in range(AJ):
                        A(prob[:, j, 0:nk], psum[:, 4 + j // 2, (j % 2) * (WIN + L):(j % 2) * (WIN + L) + nk], ACT.Exp,
                          bias=att_s[:, 4 + j:5 + j], scale=A_SCALE, accum_out=att_s[:, 8 + j:9 + j])
                    act.wait_ge(s_sn, a + 1)
                    A(att_s[:, 16:16 + AJ], att_s[:, 12:12 + AJ], ACT.Exp).then_inc(s_p, 1)
                    fill("a", c, 0)
                    act.wait_ge(s_T, a + 1)
                    if nk > L:
                        A(pT1[:], psum[:, 6, :], ACT.Copy).then_inc(s_pt1, 1)
                    fill("a", c, 1)
                    act.wait_ge(s_pv, a + 1)
                    o4 = psum[:, 6, :].rearrange("p (j g q) -> p j g q", j=AJ, g=AG)
                    A(hid_h[0:AD, 0:AJ, c * L:(c + 1) * L], o4[0:AD, :, 0, :], ACT.Copy)
                    A(hid_h[AD:P, 0:AJ, c * L:(c + 1) * L], o4[AD:P, :, 1, :], ACT.Copy).then_inc(s_aoh, 1)
                    fill("a", c, 2)

                ch = lambda b, half: psum[:, b, half * MH * L:(half + 1) * MH * L].rearrange("p (h t) -> p h t", h=MH)
                m2, r2 = (tmp[0][:, i * MH * L:(i + 1) * MH * L].rearrange("p (h t) -> p h t", h=MH) for i in range(2))

                def scores_exp(c):
                    q = slice((c % 2) * L, (c % 2 + 1) * L)
                    act.wait_ge(s_e, NC * l + c + 1)
                    A(eexp[q], ch(5, 0)[q], ACT.Exp).then_inc(s_ex, 1)

                def token_major(p, dst, arrived, done):
                    r = L if p == NP - 1 else P
                    act.wait_ge(arrived, NP * l + p + 1)
                    A(dst[0:r], psum[0:r, 7, :].rearrange("p (h d) -> p h d", h=MH), ACT.Copy).then_inc(done, 1)

                def finish(c):
                    act.wait_ge(s_hm, NC * l + c + 1)
                    A(hid_h[:, MH:2 * MH, c * L:(c + 1) * L],
                      tmp[2][:, 0:MH * L].rearrange("p (h t) -> p h t", h=MH), ACT.Copy).then_inc(s_hmh, 1)

                act.wait_ge(s_kvo, 16 * 6 * (l + 1))
                scores_exp(0)
                token_major(0, ktok, s_tk, s_kev)
                fill("a", NC, 0)
                fill("a", NC, 1)
                fill("p", 0, 0)
                token_major(0, vtok, s_tv, s_vev)
                fill("p", 0, 1)
                for c in range(NC):
                    a = NC * l + c
                    act.wait_ge(s_nd, a + 1)
                    A(z[:, 4:8, c * L:(c + 1) * L], ch(6, 0), ACT.Copy)
                    A(dsq[:], ch(6, 1), ACT.Square, scale=EPS ** 0.5).then_inc(s_dsq, 1)
                    A(hsq[:], ch(6, 0), ACT.Square).then_inc(s_hsq, 1)
                    if c:
                        finish(c - 1)
                    fill("m", c, 0)
                    if c < SAMPLE:
                        scores_exp(c + 1)
                        if c % 2:
                            token_major((c + 1) // 2, vtok, s_tv, s_vev)
                    act.wait_ge(s_s2, a + 1)
                    link(A(rstd[:], m2, ACT.Ln))
                    link(A(rstd[:], rstd[:], ACT.Exp, scale=-0.5))
                    A(r2, rstd[:], ACT.Square, scale=0.5 ** 0.5).then_inc(s_rs, 1)
                    fill("m", c, 1)
                    if c < SAMPLE and c % 2:
                        token_major((c + 1) // 2, ktok, s_tk, s_kev)
                finish(NC - 1)
                fill("m", NC, 0)
                fill("m", NC, 1)
                act.wait_ge(s_co, 2 * (l + 1))
                for w, (co, no) in enumerate(((p_C, p_n), (s_C, s_n))):
                    act.dma_start(co[l, 0].rearrange("h v k -> v h k"),
                                  cout[:, w, :].rearrange("p (h k) -> p h k", h=MH)).then_inc(s_cno, 16)
                    act.dma_start(no[l, 0], kout[0:MH, w, :]).then_inc(s_cno, 16)
                for s in range(S_WOM, S_MLP):
                    split(g0 + s + 2)
                    for k in range(2):
                        norm_tile(2 * l + 1, 2 * (s - S_WOM) + k)
                rms_of(2 * l + 1)

                tile_m = TILES * l + S_MLP + 8
                def mlp_split(j, q, m):
                    r = ((q + 2) % 4) // 2
                    act.wait_ge(s_ld[r], landed[PAIRS * l + 16 + r] + 16 * m)
                    act.wait_ge(s_tile, tile_m + j + 1)
                    A(w_hi[:, (g0 + S_MLP + q) % 2, :].rearrange("p (k c) -> p k c", k=KT),
                      stage[:, r, :].rearrange("p (k q c) -> p k q c", k=KT, q=2)[:, :, q % 2, :],
                      ACT.Copy).then_inc(s_hi, 1)

                def up_step(g, i, q):
                    mlp_split(16 * g + 4 * i + q, q, 4 * g + i + (q + 2) // 4)
                    act.wait_ge(s_hh, 8 * GROUPS * l + 8 * g + 4 * i + q + 1)
                    A(hid_h[:, bass.ds(4 * i + q, 1), :], tmp[1][:].rearrange("p (o t) -> p o t", o=1), ACT.Copy).then_inc(s_hidh, 1)

                with act.Fori(0, GROUPS - 1) as g:
                    with act.Fori(0, 2) as i:
                        for q in range(4):
                            up_step(g, i, q)
                    with act.Fori(0, 2) as i:
                        for q in range(4):
                            mlp_split(16 * g + 8 + 4 * i + q, q, 4 * g + 2 + i + (q + 2) // 4)
                with act.Fori(0, 2) as i:
                    for q in range(4):
                        up_step(GROUPS - 1, i, q)
                for k in range(KT):
                    split(g0 + SLOTS - KT + k + 2)
                    norm_tile(2 * l + 2, k)
            rms_of(2 * DEPTH)
            for t in range(5):
                act.wait_ge(s_ye, 2 * t + 2)
                dst = y_prompt[0, t * P:(t + 1) * P, :] if t < 4 else y_sample[0]
                n = P if t < 4 else DEC
                act.dma_start(dst, zf[0:n, t * DM:(t + 1) * DM]).then_inc(s_yo, 16)
            act.wait_ge(s_yo, 5 * 16)
            act.wait_ge(s_cno, 16 * 4 * DEPTH)
            act.wait_ge(s_kvo, 16 * 6 * DEPTH)

        @block.vector
        def _(dve):
            chain = [0]

            def link(ins):
                chain[0] += 1
                ins.then_inc(s_dve, 1)
                dve.wait_ge(s_dve, chain[0])

            V = nc.vector
            f = lambda ap: ap.bitcast(F32)

            def split(g):
                if g >= SLOTS * DEPTH:
                    return
                l, s = g // SLOTS, g % SLOTS
                n = PAIRS * l + (s + 1) // 2
                dve.wait_ge(s_hi, g + 1)
                if s == 0:
                    pick = lambda w: w[:, g % 2, :].rearrange("p (k a b) -> p k a b", k=KT, b=32)[:, :, 0:2, 0:MH]
                    src = stage[:, n % 2, 0:8 * KT].rearrange("p (k a c) -> p k a c", k=KT, a=2)
                else:
                    k = KT if s < S_WOA or s >= S_MLP else 4
                    pick = lambda w: w[:, g % 2, :].rearrange("p (k c) -> p k c", k=k)
                    src = stage[:, n % 2, :].rearrange("p (k q c) -> p k q c", k=k, q=2)[:, :, (s + 1) % 2, :]
                V.tensor_tensor(pick(w_lo), src, f(pick(w_hi)), ALU.subtract).then_inc(s_lo, 1)

            def norm_tile(n, k):
                dve.wait_ge(s_xh, KT * n + k + 1)
                V.scalar_tensor_tensor(xl[:, k, :], x[:, k, :], gain(n, k), f(xh[:, k, :]),
                                       ALU.mult, ALU.subtract).then_inc(s_xl, 1)

            def rms_of(n):
                dve.wait_ge(s_r0, n + 1)
                link(V.scalar_tensor_tensor(tmp[1][:], tmp[1][:], -1.0, tmp[0][:], ALU.mult, ALU.mult))
                V.scalar_tensor_tensor(rms[:], tmp[1][:], 1.5, rms[:], ALU.add, ALU.mult).then_inc(s_rms, 1)
                dve.wait_ge(s_rms, n + 1)

            V.memset(eps_col, EPS).then_inc(s_gain, 1)
            V.memset(f(w_hi[:, 0, :]), 0.0).then_inc(s_gz, 1)
            V.memset(f(w_lo[:, 0, :]), 0.0).then_inc(s_gz, 1)
            for b in (bcr, ncr, acl):
                link(V.memset(f(b[:]), 0.0))
            dve.wait_ge(s_par, 11 * 16)
            link(V.tensor_scalar(small[:, 16:24], small[:, 8:16], -1.0, None, ALU.mult))
            dve.wait_ge(s_xT, 1)
            V.tensor_copy(gains[:], psum[:, 4, 0:56]).then_inc(s_gain, 1)
            dve.wait_ge(s_xT, 2)
            V.tensor_copy(x[:, :, SEQ:T], psum[:, 7, :].rearrange("p (k t) -> p k t", k=KT)).then_inc(s_xs, 1)
            dve.wait_ge(s_xs, 1)
            for k in range(KT):
                dve.wait_ge(s_xT, 3 + k)
                V.tensor_copy(x[:, k, 0:SEQ], psum[:, k % 4, :]).then_inc(s_x0, 1)
            for k in range(KT):
                norm_tile(0, k)
            dve.wait_ge(s_gz, 2)
            split(0)
            split(1)

            rotated = [0]

            def rotary(l, s, writes):
                t = TILES * l + tile_of(s)
                src = acc[t % 2]
                dve.wait_ge(s_tile, t + 1)
                if rotated[0]:
                    dve.wait_ge(s_rot, rotated[0])
                rotated[0] += 1
                mask = list(range(32))
                for i in range(ROPE_DIM // 2):
                    mask[i], mask[i + ROPE_DIM // 2] = i + ROPE_DIM // 2, i
                link(V.stream_shuffle(two(tmp[0][:]), src, mask))
                V.tensor_tensor(two(tmp[1][:]), src, two(z[:, 0, :]), ALU.mult).then_inc(s_evac, 1)
                link(V.tensor_tensor(tmp[0][:], tmp[0][:], z[:, 1, :], ALU.mult))
                dve.wait_ge(s_evac, t + 1)
                for n, (out, sl) in enumerate(writes):
                    t0, t1 = tmp[0][sl, :], tmp[1][sl, :]
                    if len(out.shape) == 3:
                        t0, t1 = (v.rearrange("p (c q) -> p c q", c=NC) for v in (t0, t1))
                    ins = V.tensor_tensor(out, t0, t1, ALU.add)
                ins.then_inc(s_rot, 1)

            for l in range(DEPTH):
                g0, t0 = SLOTS * l, TILES * l

                def plain(s, out, scale=None):
                    t = t0 + tile_of(s)
                    dve.wait_ge(s_tile, t + 1)
                    if scale is None:
                        return V.tensor_tensor(two(out), acc[t % 2], two(rms[:]), ALU.mult).then_inc(s_evac, 1)
                    return V.scalar_tensor_tensor(two(out), acc[t % 2], scale, two(rms[:]), ALU.mult, ALU.mult).then_inc(s_evac, 1)

                def add_x(t, m):
                    dve.wait_ge(s_tile, t + 1)
                    V.tensor_tensor(two(x[:, m, :]), two(x[:, m, :]), acc[t % 2], ALU.add).then_inc(s_evac, 1)

                for b in qbd:
                    V.memset(b[0:AD, :, :, 1, :].rearrange("p j c q -> p (j c) q"), 0.0)
                    link(V.memset(b[AD:P, :, :, 0, :].rearrange("p j c q -> p (j c) q"), 0.0))
                rms_of(2 * l)
                dve.wait_ge(s_tab, 16 * (l + 1))
                V.tensor_tensor(z[:, 0, :], z[:, 0, :], rms[:], ALU.mult)
                link(V.tensor_tensor(z[:, 1, :], z[:, 1, :], rms[:], ALU.mult))
                dve.wait_ge(s_tile, t0 + 1)
                a0 = acc[t0 % 2]
                V.tensor_tensor(two(row(0)), a0[0:MH], two(rms[0:MH, :]), ALU.mult)
                link(V.tensor_tensor(two(row(1, 1)), a0[32:32 + MH], two(rms[32:32 + MH, :]), ALU.mult))
                link(V.tensor_scalar(row(4, 1), row(1, 1), bf_c[l], 0.0, ALU.add, ALU.min))
                V.tensor_scalar(row(0), row(0), bi_c[l], None, ALU.add).then_inc(s_evac, 1)
                V.memset(row(5), 1.0).then_inc(s_gf, 1)
                split(g0 + 2)
                rotary(l, S_AK, [(kT[:], slice(0, P))])
                split(g0 + 3)
                plain(S_AV, vT[:])
                split(g0 + 4)
                dve.wait_ge(s_gf, l + 1)
                link(V.memset(row(5).rearrange("p (c t) -> p c t", c=NC)[:, :, 0:1], 0.0))
                dve.wait_ge(s_g1, l + 1)
                link(V.tensor_tensor(row(1), row(4, 1), row(3, 1), ALU.subtract))
                link(V.tensor_tensor_scan(row(2), row(5), row(1), 0.0, ALU.mult, ALU.add))
                link(V.tensor_tensor(row(3), row(0), row(2), ALU.subtract))
                last_of = lambda r, c0, c1: r.rearrange("p (c t) -> p c t", c=NC)[:, c0:c1, L - 1:L]
                first_of = lambda r, c0, c1: r.rearrange("p (c t) -> p c t", c=NC)[:, c0:c1, 0:1]
                link(V.memset(row(4), 0.0))
                link(V.tensor_copy(first_of(row(4), 1, SAMPLE), last_of(row(2), 0, SAMPLE - 1)))
                link(V.tensor_tensor_scan(row(6)[:, 0:SEQ], row(4)[:, 0:SEQ], row(3)[:, 0:SEQ], 0.0, ALU.add, ALU.max))
                link(V.tensor_tensor_scan(row(6)[:, SEQ:T], row(4)[:, SEQ:T], row(3)[:, SEQ:T], ms_c[l], ALU.add, ALU.max))
                rotary(l, S_AQ, [(qbd[0][0:AD, 0, :, 0, :], slice(0, AD)), (qbd[0][AD:P, 0, :, 1, :], slice(AD, P))])
                split(g0 + 5)
                col = lambda i: g9[0:MH, 16 * i:16 * i + NC].rearrange("p (c o) -> p c o", o=1)
                if l:
                    dve.wait_ge(s_kvo, 16 * 6 * l)
                link(V.tensor_tensor(col(0), last_of(row(6), 0, NC), last_of(row(2), 0, NC), ALU.add))
                V.memset(g9[0:MH, 16:17], 0.0)
                V.tensor_copy(g9[0:MH, 17:17 + SAMPLE - 1], g9[0:MH, 0:SAMPLE - 1])
                link(V.tensor_copy(g9[0:MH, 16 + SAMPLE:17 + SAMPLE], ms_c[l]))
                chunks = lambda r: r.rearrange("p (c t) -> p c t", c=NC)
                V.tensor_tensor(chunks(row(7)), col(1).to_broadcast([MH, NC, L]), chunks(row(6)), ALU.subtract)
                V.tensor_tensor(row(1, 2), row(2), row(6), ALU.add)
                V.tensor_tensor(chunks(row(5)), chunks(row(3)), last_of(row(6), 0, NC).to_broadcast([MH, NC, L]), ALU.subtract)
                V.tensor_tensor(col(2), col(1), last_of(row(6), 0, NC), ALU.subtract).then_inc(s_g2, 1)
                V.tensor_scalar(ncr[0:MH, :], row(6), -1.0, None, ALU.mult)
                link(V.tensor_copy(acl[0:MH, 0:T], row(3)))
                V.scalar_tensor_tensor(ncr[32:32 + MH, :], row(6), -1.0, f(ncr[0:MH, :]), ALU.mult, ALU.subtract)
                V.tensor_tensor(acl[32:32 + MH, 0:T], row(3), f(acl[0:MH, 0:T]), ALU.subtract)
                rotary(l, S_AQ + 1, [(qbd[0][0:AD, 1, :, 0, :], slice(0, AD)), (qbd[0][AD:P, 1, :, 1, :], slice(AD, P))])
                split(g0 + 6)
                dve.wait_ge(s_g3, l + 1)
                link(V.tensor_scalar(row(1, 2), row(1, 2), EPS, E_TOP, ALU.mult, ALU.min))
                V.tensor_copy(bcr[0:MH, :], row(7))
                link(V.tensor_scalar(bcr[64:64 + MH, :], row(1, 2), E_LOW, None, ALU.max))
                V.tensor_tensor(bcr[32:32 + MH, :], row(7), f(bcr[0:MH, :]), ALU.subtract)
                V.scalar_tensor_tensor(bcr[96:96 + MH, :], row(1, 2), E_LOW, f(bcr[64:64 + MH, :]), ALU.max, ALU.subtract)
                V.tensor_tensor(g9[0:MH, 48:48 + MH * NC].rearrange("p (c h) -> p c h", c=NC), col(2).to_broadcast([MH, NC, MH]),
                                ident[0:MH, 0:MH].rearrange("p (o h) -> p o h", o=1).to_broadcast([MH, NC, MH]),
                                ALU.mult).then_inc(s_g4, 1)
                for j in range(2, AJ):
                    rotary(l, S_AQ + j, [(qbd[1][0:AD, j - 2, :, 0, :], slice(0, AD)), (qbd[1][AD:P, j - 2, :, 1, :], slice(AD, P))])
                    split(g0 + S_AQ + j + 2)
                if l:
                    dve.wait_ge(s_cno, 16 * 4 * l)
                dve.wait_ge(s_set, l + 1)
                V.tensor_copy(cst[:, 1, :, 0:MD], psum[:, 5, :].rearrange("p (h v) -> p h v", h=MH))
                V.tensor_copy(vwin[0:L, SAMPLE, :], psum[0:L, 7, 0:P])
                V.tensor_copy(gT[:, 0, 0:(NP - 1) * MH], psum[:, 7, P:P + (NP - 1) * MH])
                V.tensor_copy(gT[0:L, 0, (NP - 1) * MH:NP * MH], psum[0:L, 7, P + (NP - 1) * MH:P + NP * MH])
                V.tensor_copy(gT[:, 1, :], psum[:, 7, 164:164 + NC * MH])
                V.tensor_copy(cst[:, 1, :, MD], gains[:, 48 + MH * l:52 + MH * l])
                V.tensor_copy(kout[:, 0, :], psum[:, 7, 200:200 + P])
                V.tensor_copy(kout[0:DEC, 1, :], psum[0:DEC, 7, 328:328 + P]).then_inc(s_setd, 1)
                dve.wait_ge(s_set2, l + 1)
                V.tensor_copy(kcT[:], psum[:, 4, 0:P]).then_inc(s_setd2, 1)

                def gate_of(h):
                    zz = z[:, 12 + h, :]
                    dve.wait_ge(s_moe, MH * l + h + 1)
                    link(V.tensor_scalar(zz, zz, 1.0, None, ALU.add))
                    link(V.reciprocal(zz, zz))
                    V.tensor_scalar(zz, zz, gains[:, 40 + MH * l + h:41 + MH * l + h], None, ALU.mult).then_inc(s_moz, 1)

                def fill(kind, c, i):
                    for s in slots_done(kind, c, i):
                        if s < S_WOA:
                            tile = s - S_MK + (4 if S_MO <= s < S_MV else -4 if s >= S_MV else 0)
                            plain(s, z[:, tile, :], K_SCALE if s < S_MQ else None)
                            split(g0 + s + 2)
                            if S_MO < s <= S_MV:
                                gate_of(s - S_MO - 1)
                        else:
                            for m in range(2):
                                add_x(t0 + tile_of(s) + m, 2 * (s - S_WOA) + m)
                            split(g0 + s + 2)

                for c in range(NC):
                    a, nk = NC * l + c, keys(c)
                    dve.wait_ge(s_sc, a + 1)
                    for b in range(2):
                        ins = V.tensor_reduce(att_s[:, 2 * b:2 * b + 2],
                                              psum[:, 4 + b, 0:2 * (WIN + L)].rearrange("p (j k) -> p j k", j=2)[:, :, 0:nk],
                                              AX.X, ALU.max)
                    link(ins)
                    V.scalar_tensor_tensor(att_s[:, 4:8], att_s[:, 0:4], -A_SCALE, nsink_c[l], ALU.mult, ALU.min).then_inc(s_neg, 1)
                    dve.wait_ge(s_neg, a + 1)
                    V.tensor_tensor(att_s[:, 12:16], att_s[:, 4:8], sink_c[l], ALU.add).then_inc(s_sn, 1)
                    dve.wait_ge(s_p, a + 1)
                    link(V.tensor_tensor(att_s[:, 20:24], att_s[:, 8:12], att_s[:, 16:20], ALU.add))
                    link(V.reciprocal(att_s[:, 24:28], att_s[:, 20:24]))
                    for j in range(AJ):
                        ins = V.tensor_scalar(prob[:, j, 0:nk], prob[:, j, 0:nk], att_s[:, 24 + j:25 + j], None, ALU.mult)
                    ins.then_inc(s_pn, 1)
                    fill("a", c, 0)
                    dve.wait_ge(s_T, a + 1)
                    if nk != WIN:
                        V.tensor_copy(pT2[:], psum[0:L, 7, :]).then_inc(s_pt2, 1)
                    fill("a", c, 1)
                    dve.wait_ge(s_aoh, a + 1)
                    o4 = psum[:, 6, :].rearrange("p (j g q) -> p j g q", j=AJ, g=AG)
                    cs = slice(c * L, (c + 1) * L)
                    V.tensor_tensor(hid_l[0:AD, 0:AJ, cs], o4[0:AD, :, 0, :], f(hid_h[0:AD, 0:AJ, cs]), ALU.subtract)
                    V.tensor_tensor(hid_l[AD:P, 0:AJ, cs], o4[AD:P, :, 1, :], f(hid_h[AD:P, 0:AJ, cs]), ALU.subtract).then_inc(s_ao, 1)
                    fill("a", c, 2)

                ch = lambda b, half: psum[:, b, half * MH * L:(half + 1) * MH * L].rearrange("p (h t) -> p h t", h=MH)
                m2, r2 = (tmp[0][:, i * MH * L:(i + 1) * MH * L].rearrange("p (h t) -> p h t", h=MH) for i in range(2))
                hm = tmp[2][:, 0:MH * L].rearrange("p (h t) -> p h t", h=MH)

                def weighted(c):
                    w, q = int(c == SAMPLE), slice((c % 2) * L, (c % 2 + 1) * L)
                    dve.wait_ge(s_swp, NC * l + c + 1)
                    dve.wait_ge(s_ex, NC * l + c + 1)
                    ins = V.tensor_tensor(sw[q], ch(4, 0)[q], eexp[q], ALU.mult)
                    if c:
                        link(V.tensor_tensor(qw[:], z[:, 4:8, c * L:(c + 1) * L], ch(4, 1), ALU.mult))
                        dve.wait_ge(s_st, NC * l + c)
                        ins = V.tensor_tensor(nq[:], qw[:], cst[:, w, :, MD:MD + 1].to_broadcast([P, MH, L]), ALU.mult)
                    ins.then_inc(s_sw, 1)

                def low_part(c):
                    dve.wait_ge(s_hmh, NC * l + c + 1)
                    V.tensor_tensor(hid_l[:, MH:2 * MH, c * L:(c + 1) * L], hm, f(hid_h[:, MH:2 * MH, c * L:(c + 1) * L]),
                                    ALU.subtract).then_inc(s_hmd, 1)

                weighted(0)
                fill("a", NC, 0)
                fill("a", NC, 1)
                fill("p", 0, 0)
                fill("p", 0, 1)
                for c in range(NC):
                    a, w = NC * l + c, int(c == SAMPLE)
                    dve.wait_ge(s_dsq, a + 1)
                    dve.wait_ge(s_em, a + 1)
                    V.tensor_tensor(dsq[:], dsq[:], ch(5, 0), ALU.max).then_inc(s_mx, 1)
                    if c > 1:
                        dve.wait_ge(s_st, a)
                    for h in (MH - 1, 0, 1, 2):
                        if h == MH - 1:
                            dve.wait_ge(s_nu, a + 1)
                            new = psum[:, 4, 0:MD + 1]
                        else:
                            if h == 0:
                                dve.wait_ge(s_u, a + 1)
                            new = psum[:, 7, h * (MD + 1):(h + 1) * (MD + 1)]
                        if c == 0:
                            ins = V.tensor_copy(cst[:, 0, h], new)
                        else:
                            ins = V.scalar_tensor_tensor(cst[:, w, h], cst[:, w, h], gT[:, 1, c * MH + h:c * MH + h + 1], new,
                                                         ALU.mult, ALU.add)
                        if h == MH - 1:
                            ins.then_inc(s_nn, 1)
                    ins.then_inc(s_st, 1)
                    if c:
                        low_part(c - 1)
                    fill("m", c, 0)
                    dve.wait_ge(s_ssm, a + 1)
                    dve.wait_ge(s_mx, a + 1)
                    V.scalar_tensor_tensor(m2, ch(6, 0), 1.0 / MD, dsq[:], ALU.mult, ALU.add).then_inc(s_s2, 1)
                    if c < SAMPLE:
                        weighted(c + 1)
                    dve.wait_ge(s_rs, a + 1)
                    link(V.scalar_tensor_tensor(r2, r2, -1.0, m2, ALU.mult, ALU.mult))
                    link(V.scalar_tensor_tensor(rstd[:], r2, 1.5, rstd[:], ALU.add, ALU.mult))
                    link(V.tensor_tensor(rstd[:], rstd[:], z[:, 12:16, c * L:(c + 1) * L], ALU.mult))
                    V.tensor_tensor(hm, z[:, 4:8, c * L:(c + 1) * L], rstd[:], ALU.mult).then_inc(s_hm, 1)
                    fill("m", c, 1)
                low_part(NC - 1)
                fill("m", NC, 0)
                fill("m", NC, 1)
                for w in range(2):
                    dve.wait_ge(s_ct, 2 * (l + 1))
                    V.tensor_copy(cout[:, w, :], psum[:, 6 + w, :])
                    V.tensor_copy(kout[0:MH, w, :], psum[0:MH, 4, w * P:(w + 1) * P]).then_inc(s_co, 1)
                for s in range(S_WOM, S_MLP):
                    for m in range(2):
                        add_x(t0 + tile_of(s) + m, 2 * (s - S_WOM) + m)
                    split(g0 + s + 2)
                    for m in range(2):
                        norm_tile(2 * l + 1, 2 * (s - S_WOM) + m)

                tile_m, slot_m = t0 + S_MLP + 8, g0 + S_MLP
                hid0 = 8 * GROUPS * l
                rms_of(2 * l + 1)

                def mlp_split(j, q):
                    r = ((q + 2) % 4) // 2
                    pick = lambda w: w[:, (slot_m + q) % 2, :].rearrange("p (k c) -> p k c", k=KT)
                    dve.wait_ge(s_hi, slot_m + 3 + j)
                    V.tensor_tensor(pick(w_lo), stage[:, r, :].rearrange("p (k q c) -> p k q c", k=KT, q=2)[:, :, q % 2, :],
                                    f(pick(w_hi)), ALU.subtract).then_inc(s_lo, 1)

                def up_step(g, i, q):
                    j = 16 * g + 4 * i + q
                    n = hid0 + 8 * g + 4 * i + q + 1
                    dve.wait_ge(s_tile, tile_m + 1 + j)
                    V.tensor_tensor(two(tmp[0][:]), acc[(tile_m + q) % 2], two(rms[:]), ALU.mult).then_inc(s_evac, 1)
                    mlp_split(j, q)
                    dve.wait_ge(s_evac, tile_m + 1 + j)
                    V.scalar_tensor_tensor(tmp[1][:], tmp[0][:], 0.0, tmp[0][:], ALU.max, ALU.mult).then_inc(s_hh, 1)
                    dve.wait_ge(s_hidh, n)
                    V.tensor_tensor(hid_l[:, bass.ds(4 * i + q, 1), :], tmp[1][:].rearrange("p (o t) -> p o t", o=1),
                                    f(hid_h[:, bass.ds(4 * i + q, 1), :]), ALU.subtract).then_inc(s_hid, 1)

                with dve.Fori(0, GROUPS - 1) as g:
                    with dve.Fori(0, 2) as i:
                        for q in range(4):
                            up_step(g, i, q)
                    with dve.Fori(0, 2) as i:
                        for q in range(4):
                            j = 16 * g + 8 + 4 * i + q
                            dve.wait_ge(s_tile, tile_m + 1 + j)
                            xt = x[:, bass.ds(4 * i + q, 1), :].rearrange("p o (a t) -> p (o a) t", a=2)
                            V.tensor_tensor(xt, xt, acc[(tile_m + q) % 2], ALU.add).then_inc(s_evac, 1)
                            mlp_split(j, q)
                with dve.Fori(0, 2) as i:
                    for q in range(4):
                        up_step(GROUPS - 1, i, q)
                for k in range(KT):
                    add_x(t0 + TILES - KT + k, k)
                    split(g0 + SLOTS - KT + k + 2)
                    norm_tile(2 * l + 2, k)

            n = 2 * DEPTH
            rms_of(n)
            for k in range(KT):
                V.scalar_tensor_tensor(x[:, k, :], x[:, k, :], gain(n, k), rms[:],
                                       ALU.mult, ALU.mult).then_inc(s_y, 1)
            zf = z[:, :, :].rearrange("p a t -> p (a t)")
            for i in range(10):
                t, half = i // 2, i % 2
                m = P if t < 4 else DEC
                dve.wait_ge(s_yt, i + 1)
                V.tensor_copy(zf[0:m, t * DM + half * 512:t * DM + (half + 1) * 512], psum[0:m, i % 4, :]).then_inc(s_ye, 1)

        @block.tensor
        def _(pe):
            M = nc.tensor.matmul
            TR = nc.tensor.transpose
            zf = z[:, :, :].rearrange("p a t -> p (a t)")

            def products(t, lhs, k, first, last, hi_mov, lo_mov):
                ins = None
                for n, (w, mov) in enumerate(((w_hi, hi_mov), (w_hi, lo_mov), (w_lo, hi_mov))):
                    for a in range(2):
                        ins = M(acc[t % 2][:, a, :], lhs(w), mov[:, k, a * HALF:(a + 1) * HALF],
                                start=first and n == 0, stop=last and n == 2)
                return ins

            def sum_squares(n):
                pe.wait_ge(s_sum, n + 1)
                for a in range(2):
                    ins = M(psum[:, 4 + a, 0:HALF], ones, ssum[:, a * HALF:(a + 1) * HALF], start=True, stop=True)
                ins.then_inc(s_ss, 1)

            def unit(l, u):
                s, e = u // 8, u % 8
                g = SLOTS * l + s
                if e == 0:
                    pe.wait_ge(s_lo, g + 1)
                    if s == S_WOA:
                        pe.wait_ge(s_ao, NC * (l + 1))
                    if s == S_WOM:
                        pe.wait_ge(s_hmd, NC * (l + 1))
                if s < S_WOA:
                    t, k, first, last = TILES * l + s, e, e == 0, e == 7
                    if s == 0:
                        pe.wait_ge(s_xl, KT * 2 * l + k + 1)
                    lhs = lambda w: w[:, g % 2, k * P:(k + 1) * P]
                    mov = (xh, xl)
                    kk = k
                else:
                    m, k = e // 4, e % 4
                    t, first, last = TILES * l + tile_of(s) + m, k == 0, k == 3
                    lhs = lambda w: w[:, g % 2, k * 2 * P + m * P:k * 2 * P + (m + 1) * P]
                    mov = (hid_h, hid_l)
                    kk = k + (4 if s >= S_WOM else 0)
                if first and t >= 2:
                    pe.wait_ge(s_evac, t - 1)
                ins = products(t, lhs, kk, first, last, *mov)
                if last:
                    ins.then_inc(s_tile, 1)

            def fill(l, kind, c, i):
                for u in range(*fills[kind, c, i]):
                    unit(l, u)

            pe.wait_ge(s_const, 16)
            pe.wait_ge(s_par, 11 * 16)
            TR(psum[:, 4, 0:56], zf[0:56, 5 * DM + R_COLS:5 * DM + R_COLS + P], ident[0:56, 0:56]).then_inc(s_xT, 1)
            pe.wait_ge(s_xin, 5 * 16)
            for k in range(KT):
                ins = TR(psum[:, 7, k * DEC:(k + 1) * DEC], zf[0:DEC, 4 * DM + k * P:4 * DM + (k + 1) * P], ident[0:DEC, 0:DEC])
            ins.then_inc(s_xT, 1)
            for k in range(KT):
                if k >= 4:
                    pe.wait_ge(s_x0, k - 3)
                for t in range(4):
                    ins = TR(psum[:, k % 4, t * P:(t + 1) * P], zf[:, t * DM + k * P:t * DM + (k + 1) * P], ident)
                ins.then_inc(s_xT, 1)
            pe.wait_ge(s_rcon, 1)
            pe.wait_ge(s_x0, KT)

            for l in range(DEPTH):
                for u in range(8):
                    unit(l, u)
                sum_squares(2 * l)
                for u in range(8, 8 * S_MK):
                    unit(l, u)
                pe.wait_ge(s_rot, 5 * l + 1)
                pe.wait_ge(s_evac, TILES * l + S_AV + 1)
                pe.wait_ge(s_cl, 16 * 3 * (l + 1))
                pe.wait_ge(s_g4, l + 1)
                pe.wait_ge(s_rms, 2 * l + 1)
                for n in range(8):
                    TR(psum[:, 4 + n // 4 * 2, (n % 4) * P:(n % 4 + 1) * P], vT[:, n * L:n * L + P], ident)
                for h in range(MH):
                    TR(psum[:, 5, h * P:(h + 1) * P], pT1[:, h * P:(h + 1) * P], ident)
                TR(psum[0:L, 7, 0:P], vT[:, SEQ:T], ident)
                for p in range(NP):
                    r = L if p == NP - 1 else P
                    TR(psum[0:r, 7, P + p * MH:P + (p + 1) * MH], row(5)[:, p * P:p * P + r], ident[0:MH, 0:MH])
                M(psum[:, 7, 164:164 + NC * MH], ones[0:MH, :], g9[0:MH, 48:48 + NC * MH], start=True, stop=True)
                TR(psum[:, 7, 200:200 + P], kT[:, SEQ - WIN:SEQ], ident)
                TR(psum[0:DEC, 7, 328:328 + P], kT[:, SEQ:T], ident).then_inc(s_set, 1)
                pe.wait_ge(s_seta, l + 1)
                TR(psum[:, 4, 0:P], kraw[:], ident).then_inc(s_set2, 1)
                pe.wait_ge(s_setd, l + 1)
                pe.wait_ge(s_setd2, l + 1)
                pe.wait_ge(s_rot, 5 * (l + 1))

                for c in range(NC):
                    a, nk = NC * l + c, keys(c)
                    for j in range(AJ):
                        out = psum[:, 4 + j // 2, (j % 2) * (WIN + L):(j % 2) * (WIN + L) + nk]
                        q = qbd[j // 2][:, j % 2, c].rearrange("p g q -> p (g q)")
                        if c == SAMPLE:
                            M(out[:, 0:WIN], q, kcT[:], start=True, stop=True)
                            ins = M(out[:, WIN:nk], q, kT[:, SEQ:T], start=True, stop=True)
                        else:
                            ins = M(out, q, kT[:, (c + 1) * L - nk:(c + 1) * L], start=True, stop=True)
                    ins.then_inc(s_sc, 1)
                    fill(l, "a", c, 0)
                    pe.wait_ge(s_pn, a + 1)
                    if a:
                        pe.wait_ge(s_ao, a)
                    if n_pt1(l, c):
                        pe.wait_ge(s_pt1, n_pt1(l, c))
                    if n_pt2(l, c):
                        pe.wait_ge(s_pt2, n_pt2(l, c))
                    old = nk // P * P
                    for j in range(AJ):
                        if old:
                            ins = TR(psum[:, 6, j * P:(j + 1) * P], prob[:, j, 0:P], ident)
                        if nk != WIN:
                            ins = TR(psum[0:L, 7, j * P:(j + 1) * P], prob[:, j, old:nk], ident)
                    ins.then_inc(s_T, 1)
                    fill(l, "a", c, 1)
                    if old:
                        pe.wait_ge(s_pt1, n_pt1(l, c) + 1)
                        older = vcache[:] if c == SAMPLE else vwin[:, max(c - 2, 0), :]
                        ins = M(psum[:, 6, :], older, pT1[:], start=True, stop=nk == WIN)
                    if nk != WIN:
                        pe.wait_ge(s_pt2, n_pt2(l, c) + 1)
                        ins = M(psum[:, 6, :], vwin[0:L, c, :], pT2[:], start=not old, stop=True)
                    ins.then_inc(s_pv, 1)
                    fill(l, "a", c, 2)

                sel = lambda i: rconst[:, R_SEL + i * P:R_SEL + (i + 1) * P]
                head = lambda i, h: slice(i * MH * L + h * L, i * MH * L + (h + 1) * L)

                def scores(c):
                    p0 = c // 2 * P
                    cs = slice(c * L, (c + 1) * L)
                    if c:
                        pe.wait_ge(s_mx, NC * l + c)
                    M(psum[:, 5, 0:MH * L], rconst[:, R_ID:R_ID + P], rconst[:, R_NEG:R_NEG + MH * L], start=True, stop=False)
                    M(psum[:, 5, 0:MH * L], acl[:, p0:p0 + P], rconst[:, R_ROW:R_ROW + MH * L], start=False, stop=False)
                    for h in range(MH):
                        ins = M(psum[:, 5, head(0, h)], sel(h), ncr[:, cs], start=False, stop=h == MH - 1)
                    ins.then_inc(s_e, 1)
                    if c:
                        pe.wait_ge(s_nn, NC * l + c)
                    r = L if c == SAMPLE else P
                    for h in range(MH):
                        ins = M(psum[0:r, 4, head(0, h)], z[:, h, p0:p0 + r], z[:, 4 + h, cs], start=True, stop=True)
                    if c:
                        for h in range(MH):
                            ins = M(psum[:, 4, head(1, h)], sel(h), bcr[:, cs], start=True, stop=True)
                    ins.then_inc(s_swp, 1)

                def token_major(p, tile, signal):
                    r = L if p == NP - 1 else P
                    for h in range(MH):
                        ins = TR(psum[0:r, 7, h * MD:(h + 1) * MD], z[:, tile + h, p * P:p * P + r], ident)
                    ins.then_inc(signal, 1)

                pe.wait_ge(s_evac, TILES * l + S_MO)
                scores(0)
                token_major(0, 0, s_tk)
                fill(l, "a", NC, 0)
                fill(l, "a", NC, 1)
                fill(l, "p", 0, 0)
                pe.wait_ge(s_kev, NP * l + 1)
                pe.wait_ge(s_evac, TILES * l + S_WOA)
                token_major(0, 8, s_tv)
                fill(l, "p", 0, 1)
                pe.wait_ge(s_ao, NC * (l + 1))
                for c in range(NC):
                    a, w, pair = NC * l + c, int(c == SAMPLE), NP * l + c // 2
                    cs, q = slice(c * L, (c + 1) * L), slice((c % 2) * L, (c % 2 + 1) * L)
                    pe.wait_ge(s_sw, a + 1)
                    pe.wait_ge(s_vev, pair + 1)
                    if c:
                        pe.wait_ge(s_st, a)
                        pe.wait_ge(s_s2, a)
                    for h in range(MH):
                        M(psum[:, 6, head(0, h)], vtok[q, h], sw[q, h], start=True, stop=c == 0)
                        if c:
                            M(psum[:, 6, head(0, h)], cst[:, w, h, 0:MD], qw[:, h], start=False, stop=True)
                    for h in range(MH):
                        ins = M(psum[:, 5, head(0, h)], sel(MH + h), bcr[:, cs], start=True, stop=True)
                    ins.then_inc(s_em, 1)
                    if c:
                        pe.wait_ge(s_dn, (NC - 1) * l + c)
                    den = nq[:] if c else sw[q]
                    M(psum[:, 6, MH * L:2 * MH * L], ones[0:P if c else L, :], den.rearrange("p h t -> p (h t)"),
                      start=True, stop=True).then_inc(s_nd, 1)
                    pe.wait_ge(s_kev, pair + 1)
                    pe.wait_ge(s_wv, pair + 1)
                    M(psum[:, 4, 0:MD + 1], ktok[q, MH - 1], wsv[q, MH - 1], start=True, stop=True).then_inc(s_nu, 1)
                    for h in range(MH - 1):
                        ins = M(psum[:, 7, h * (MD + 1):(h + 1) * (MD + 1)], ktok[q, h], wsv[q, h], start=True, stop=True)
                    ins.then_inc(s_u, 1)
                    fill(l, "m", c, 0)
                    pe.wait_ge(s_hsq, a + 1)
                    M(psum[:, 6, 0:MH * L], ones, hsq[:].rearrange("p h t -> p (h t)"), start=True, stop=True).then_inc(s_ssm, 1)
                    if c < SAMPLE:
                        scores(c + 1)
                        if c % 2:
                            pe.wait_ge(s_st, a + 1)
                            token_major((c + 1) // 2, 8, s_tv)
                    fill(l, "m", c, 1)
                    if c < SAMPLE and c % 2:
                        pe.wait_ge(s_vev, pair + 2)
                        token_major((c + 1) // 2, 0, s_tk)
                fill(l, "m", NC, 0)
                fill(l, "m", NC, 1)
                pe.wait_ge(s_st, NC * (l + 1))
                pe.wait_ge(s_s2, NC * (l + 1))
                for w in range(2):
                    for h in range(MH):
                        TR(psum[:, 6 + w, h * P:(h + 1) * P], cst[:, w, h, 0:MD], ident)
                    TR(psum[0:MH, 4, w * P:(w + 1) * P], cst[:, w, :, MD], ident).then_inc(s_ct, 1)
                for u in range(8 * S_WOM, 8 * S_MLP):
                    unit(l, u)
                pe.wait_ge(s_rs, NC * (l + 1))
                pe.wait_ge(s_co, 2 * (l + 1))

                tile_m, slot_m, hid0 = TILES * l + S_MLP + 8, SLOTS * l + S_MLP, 8 * GROUPS * l

                def mlp_slot(g, down, i, q):
                    j = 16 * g + 8 * down + 4 * i + q
                    pe.wait_ge(s_lo, slot_m + 1 + j)
                    pe.wait_ge(s_evac, tile_m - 1 + j)
                    for k in range(KT):
                        if down and q == 0:
                            pe.wait_ge(s_hid, hid0 + 8 * g + k + 1)
                        lhs = lambda w: w[:, (slot_m + q) % 2, k * P:(k + 1) * P]
                        mov = (hid_h, hid_l) if down else (xh, xl)
                        ins = products(tile_m + q, lhs, k, k == 0, k == KT - 1, *mov)
                    ins.then_inc(s_tile, 1)

                pe.wait_ge(s_xl, KT * (2 * l + 2))
                for j in range(KT):
                    mlp_slot(0, 0, j // 4, j % 4)
                    if j == 0:
                        sum_squares(2 * l + 1)
                with pe.Fori(0, 2) as i:
                    for q in range(4):
                        mlp_slot(0, 1, i, q)
                with pe.Fori(1, GROUPS) as g:
                    for down in range(2):
                        with pe.Fori(0, 2) as i:
                            for q in range(4):
                                mlp_slot(g, down, i, q)

            n = 2 * DEPTH
            sum_squares(n)
            pe.wait_ge(s_y, KT)
            pe.wait_ge(s_evac, TILES * DEPTH)
            for i in range(10):
                t, half = i // 2, i % 2
                m = P if t < 4 else DEC
                if i >= 4:
                    pe.wait_ge(s_ye, i - 3)
                for k in range(4):
                    ins = TR(psum[0:m, i % 4, k * P:(k + 1) * P], x[:, half * 4 + k, t * P:t * P + m], ident)
                ins.then_inc(s_yt, 1)


def norm_rows(g):
    return g.rearrange("l (k p) -> (l k) p", p=P)


_INS = ["x_prompt", "x_sample", "cache_k", "cache_v", "state_C", "state_n", "state_m", "norm1_g", "w_in", "gate_b",
        "attn_sink", "mnorm_g", "w_out", "norm2_g", "w_up", "w_down", "final_g"]
_OUTS = [(1, SEQ, DM), (1, DEC, DM)] + [(DEPTH, 1, WIN, AG, AD)] * 2 + [
    (DEPTH, 1, MH, MD, MD), (DEPTH, 1, MH, MD), (DEPTH, 1, MH)] + [(DEPTH, 1, DEC, AG, AD)] * 2 + [
    (DEPTH, 1, MH, MD, MD), (DEPTH, 1, MH, MD), (DEPTH, 1, MH)]


def kernel(**inputs):
    import numpy as _np
    import concourse.bacc as _bacc
    from concourse.bass_utils import run_bass_kernel_spmd as _run

    nc = _bacc.Bacc("TRN2", target_bir_lowering=False, num_devices=1)
    arrays = {f"in_{name}": _np.ascontiguousarray(inputs[name]) for name in _INS}
    arrays["in_const"] = constants()
    ins = [nc.dram_tensor(name, a.shape, F32, kind="ExternalInput").ap() for name, a in arrays.items()]
    outs = [nc.dram_tensor(f"out_{i}", shape, F32, kind="ExternalOutput").ap() for i, shape in enumerate(_OUTS)]
    hymba_step(nc, ins, outs)
    r = _run(nc, [arrays], core_ids=[0])
    return tuple(r.results[0][f"out_{i}"] for i in range(len(_OUTS)))
```

```python
from contextlib import ExitStack

import concourse.bass as bass
from concourse import mybir

F32 = mybir.dt.float32
F32R = mybir.dt.float32r
ALU = mybir.AluOpType
ACT = mybir.ActivationFunctionType
AX = mybir.AxisListType

P = 128
DM = 1024
KT = DM // P
SEQ, DEC = 512, 64
T = SEQ + DEC
HALF = T // 2
DEPTH = 2
L = 64
NC = T // L
SAMPLE = NC - 1
NP = (NC + 1) // 2
WIN = 128
AH, AG, AD = 8, 2, 64
AJ = AH // AG
MH, MD = 4, 128
AQ, AKV, MW = AH * AD, AG * AD, MH * MD
COL_K, COL_V = AQ, AQ + AKV
COL_MQ = AQ + 2 * AKV
COL_MK, COL_MV, COL_MO = COL_MQ + MW, COL_MQ + 2 * MW, COL_MQ + 3 * MW
COL_GATE = COL_MQ + 4 * MW
FF = 4 * DM
GROUPS = FF // DM
EPS = 1e-6
A_SCALE = float(AD) ** -0.5
K_SCALE = float(MD) ** -0.5
ROPE_DIM = AD // 4
E_TOP, E_LOW = 1e30, 1e-36
PAST = 1024

S_GATE = 0
S_AK, S_AV = 1, 2
S_AQ = 3
S_MK, S_MQ, S_MO, S_MV = 7, 11, 15, 19
S_WOA, S_WOM = 23, 27
S_MLP = 31
SLOTS = S_MLP + GROUPS * 2 * KT
TILES = SLOTS + 8
PAIRS = 1 + (SLOTS - 1) // 2

C_ID, C_ONE, C_COS, C_SIN = 0, 128, 256, 832
C_R = 1408
R_SEL, R_ROW, R_NEG, R_ID = 0, 1024, 1280, 1536
R_COLS = 1664


def constants():
    import numpy as np
    c = np.zeros((P, C_R + R_COLS), np.float32)
    c[:, C_ID:C_ID + P] = np.eye(P)
    c[:, C_ONE:C_ONE + P] = 1.0
    half = ROPE_DIM // 2
    inv = np.float32(500000.0) ** (-(np.arange(half, dtype=np.float32) * np.float32(2.0) / np.float32(ROPE_DIM)))
    pos = np.concatenate([np.arange(SEQ), np.arange(DEC) + PAST]).astype(np.float32)
    ang = inv.astype(np.float32)[:, None] * pos[None, :]
    c[:, C_COS:C_COS + T] = 1.0
    for g in range(AG):
        a = g * AD
        c[a:a + half, C_COS:C_COS + T] = np.cos(ang)
        c[a + half:a + 2 * half, C_COS:C_COS + T] = np.cos(ang)
        c[a:a + half, C_SIN:C_SIN + T] = -np.sin(ang)
        c[a + half:a + 2 * half, C_SIN:C_SIN + T] = np.sin(ang)
    r = c[:, C_R:]
    for h in range(MH):
        for which, base in ((h, 0), (MH + h, 64)):
            r[base + h, R_SEL + which * P:R_SEL + (which + 1) * P] = 1.0
            r[base + 32 + h, R_SEL + which * P:R_SEL + (which + 1) * P] = 1.0
        r[h, R_ROW + h * L:R_ROW + (h + 1) * L] = 1.0
        r[32 + h, R_ROW + h * L:R_ROW + (h + 1) * L] = 1.0
        for q in range(2):
            r[q * L:(q + 1) * L, R_NEG + h * L:R_NEG + (h + 1) * L] = np.tril(np.full((L, L), -1e30, np.float32), -1)
    r[:, R_ID:R_ID + P] = np.eye(P)
    return c


S_FILL = 6
A_FILL = (9, 3, 1)
P_FILL = (2, 2)
M_FILL = (1, 2)
M_LAST = (1, 0)


def hymba_step(nc, inputs, outs):
    (x_prompt, x_sample, cache_k, cache_v, state_C, state_n, state_m, norm1_g, w_in, gate_b,
     attn_sink, mnorm_g, w_out, norm2_g, w_up, w_down, final_g, const) = inputs
    (y_prompt, y_sample, p_k, p_v, p_C, p_n, p_m, s_k, s_v, s_C, s_n, s_m) = outs

    with ExitStack() as ctx:
        def sem(name):
            return ctx.enter_context(nc.semaphore(name))

        base = (nc.sbuf_base + 63) // 64 * 64
        top = [base]

        def place(name, shape, dt=F32, where=None):
            size = 4
            for n in shape[1:]:
                size *= n
            off = top[0] if where is None else where
            if where is None:
                top[0] += (size + 31) // 32 * 32
                assert top[0] <= nc.sbuf_usable_end, (name, top[0] - nc.sbuf_usable_end)
            return nc.alloc_sbuf_tensor_at(name, shape, dt, offset=off)

        x = place("x", [P, KT, T])
        xg = place("xg", [P, KT, T], where=top[0])
        xh = place("xh", [P, KT, T], F32R)
        xl = place("xl", [P, KT, T], F32R)
        hh_off = top[0]
        hid_h = place("hid_h", [P, KT, T], F32R)
        hl_off = top[0]
        hid_l = place("hid_l", [P, KT, T], F32R)
        rstage = place("rstage", [P, R_COLS], where=hl_off)
        upper = 4 * T * 4
        qbd = [place("qbd_a", [P, 2, NC, AG, L], where=hh_off + upper),
               place("qbd_b", [P, 2, NC, AG, L], where=hl_off + upper)]
        z = place("z", [P, 4 * MH, T])
        kT = place("kT", [P, T])
        vT = place("vT", [P, T])
        rms = place("rms", [P, T])
        ssum = place("ssum", [P, T])
        tmp = [place(f"tmp{i}", [P, T]) for i in range(3)]
        sqr = tmp[2]
        stage = place("stage", [P, 2, KT * 2 * P])
        w_hi = place("w_hi", [P, 2, KT * P], F32R)
        w_lo = place("w_lo", [P, 2, KT * P], F32R)
        io = place("io", [P, 2 * P])
        ident, ones = io[:, 0:P], io[:, P:2 * P]
        rconst = place("rconst", [P, R_COLS], F32R)
        bcr = place("bcr", [P, T], F32R)
        ncr = place("ncr", [P, T], F32R)
        acl = place("acl", [P, T + L], F32R)
        gains = place("gains", [P, 56])
        cst = place("cst", [P, 2, MH, MD + 1])
        g9 = place("g9", [P, 6 * 16])
        gT = place("gT", [P, 2, NC * MH])
        small = place("small", [P, 64])
        kout = place("kout", [P, 2, P])
        arena = top[0]
        vwin = place("vwin", [P, NC, P])
        kcT = place("kcT", [P, WIN])
        kraw = place("kraw", [P, WIN])
        vcache = place("vcache", [P, WIN])
        prob = place("prob", [P, AJ, WIN + L])
        pT1 = place("pT1", [P, AJ * P])
        pT2 = place("pT2", [L, AJ * P])
        end = top[0]
        top[0] = arena
        ktok = place("ktok", [P, MH, MD])
        vtok = place("vtok", [P, MH, MD])
        wsv = place("wsv", [P, MH, MD + 1])
        eexp = place("eexp", [P, MH, L])
        sw = place("sw", [P, MH, L])
        qw = place("qw", [P, MH, L])
        nq = place("nq", [P, MH, L])
        dsq = place("dsq", [P, MH, L])
        hsq = place("hsq", [P, MH, L])
        rstd = place("rstd", [P, MH, L])
        top[0] = max(top[0], end)
        cout = place("cout", [P, 2, MH * MD], where=arena)

        def row(i, q=0):
            return z[32 * q:32 * q + MH, 8 + i, :]

        eps_col = small[:, 0:1]
        sink_c = [small[:, 8 + AJ * l:8 + AJ * (l + 1)] for l in range(DEPTH)]
        nsink_c = [small[:, 16 + AJ * l:16 + AJ * (l + 1)] for l in range(DEPTH)]
        bi_c = [small[0:MH, 24 + l:25 + l] for l in range(DEPTH)]
        ms_c = [small[0:MH, 26 + l:27 + l] for l in range(DEPTH)]
        bf_c = [small[32:32 + MH, 24 + l:25 + l] for l in range(DEPTH)]
        att_s = small[:, 32:64]

        def gain(n, k):
            r = 2 * DEPTH if n == 2 * DEPTH else n // 2 + (DEPTH if n % 2 else 0)
            return gains[:, r * KT + k:r * KT + k + 1]

        psum = ctx.enter_context(nc.psum_tensor("psum", [P, 8, 512], F32))
        acc = [psum[:, 2 * i:2 * i + 2, 0:HALF] for i in range(2)]
        two = lambda ap: ap.rearrange("p (a t) -> p a t", a=2)

        s_const = sem("s_const")
        s_xin = [sem(f"s_xin{t}") for t in range(5)]
        s_par, s_sml, s_rc = sem("s_par"), sem("s_sml"), sem("s_rc")
        s_ld = [sem("s_ld0"), sem("s_ld1")]
        s_hi, s_lo = sem("s_hi"), sem("s_lo")
        s_gz = sem("s_gz")
        s_tile = sem("s_tile")
        s_evac = sem("s_evac")
        s_x0, s_x0a = sem("s_x0"), sem("s_x0a")
        s_xs = sem("s_xs")
        s_sqa, s_sqd = sem("s_sqa"), sem("s_sqd")
        s_gain, s_rcon = sem("s_gain"), sem("s_rcon")
        s_xT = sem("s_xT")
        s_xh, s_xl = sem("s_xh"), sem("s_xl")
        s_r0 = sem("s_r0")
        s_sum, s_ss, s_rms = sem("s_sum"), sem("s_ss"), sem("s_rms")
        s_hh, s_hidh, s_hid = sem("s_hh"), sem("s_hidh"), sem("s_hid")
        s_dve, s_act, s_pool = sem("s_dve"), sem("s_act"), sem("s_pool")
        s_rot = sem("s_rot")
        s_tab = sem("s_tab")
        s_gf, s_g1, s_g2, s_g3, s_g4 = sem("s_gf"), sem("s_g1"), sem("s_g2"), sem("s_g3"), sem("s_g4")
        s_moz, s_moe = sem("s_moz"), sem("s_moe")
        s_cl = sem("s_cl")
        s_set, s_seta, s_setd = sem("s_set"), sem("s_seta"), sem("s_setd")
        s_gt, s_gtd = sem("s_gt"), sem("s_gtd")
        s_sc, s_neg, s_sn, s_p, s_pn = sem("s_sc"), sem("s_neg"), sem("s_sn"), sem("s_p"), sem("s_pn")
        s_T, s_pt1, s_pt2, s_pv = sem("s_T"), sem("s_pt1"), sem("s_pt2"), sem("s_pv")
        s_aoh, s_ao = sem("s_aoh"), sem("s_ao")
        s_dn = sem("s_dn")
        s_tv, s_vev, s_tk, s_kev, s_wv = sem("s_tv"), sem("s_vev"), sem("s_tk"), sem("s_kev"), sem("s_wv")
        s_e, s_ex, s_swp, s_sw, s_nd = sem("s_e"), sem("s_ex"), sem("s_swp"), sem("s_sw"), sem("s_nd")
        s_dsq, s_hsq, s_em, s_mx = sem("s_dsq"), sem("s_hsq"), sem("s_em"), sem("s_mx")
        s_nu, s_nn, s_u, s_st = sem("s_nu"), sem("s_nn"), sem("s_u"), sem("s_st")
        s_ssm, s_s2, s_rs, s_hm, s_hmh, s_hmd = (sem("s_ssm"), sem("s_s2"), sem("s_rs"), sem("s_hm"), sem("s_hmh"),
                                                 sem("s_hmd"))
        s_ct, s_co = sem("s_ct"), sem("s_co")
        s_xg, s_yt, s_yed, s_yea = sem("s_xg"), sem("s_yt"), sem("s_yed"), sem("s_yea")
        s_kvo, s_mo, s_cno, s_yo = sem("s_kvo"), sem("s_mo"), sem("s_cno"), sem("s_yo")

        def tile_of(s):
            return s if s < S_WOA else (S_WOA + 2 * (s - S_WOA) if s < S_MLP else s + 8)

        def end_tile(g):
            return TILES * (g // SLOTS) + tile_of(g % SLOTS + 1)

        landed, got = {}, [0, 0]
        for n in range(PAIRS * DEPTH):
            got[n % 2] += 16 * {2: 4, 3: 4, 12: 2, 13: 2}.get(n % PAIRS, 1)
            landed[n] = got[n % 2]

        fills = {}

        def plan_fills(kind, first, end, counts, at_last):
            u = first
            for c in range(NC):
                for i, n in enumerate(at_last if c == SAMPLE else counts):
                    fills[kind, c, i] = (u, min(u + n, end))
                    u = min(u + n, end)
            fills[kind, NC, 0] = (u, end)

        fills["s", 0, 0] = (8 * S_MK, 8 * S_MK + S_FILL)
        plan_fills("a", 8 * S_MK + S_FILL, 8 * S_WOA, A_FILL, A_FILL)
        fills["p", 0, 0] = (8 * S_WOA, 8 * S_WOA + P_FILL[0])
        fills["p", 0, 1] = (8 * S_WOA + P_FILL[0], 8 * S_WOA + sum(P_FILL))
        plan_fills("m", 8 * S_WOA + sum(P_FILL), 8 * S_WOM, M_FILL, M_LAST)

        def slots_done(kind, c, i):
            a, b = fills[kind, c, i]
            return range(-(-(a + 1) // 8) - 1, b // 8) if b > a else range(0)

        def tiles_done(kind, c, i):
            return [(u // 8, u % 8 // 4, u % 8 == 7) for u in range(*fills[kind, c, i])
                    if u % 8 == 7 or (u >= 8 * S_WOA and u % 8 == 3)]

        def gate_pieces(c, i):
            done = []
            for cc in range(NC):
                for ii in range(3):
                    ready = 4 * (min(max(fills["a", cc, ii][1] // 8, S_MO), S_MV) - S_MO)
                    now = range(len(done), min(ready, len(done) + 1))
                    done += now
                    if (cc, ii) == (c, i):
                        return [(n // 4, n % 4) for n in now]
            rest = range(len(done), 4 * MH)
            return [(n // 4, n % 4) for n in (rest[2:] if i else rest[:2])]

        def x_ready(n, k):
            if n == 0:
                return (s_x0a if k % 2 else s_x0), k // 2 + 1
            l, second = (n - 1) // 2, n % 2
            return s_evac, TILES * l + (S_WOA + 8 if second else TILES - 8) + k + 1

        def keys(c):
            return WIN + L if c >= 2 else (c + 1) * L

        def n_pt1(l, c):
            return (NC - 1) * l + max(c - 1, 0)

        def n_pt2(l, c):
            return (NC - 1) * l + (c if c < 2 else c - 1)

        block = ctx.enter_context(nc.Block())

        @block.sync
        def _(sp):
            sp.dma_start(io[:], const[:, C_ID:C_ID + 2 * P]).then_inc(s_const, 16)
            zf = z[:, :, :].rearrange("p a t -> p (a t)")
            sp.dma_start(zf[0:DEC, 4 * DM:5 * DM], x_sample[0]).then_inc(s_xin[4], 16)
            for t in range(SEQ // P):
                sp.dma_start(zf[:, t * DM:(t + 1) * DM], x_prompt[0, t * P:(t + 1) * P, :]).then_inc(s_xin[t], 16)
            for l in range(DEPTH):
                for p in range(S_MLP // 2 + 1):
                    n = PAIRS * l + p
                    if n >= 2:
                        sp.wait_ge(s_lo, SLOTS * ((n - 2) // PAIRS) + 2 * ((n - 2) % PAIRS) + 1)
                    dst = stage[:, n % 2, :]
                    if p == 0:
                        sp.dma_start(dst[:, 0:8 * KT].rearrange("p (k c) -> p k c", k=KT),
                                     w_in[l, :, COL_GATE:].rearrange("(k p) c -> p k c", p=P)).then_inc(s_ld[n % 2], 16)
                    elif p in (2, 3):
                        d5 = dst.rearrange("p (k q g c) -> p k q g c", k=KT, q=2, g=AG)
                        for q in range(2):
                            for g in range(AG):
                                col = g * AJ * AD + (2 * (p - 2) + q) * AD
                                sp.dma_start(d5[:, :, q, g, :], w_in[l, :, col:col + AD].rearrange(
                                    "(k p) c -> p k c", p=P)).then_inc(s_ld[n % 2], 16)
                    elif p < 12:
                        col = COL_K if p == 1 else (COL_MK, COL_MQ, COL_MO, COL_MV)[(p - 4) // 2] + (p % 2) * 2 * P
                        sp.dma_start(dst.rearrange("p (k c) -> p k c", k=KT),
                                     w_in[l, :, col:col + 2 * P].rearrange("(k p) c -> p k c", p=P)).then_inc(s_ld[n % 2], 16)
                        if n == 1:
                            sp.dma_start(rstage[:], const[:, C_R:C_R + R_COLS]).then_inc(s_rc, 16)
                    else:
                        cols = slice((p % 2) * 4 * P, (p % 2 + 1) * 4 * P)
                        d3 = dst.rearrange("p (k c) -> p k c", k=AJ)
                        if p < 14:
                            for g in range(AG):
                                sp.dma_start(d3[g * AD:(g + 1) * AD], w_out[l, g * AJ * AD:(g + 1) * AJ * AD, cols].rearrange(
                                    "(j p) c -> p j c", p=AD)).then_inc(s_ld[n % 2], 16)
                        else:
                            sp.dma_start(d3, w_out[l, AQ:, cols].rearrange("(k p) c -> p k c", p=P)).then_inc(s_ld[n % 2], 16)
                free0 = SLOTS * l + S_MLP - 2
                with sp.Fori(0, GROUPS) as g:
                    with sp.Fori(0, 2) as i:
                        for q in range(2):
                            sp.wait_ge(s_lo, free0 + 16 * g + 4 * i + 2 * q)
                            sp.dma_start(stage[:, q, :].rearrange("p (k c) -> p k c", k=KT),
                                         w_up[l, :, bass.ds(g * DM + i * 4 * P + q * 2 * P, 2 * P)].rearrange(
                                             "(k p) c -> p k c", p=P)).then_inc(s_ld[q], 16)
                    with sp.Fori(0, 2) as i:
                        for q in range(2):
                            sp.wait_ge(s_lo, free0 + 8 + 16 * g + 4 * i + 2 * q)
                            sp.dma_start(stage[:, q, :].rearrange("p (k c) -> p k c", k=KT),
                                         w_down[l, bass.ds(g * DM, DM), bass.ds(i * 4 * P + q * 2 * P, 2 * P)].rearrange(
                                             "(k p) c -> p k c", p=P)).then_inc(s_ld[q], 16)
            for t in range(5):
                sp.wait_ge(s_yed, t + 1)
                sp.wait_ge(s_yea, t + 1)
                n = P if t < 4 else DEC
                sp.dma_start(y_prompt[0, t * P:(t + 1) * P, :] if t < 4 else y_sample[0],
                             zf[0:n, t * DM:(t + 1) * DM]).then_inc(s_yo, 16)
            sp.wait_ge(s_yo, 5 * 16)

        @block.gpsimd
        def _(pool):
            chain = [0]

            def link(ins):
                chain[0] += 1
                ins.then_inc(s_pool, 1)
                pool.wait_ge(s_pool, chain[0])

            def squares(n):
                if n:
                    pool.wait_ge(s_ss, n)
                tiles = KT if n else 3
                for k in range(tiles):
                    pool.wait_ge(*x_ready(n, k))
                    if k == 0:
                        link(nc.gpsimd.tensor_tensor(ssum[:], x[:, k, :], x[:, k, :], ALU.mult))
                    else:
                        link(nc.gpsimd.tensor_tensor(sqr[:], x[:, k, :], x[:, k, :], ALU.mult))
                        last = nc.gpsimd.tensor_tensor(ssum[:], ssum[:], sqr[:], ALU.add)
                        if k < tiles - 1:
                            link(last)
                last.then_inc(s_sum, 1)

            squares(0)
            for l in range(DEPTH):
                for c in range(NC):
                    if c % 2 == 0:
                        p = c // 2
                        pool.wait_ge(s_vev, NP * l + p + 1)
                        r = L if p == NP - 1 else P
                        w = gT[0:r, 0, p * MH:(p + 1) * MH].rearrange("p (h o) -> p h o", o=1)
                        nc.gpsimd.tensor_copy(wsv[0:r, :, MD:MD + 1], w)
                        nc.gpsimd.tensor_tensor(wsv[0:r, :, 0:MD], vtok[0:r], w.to_broadcast([r, MH, MD]), ALU.mult).then_inc(s_wv, 1)
                    if c:
                        q = slice((c % 2) * L, (c % 2 + 1) * L)
                        pool.wait_ge(s_sw, NC * l + c + 1)
                        nc.gpsimd.tensor_tensor(nq[q], nq[q], sw[q], ALU.add).then_inc(s_dn, 1)
                squares(2 * l + 1)
                squares(2 * l + 2)

        @block.scalar
        def _(act):
            chain = [0]

            def link(ins):
                chain[0] += 1
                ins.then_inc(s_act, 1)
                act.wait_ge(s_act, chain[0])

            A = nc.scalar.activation
            zf = z[:, :, :].rearrange("p a t -> p (a t)")

            def split(g):
                if g >= SLOTS * DEPTH:
                    return
                l, s = g // SLOTS, g % SLOTS
                n = PAIRS * l + (s + 1) // 2
                act.wait_ge(s_ld[n % 2], landed[n])
                if g >= 2:
                    act.wait_ge(s_tile, end_tile(g - 2))
                if s == 0:
                    act.wait_ge(s_gz, 2)
                    A(w_hi[:, g % 2, :].rearrange("p (k a b) -> p k a b", k=KT, b=32)[:, :, 0:2, 0:MH],
                      stage[:, n % 2, 0:8 * KT].rearrange("p (k a c) -> p k a c", k=KT, a=2), ACT.Copy).then_inc(s_hi, 1)
                    return
                k = KT if s < S_WOA or s >= S_MLP else 4
                A(w_hi[:, g % 2, :].rearrange("p (k c) -> p k c", k=k),
                  stage[:, n % 2, :].rearrange("p (k q c) -> p k q c", k=k, q=2)[:, :, (s + 1) % 2, :],
                  ACT.Copy).then_inc(s_hi, 1)

            def norm_tile(n, k):
                act.wait_ge(*x_ready(n, k))
                A(xh[:, k, :], x[:, k, :], ACT.Copy, scale=gain(n, k)).then_inc(s_xh, 1)

            def rms_of(n):
                act.wait_ge(s_ss, n + 1)
                link(A(two(rms[:]), psum[:, 4:6, 0:HALF], ACT.Ln, bias=eps_col, scale=1.0 / DM))
                link(A(rms[:], rms[:], ACT.Exp, scale=-0.5))
                A(tmp[1][:], rms[:], ACT.Square, scale=0.5 ** 0.5)
                A(two(tmp[0][:]), psum[:, 4:6, 0:HALF], ACT.Identity, bias=eps_col, scale=1.0 / DM).then_inc(s_r0, 1)

            nc.scalar.preload_act_table_set("natural_log_exp_and_others")

            graw = zf[0:56, 5 * DM:5 * DM + P]
            act.dma_start(graw[0:16], norm_rows(norm1_g)).then_inc(s_par, 16)
            act.dma_start(graw[16:32], norm_rows(norm2_g)).then_inc(s_par, 16)
            act.dma_start(graw[32:40], final_g.rearrange("(k p) -> k p", p=P)).then_inc(s_par, 16)
            act.dma_start(graw[40:48], norm_rows(mnorm_g)).then_inc(s_par, 16)
            act.dma_start(graw[48:56], state_n.rearrange("l b h k -> (l b h) k")).then_inc(s_par, 16)
            with nc.allow_non_contiguous_dma(reason="a few bytes"):
                for g in range(AG):
                    act.dma_start(small[g * AD:(g + 1) * AD, 8:8 + DEPTH * AJ].rearrange("p (l j) -> p l j", l=DEPTH),
                                  attn_sink[:, g * AJ:(g + 1) * AJ].rearrange("(o l) j -> o l j", o=1).to_broadcast(
                                      [AD, DEPTH, AJ])).then_inc(s_sml, 16)
                act.dma_start(small[0:MH, 24:24 + DEPTH], gate_b[:, 0:MH].rearrange("l h -> h l")).then_inc(s_sml, 16)
                act.dma_start(small[32:32 + MH, 24:24 + DEPTH], gate_b[:, MH:].rearrange("l h -> h l")).then_inc(s_sml, 16)
                act.dma_start(small[0:MH, 26:26 + DEPTH], state_m.rearrange("l b h -> (b h) l")).then_inc(s_sml, 16)
            act.wait_ge(s_gain, 2)
            act.wait_ge(s_xs, 1)

            def copy_x(k):
                act.wait_ge(s_xT, 3 + k)
                A(x[:, k, 0:SEQ], psum[:, k, :], ACT.Copy).then_inc(s_x0a, 1)
                act.wait_ge(s_x0a, k // 2 + 1)

            for k in range(KT):
                if k % 2 == 0:
                    copy_x(k + 1)
                norm_tile(0, k)
                if k == 1:
                    split(0)
            split(1)
            act.wait_ge(s_xT, KT + 2)
            for k in range(3, KT):
                A(z[:, 2 + k - 3, :], x[:, k, :], ACT.Square).then_inc(s_sqa, 1)
            act.wait_ge(s_rc, 16)
            A(rconst[:], rstage[:], ACT.Copy).then_inc(s_rcon, 1)

            for l in range(DEPTH):
                g0 = SLOTS * l

                def load_side():
                    if l == 0:
                        act.wait_ge(s_xT, KT + 2)
                    act.dma_start(z[:, 0:2, :].rearrange("p a t -> p (a t)"), const[:, C_COS:C_COS + 2 * T]).then_inc(s_tab, 16)
                    if l:
                        act.wait_ge(s_cno, 16 * 4 * l)
                    act.dma_start(kraw[:], cache_k[l, 0].rearrange("t g d -> t (g d)")).then_inc(s_cl, 16)
                    act.dma_start(vcache[:], cache_v[l, 0].rearrange("t g d -> t (g d)")).then_inc(s_cl, 16)
                    act.dma_start(pT1[:].rearrange("p (h k) -> p h k", h=MH), state_C[l, 0].rearrange("h v k -> v h k")).then_inc(s_cl, 16)

                load_side()
                split(g0 + 2)
                rms_of(2 * l)
                split(g0 + 3)
                split(g0 + 4)
                act.wait_ge(s_sml, 16 * 5)
                act.wait_ge(s_gf, l + 1)
                link(A(row(2, 1), row(1, 1), ACT.Abs, bias=bf_c[l]))
                link(A(row(2, 1), row(2, 1), ACT.Exp, scale=-1.0))
                nc.scalar.preload_act_table_set("natural_log")
                A(row(3, 1), row(2, 1), ACT.Ln, bias=1.0).then_inc(s_g1, 1)
                nc.scalar.preload_act_table_set("natural_log_exp_and_others")
                split(g0 + 5)
                split(g0 + 6)
                split(g0 + 7)
                split(g0 + 8)
                act.wait_ge(s_set, l + 1)
                A(vwin[:, 0:4, :], psum[:, 4, :].rearrange("p (n c) -> p n c", n=4), ACT.Copy)
                A(vwin[:, 4:8, :], psum[:, 6, :].rearrange("p (n c) -> p n c", n=4), ACT.Copy).then_inc(s_seta, 1)
                act.wait_ge(s_setd, l + 1)
                act.wait_ge(s_seta, l + 1)
                act.dma_start(p_k[l, 0].rearrange("t g d -> t (g d)"), kout[:, 0, :]).then_inc(s_kvo, 16)
                act.dma_start(s_k[l, 0].rearrange("t g d -> t (g d)"), kout[0:DEC, 1, :]).then_inc(s_kvo, 16)
                act.dma_start(p_v[l, 0].rearrange("t g d -> t (g d)"), vwin[:, SAMPLE - 2, :]).then_inc(s_kvo, 16)
                act.dma_start(s_v[l, 0].rearrange("t g d -> t (g d)"), vwin[0:DEC, SAMPLE, :]).then_inc(s_kvo, 16)

                def fill(kind, c, i):
                    for s in slots_done(kind, c, i):
                        split(g0 + s + 2)
                        if S_MO <= s < S_MV:
                            act.wait_ge(s_evac, TILES * l + s + 1)
                            A(z[:, 12 + s - S_MO, :], z[:, 12 + s - S_MO, :], ACT.Exp, scale=-1.0).then_inc(s_moe, 1)

                fill("s", 0, 0)
                for c in range(NC):
                    a, nk = NC * l + c, keys(c)
                    act.wait_ge(s_neg, a + 1)
                    if c or l:
                        act.wait_ge(s_T, a)
                    for j in range(AJ):
                        A(prob[:, j, 0:nk], psum[:, 4 + j // 2, (j % 2) * (WIN + L):(j % 2) * (WIN + L) + nk], ACT.Exp,
                          bias=att_s[:, 4 + j:5 + j], scale=A_SCALE, accum_out=att_s[:, 8 + j:9 + j])
                    act.wait_ge(s_sn, a + 1)
                    A(att_s[:, 16:16 + AJ], att_s[:, 12:12 + AJ], ACT.Exp).then_inc(s_p, 1)
                    if c == 2:
                        act.wait_ge(s_g2, l + 1)
                        A(row(7), row(7), ACT.Exp)
                        A(row(1, 2), row(1, 2), ACT.Exp, scale=-2.0)
                        A(row(5), row(5), ACT.Exp)
                        A(g9[0:MH, 32:32 + NC], g9[0:MH, 32:32 + NC], ACT.Exp).then_inc(s_g3, 1)
                    if c == 3:
                        act.wait_ge(s_g4, l + 1)
                        with nc.allow_non_contiguous_dma(reason="four values"):
                            act.dma_start(p_m[l].rearrange("b h -> h b"), g9[0:MH, NC - 2:NC - 1]).then_inc(s_kvo, 16)
                            act.dma_start(s_m[l].rearrange("b h -> h b"), g9[0:MH, NC - 1:NC]).then_inc(s_kvo, 16)
                    fill("a", c, 0)
                    act.wait_ge(s_T, a + 1)
                    if nk > L:
                        A(pT1[:], psum[:, 6, :], ACT.Copy).then_inc(s_pt1, 1)
                    fill("a", c, 1)
                    act.wait_ge(s_pv, a + 1)
                    o4 = psum[:, 6, :].rearrange("p (j g q) -> p j g q", j=AJ, g=AG)
                    A(hid_h[0:AD, 0:AJ, c * L:(c + 1) * L], o4[0:AD, :, 0, :], ACT.Copy)
                    A(hid_h[AD:P, 0:AJ, c * L:(c + 1) * L], o4[AD:P, :, 1, :], ACT.Copy).then_inc(s_aoh, 1)
                    fill("a", c, 2)

                ch = lambda b, half: psum[:, b, half * MH * L:(half + 1) * MH * L].rearrange("p (h t) -> p h t", h=MH)
                m2, r2 = (tmp[0][:, i * MH * L:(i + 1) * MH * L].rearrange("p (h t) -> p h t", h=MH) for i in range(2))

                def scores_exp(c):
                    q = slice((c % 2) * L, (c % 2 + 1) * L)
                    act.wait_ge(s_e, NC * l + c + 1)
                    A(eexp[q], ch(5, 0)[q], ACT.Exp).then_inc(s_ex, 1)

                def token_major(p, dst, arrived, done):
                    r = L if p == NP - 1 else P
                    act.wait_ge(arrived, NP * l + p + 1)
                    A(dst[0:r], psum[0:r, 7, :].rearrange("p (h d) -> p h d", h=MH), ACT.Copy).then_inc(done, 1)

                def finish(c):
                    act.wait_ge(s_hm, NC * l + c + 1)
                    A(hid_h[:, MH:2 * MH, c * L:(c + 1) * L],
                      tmp[2][:, 0:MH * L].rearrange("p (h t) -> p h t", h=MH), ACT.Copy).then_inc(s_hmh, 1)

                act.wait_ge(s_kvo, 16 * 6 * (l + 1))
                scores_exp(0)
                token_major(0, ktok, s_tk, s_kev)
                fill("a", NC, 0)
                fill("p", 0, 0)
                token_major(0, vtok, s_tv, s_vev)
                fill("p", 0, 1)
                for c in range(NC):
                    a = NC * l + c
                    act.wait_ge(s_nd, a + 1)
                    A(z[:, 4:8, c * L:(c + 1) * L], ch(6, 0), ACT.Copy)
                    A(dsq[:], ch(6, 1), ACT.Square, scale=EPS ** 0.5).then_inc(s_dsq, 1)
                    A(hsq[:], ch(6, 0), ACT.Square).then_inc(s_hsq, 1)
                    if c:
                        finish(c - 1)
                    fill("m", c, 0)
                    if c < SAMPLE:
                        scores_exp(c + 1)
                        if c % 2:
                            token_major((c + 1) // 2, vtok, s_tv, s_vev)
                    act.wait_ge(s_s2, a + 1)
                    link(A(rstd[:], m2, ACT.Ln))
                    link(A(rstd[:], rstd[:], ACT.Exp, scale=-0.5))
                    A(r2, rstd[:], ACT.Square, scale=0.5 ** 0.5).then_inc(s_rs, 1)
                    fill("m", c, 1)
                    if c < SAMPLE and c % 2:
                        token_major((c + 1) // 2, ktok, s_tk, s_kev)
                finish(NC - 1)
                fill("m", NC, 0)
                act.wait_ge(s_co, 2 * (l + 1))
                for w, (co, no) in enumerate(((p_C, p_n), (s_C, s_n))):
                    act.dma_start(co[l, 0].rearrange("h v k -> v h k"),
                                  cout[:, w, :].rearrange("p (h k) -> p h k", h=MH)).then_inc(s_cno, 16)
                    act.dma_start(no[l, 0], kout[0:MH, w, :]).then_inc(s_cno, 16)
                for s in range(S_WOM, S_MLP):
                    split(g0 + s + 2)
                    for k in range(2):
                        norm_tile(2 * l + 1, 2 * (s - S_WOM) + k)
                rms_of(2 * l + 1)

                tile_m = TILES * l + S_MLP + 8
                def mlp_split(j, q, m):
                    r = ((q + 2) % 4) // 2
                    act.wait_ge(s_ld[r], landed[PAIRS * l + 16 + r] + 16 * m)
                    act.wait_ge(s_tile, tile_m + j + 1)
                    A(w_hi[:, (g0 + S_MLP + q) % 2, :].rearrange("p (k c) -> p k c", k=KT),
                      stage[:, r, :].rearrange("p (k q c) -> p k q c", k=KT, q=2)[:, :, q % 2, :],
                      ACT.Copy).then_inc(s_hi, 1)

                def up_step(g, i, q):
                    mlp_split(16 * g + 4 * i + q, q, 4 * g + i + (q + 2) // 4)
                    act.wait_ge(s_hh, 8 * GROUPS * l + 8 * g + 4 * i + q + 1)
                    A(hid_h[:, bass.ds(4 * i + q, 1), :], tmp[1][:].rearrange("p (o t) -> p o t", o=1), ACT.Copy).then_inc(s_hidh, 1)

                with act.Fori(0, GROUPS - 1) as g:
                    with act.Fori(0, 2) as i:
                        for q in range(4):
                            up_step(g, i, q)
                    with act.Fori(0, 2) as i:
                        for q in range(4):
                            mlp_split(16 * g + 8 + 4 * i + q, q, 4 * g + 2 + i + (q + 2) // 4)
                with act.Fori(0, 2) as i:
                    for q in range(4):
                        up_step(GROUPS - 1, i, q)
                for k in range(KT):
                    split(g0 + SLOTS - KT + k + 2)
                    if l < DEPTH - 1:
                        norm_tile(2 * l + 2, k)
                    else:
                        act.wait_ge(*x_ready(2 * DEPTH, k))
                        A(xg[:, k, :], x[:, k, :], ACT.Copy, scale=gain(2 * DEPTH, k)).then_inc(s_xg, 1)
            act.wait_ge(s_ss, 2 * DEPTH + 1)
            sums = psum[:, 3, 0:5]
            link(A(att_s[:, 0:5], sums, ACT.Ln, bias=eps_col, scale=1.0 / DM))
            link(A(att_s[:, 0:5], att_s[:, 0:5], ACT.Exp, scale=-0.5))
            A(att_s[:, 5:10], att_s[:, 0:5], ACT.Square, scale=0.5 ** 0.5)
            A(att_s[:, 10:15], sums, ACT.Identity, bias=eps_col, scale=1.0 / DM).then_inc(s_r0, 1)
            act.wait_ge(s_rms, 2 * DEPTH + 1)
            for t in range(5):
                m = P if t < 4 else DEC
                act.wait_ge(s_yt, (5, 6, 7, 8, 10)[t])
                A(zf[0:m, t * DM + 512:(t + 1) * DM], psum[0:m, t % 4, :], ACT.Copy, scale=att_s[0:m, t:t + 1]).then_inc(s_yea, 1)
            act.wait_ge(s_cno, 16 * 4 * DEPTH)
            act.wait_ge(s_kvo, 16 * 6 * DEPTH)

        @block.vector
        def _(dve):
            chain = [0]

            def link(ins):
                chain[0] += 1
                ins.then_inc(s_dve, 1)
                dve.wait_ge(s_dve, chain[0])

            V = nc.vector
            f = lambda ap: ap.bitcast(F32)

            def split(g):
                if g >= SLOTS * DEPTH:
                    return
                l, s = g // SLOTS, g % SLOTS
                n = PAIRS * l + (s + 1) // 2
                dve.wait_ge(s_hi, g + 1)
                if s == 0:
                    pick = lambda w: w[:, g % 2, :].rearrange("p (k a b) -> p k a b", k=KT, b=32)[:, :, 0:2, 0:MH]
                    src = stage[:, n % 2, 0:8 * KT].rearrange("p (k a c) -> p k a c", k=KT, a=2)
                else:
                    k = KT if s < S_WOA or s >= S_MLP else 4
                    pick = lambda w: w[:, g % 2, :].rearrange("p (k c) -> p k c", k=k)
                    src = stage[:, n % 2, :].rearrange("p (k q c) -> p k q c", k=k, q=2)[:, :, (s + 1) % 2, :]
                V.tensor_tensor(pick(w_lo), src, f(pick(w_hi)), ALU.subtract).then_inc(s_lo, 1)

            def norm_tile(n, k):
                dve.wait_ge(s_xh, KT * n + k + 1)
                V.scalar_tensor_tensor(xl[:, k, :], x[:, k, :], gain(n, k), f(xh[:, k, :]),
                                       ALU.mult, ALU.subtract).then_inc(s_xl, 1)

            def rms_of(n):
                dve.wait_ge(s_r0, n + 1)
                link(V.scalar_tensor_tensor(tmp[1][:], tmp[1][:], -1.0, tmp[0][:], ALU.mult, ALU.mult))
                V.scalar_tensor_tensor(rms[:], tmp[1][:], 1.5, rms[:], ALU.add, ALU.mult).then_inc(s_rms, 1)
                dve.wait_ge(s_rms, n + 1)

            V.memset(eps_col, EPS).then_inc(s_gain, 1)
            V.memset(f(w_hi[:, 0, :]), 0.0).then_inc(s_gz, 1)
            V.memset(f(w_lo[:, 0, :]), 0.0).then_inc(s_gz, 1)
            for b in (bcr, ncr, acl):
                link(V.memset(f(b[:]), 0.0))
            dve.wait_ge(s_xT, 1)
            V.tensor_copy(x[:, :, SEQ:T], psum[:, 7, :].rearrange("p (k t) -> p k t", k=KT)).then_inc(s_xs, 1)
            dve.wait_ge(s_xT, 2)
            V.tensor_copy(gains[:], psum[:, 7, 0:56]).then_inc(s_gain, 1)
            dve.wait_ge(s_xs, 1)
            for k in range(0, KT, 2):
                dve.wait_ge(s_xT, 3 + k)
                V.tensor_copy(x[:, k, 0:SEQ], psum[:, k, :]).then_inc(s_x0, 1)
            for k in range(2):
                norm_tile(0, k)
            dve.wait_ge(s_gz, 2)
            split(0)
            for k in range(2, KT):
                norm_tile(0, k)
            split(1)
            for k in range(4, KT):
                dve.wait_ge(s_sqa, k - 2)
                ins = V.tensor_tensor(z[:, 2, :], z[:, 2, :], z[:, 2 + k - 3, :], ALU.add)
                if k < KT - 1:
                    link(ins)
            ins.then_inc(s_sqd, 1)
            dve.wait_ge(s_sml, 5 * 16)
            link(V.tensor_scalar(small[:, 16:24], small[:, 8:16], -1.0, None, ALU.mult))

            rotated = [0]

            def rotary(l, s, writes):
                t = TILES * l + tile_of(s)
                src = acc[t % 2]
                dve.wait_ge(s_tile, t + 1)
                if rotated[0]:
                    dve.wait_ge(s_rot, rotated[0])
                rotated[0] += 1
                mask = list(range(32))
                for i in range(ROPE_DIM // 2):
                    mask[i], mask[i + ROPE_DIM // 2] = i + ROPE_DIM // 2, i
                link(V.stream_shuffle(two(tmp[0][:]), src, mask))
                V.tensor_tensor(two(tmp[1][:]), src, two(z[:, 0, :]), ALU.mult).then_inc(s_evac, 1)
                link(V.tensor_tensor(tmp[0][:], tmp[0][:], z[:, 1, :], ALU.mult))
                dve.wait_ge(s_evac, t + 1)
                for n, (out, sl) in enumerate(writes):
                    t0, t1 = tmp[0][sl, :], tmp[1][sl, :]
                    if len(out.shape) == 3:
                        t0, t1 = (v.rearrange("p (c q) -> p c q", c=NC) for v in (t0, t1))
                    ins = V.tensor_tensor(out, t0, t1, ALU.add)
                ins.then_inc(s_rot, 1)

            for l in range(DEPTH):
                g0, t0 = SLOTS * l, TILES * l

                def plain(s, out, scale=None):
                    t = t0 + tile_of(s)
                    dve.wait_ge(s_tile, t + 1)
                    if scale is None:
                        return V.tensor_tensor(two(out), acc[t % 2], two(rms[:]), ALU.mult).then_inc(s_evac, 1)
                    return V.scalar_tensor_tensor(two(out), acc[t % 2], scale, two(rms[:]), ALU.mult, ALU.mult).then_inc(s_evac, 1)

                def add_x(t, m):
                    dve.wait_ge(s_tile, t + 1)
                    V.tensor_tensor(two(x[:, m, :]), two(x[:, m, :]), acc[t % 2], ALU.add).then_inc(s_evac, 1)

                for b in qbd:
                    V.memset(b[0:AD, :, :, 1, :].rearrange("p j c q -> p (j c) q"), 0.0)
                    link(V.memset(b[AD:P, :, :, 0, :].rearrange("p j c q -> p (j c) q"), 0.0))
                split(g0 + 2)
                rms_of(2 * l)
                dve.wait_ge(s_tile, t0 + 1)
                a0 = acc[t0 % 2]
                V.tensor_tensor(two(row(0)), a0[0:MH], two(rms[0:MH, :]), ALU.mult)
                V.tensor_tensor(two(row(1, 1)), a0[32:32 + MH], two(rms[32:32 + MH, :]), ALU.mult).then_inc(s_evac, 1)
                dve.wait_ge(s_tab, 16 * (l + 1))
                V.tensor_tensor(z[:, 0, :], z[:, 0, :], rms[:], ALU.mult)
                link(V.tensor_tensor(z[:, 1, :], z[:, 1, :], rms[:], ALU.mult))
                rotary(l, S_AK, [(kT[:], slice(0, P))])
                split(g0 + 3)
                link(V.tensor_scalar(row(4, 1), row(1, 1), bf_c[l], 0.0, ALU.add, ALU.min))
                V.tensor_scalar(row(0), row(0), bi_c[l], None, ALU.add)
                V.memset(row(5), 1.0).then_inc(s_gf, 1)
                plain(S_AV, vT[:])
                split(g0 + 4)
                rotary(l, S_AQ, [(qbd[0][0:AD, 0, :, 0, :], slice(0, AD)), (qbd[0][AD:P, 0, :, 1, :], slice(AD, P))])
                split(g0 + 5)
                rotary(l, S_AQ + 1, [(qbd[0][0:AD, 1, :, 0, :], slice(0, AD)), (qbd[0][AD:P, 1, :, 1, :], slice(AD, P))])
                split(g0 + 6)
                for j in range(2, AJ):
                    rotary(l, S_AQ + j, [(qbd[1][0:AD, j - 2, :, 0, :], slice(0, AD)), (qbd[1][AD:P, j - 2, :, 1, :], slice(AD, P))])
                    split(g0 + S_AQ + j + 2)
                last_of = lambda r, c0, c1: r.rearrange("p (c t) -> p c t", c=NC)[:, c0:c1, L - 1:L]
                first_of = lambda r, c0, c1: r.rearrange("p (c t) -> p c t", c=NC)[:, c0:c1, 0:1]
                col = lambda i: g9[0:MH, 16 * i:16 * i + NC].rearrange("p (c o) -> p c o", o=1)

                def gates_sums():
                    dve.wait_ge(s_gf, l + 1)
                    link(V.memset(row(5).rearrange("p (c t) -> p c t", c=NC)[:, :, 0:1], 0.0))
                    dve.wait_ge(s_g1, l + 1)
                    link(V.tensor_tensor(row(1), row(4, 1), row(3, 1), ALU.subtract))
                    link(V.tensor_tensor_scan(row(2), row(5), row(1), 0.0, ALU.mult, ALU.add))
                    link(V.tensor_tensor(row(3), row(0), row(2), ALU.subtract))

                def gates_maxima():
                    link(V.memset(row(4), 0.0))
                    link(V.tensor_copy(first_of(row(4), 1, SAMPLE), last_of(row(2), 0, SAMPLE - 1)))
                    link(V.tensor_tensor_scan(row(6)[:, 0:SEQ], row(4)[:, 0:SEQ], row(3)[:, 0:SEQ], 0.0, ALU.add, ALU.max))
                    link(V.tensor_tensor_scan(row(6)[:, SEQ:T], row(4)[:, SEQ:T], row(3)[:, SEQ:T], ms_c[l], ALU.add, ALU.max))

                def gates_exponents():
                    if l:
                        dve.wait_ge(s_kvo, 16 * 6 * l)
                    link(V.tensor_tensor(col(0), last_of(row(6), 0, NC), last_of(row(2), 0, NC), ALU.add))
                    V.memset(g9[0:MH, 16:17], 0.0)
                    V.tensor_copy(g9[0:MH, 17:17 + SAMPLE - 1], g9[0:MH, 0:SAMPLE - 1])
                    link(V.tensor_copy(g9[0:MH, 16 + SAMPLE:17 + SAMPLE], ms_c[l]))
                    chunks = lambda r: r.rearrange("p (c t) -> p c t", c=NC)
                    V.tensor_tensor(chunks(row(7)), col(1).to_broadcast([MH, NC, L]), chunks(row(6)), ALU.subtract)
                    V.tensor_tensor(row(1, 2), row(2), row(6), ALU.add)
                    V.tensor_tensor(chunks(row(5)), chunks(row(3)), last_of(row(6), 0, NC).to_broadcast([MH, NC, L]), ALU.subtract)
                    V.tensor_tensor(col(2), col(1), last_of(row(6), 0, NC), ALU.subtract).then_inc(s_g2, 1)

                def gates_score_rows():
                    V.tensor_scalar(ncr[0:MH, :], row(6), -1.0, None, ALU.mult)
                    link(V.tensor_copy(acl[0:MH, 0:T], row(3)))
                    V.scalar_tensor_tensor(ncr[32:32 + MH, :], row(6), -1.0, f(ncr[0:MH, :]), ALU.mult, ALU.subtract)
                    V.tensor_tensor(acl[32:32 + MH, 0:T], row(3), f(acl[0:MH, 0:T]), ALU.subtract)

                def gates_bounds():
                    dve.wait_ge(s_g3, l + 1)
                    link(V.tensor_scalar(row(1, 2), row(1, 2), EPS, E_TOP, ALU.mult, ALU.min))
                    link(V.tensor_scalar(bcr[64:64 + MH, :], row(1, 2), E_LOW, None, ALU.max))
                    V.scalar_tensor_tensor(bcr[96:96 + MH, :], row(1, 2), E_LOW, f(bcr[64:64 + MH, :]), ALU.max, ALU.subtract)

                def gates_parts():
                    link(V.tensor_copy(bcr[0:MH, :], row(7)))
                    V.tensor_tensor(bcr[32:32 + MH, :], row(7), f(bcr[0:MH, :]), ALU.subtract)
                    V.tensor_tensor(g9[0:MH, 48:48 + MH * NC].rearrange("p (c h) -> p c h", c=NC), col(2).to_broadcast([MH, NC, MH]),
                                    ident[0:MH, 0:MH].rearrange("p (o h) -> p o h", o=1).to_broadcast([MH, NC, MH]),
                                    ALU.mult).then_inc(s_g4, 1)

                if l:
                    dve.wait_ge(s_cno, 16 * 4 * l)
                dve.wait_ge(s_set, l + 1)
                V.tensor_copy(cst[:, 1, :, 0:MD], psum[:, 5, :].rearrange("p (h v) -> p h v", h=MH))
                V.tensor_copy(vwin[0:L, SAMPLE, :], psum[0:L, 7, 0:P])
                V.tensor_copy(cst[:, 1, :, MD], gains[:, 48 + MH * l:52 + MH * l])
                V.tensor_copy(kout[:, 0, :], psum[:, 7, P:2 * P])
                V.tensor_copy(kout[0:DEC, 1, :], psum[0:DEC, 7, 2 * P:3 * P])
                V.tensor_copy(kcT[:], psum[:, 7, 3 * P:4 * P]).then_inc(s_setd, 1)

                def gate_of(c, i):
                    for h, n in gate_pieces(c, i):
                        zz = z[:, 12 + h, n * T // 4:(n + 1) * T // 4]
                        dve.wait_ge(s_moe, MH * l + h + 1)
                        link(V.tensor_scalar(zz, zz, 1.0, None, ALU.add))
                        link(V.reciprocal(zz, zz))
                        V.tensor_scalar(zz, zz, gains[:, 40 + MH * l + h:41 + MH * l + h], None, ALU.mult).then_inc(s_moz, 1)

                def fill(kind, c, i):
                    for s, m, whole in tiles_done(kind, c, i):
                        if s < S_WOA:
                            tile = s - S_MK + (4 if S_MO <= s < S_MV else -4 if s >= S_MV else 0)
                            plain(s, z[:, tile, :], K_SCALE if s < S_MQ else None)
                        else:
                            add_x(t0 + tile_of(s) + m, 2 * (s - S_WOA) + m)
                        if whole:
                            split(g0 + s + 2)

                fill("s", 0, 0)
                for c in range(NC):
                    a, nk = NC * l + c, keys(c)
                    dve.wait_ge(s_sc, a + 1)
                    for b in range(2):
                        ins = V.tensor_reduce(att_s[:, 2 * b:2 * b + 2],
                                              psum[:, 4 + b, 0:2 * (WIN + L)].rearrange("p (j k) -> p j k", j=2)[:, :, 0:nk],
                                              AX.X, ALU.max)
                    link(ins)
                    V.scalar_tensor_tensor(att_s[:, 4:8], att_s[:, 0:4], -A_SCALE, nsink_c[l], ALU.mult, ALU.min).then_inc(s_neg, 1)
                    dve.wait_ge(s_neg, a + 1)
                    V.tensor_tensor(att_s[:, 12:16], att_s[:, 4:8], sink_c[l], ALU.add).then_inc(s_sn, 1)
                    dve.wait_ge(s_p, a + 1)
                    link(V.tensor_tensor(att_s[:, 20:24], att_s[:, 8:12], att_s[:, 16:20], ALU.add))
                    link(V.reciprocal(att_s[:, 24:28], att_s[:, 20:24]))
                    for j in range(AJ):
                        ins = V.tensor_scalar(prob[:, j, 0:nk], prob[:, j, 0:nk], att_s[:, 24 + j:25 + j], None, ALU.mult)
                    ins.then_inc(s_pn, 1)
                    fill("a", c, 0)
                    gate_of(c, 0)
                    dve.wait_ge(s_T, a + 1)
                    if nk != WIN:
                        V.tensor_copy(pT2[:], psum[0:L, 7, :]).then_inc(s_pt2, 1)
                    fill("a", c, 1)
                    gate_of(c, 1)
                    if c < 3:
                        (gates_sums, gates_exponents, gates_bounds)[c]()
                    dve.wait_ge(s_aoh, a + 1)
                    o4 = psum[:, 6, :].rearrange("p (j g q) -> p j g q", j=AJ, g=AG)
                    cs = slice(c * L, (c + 1) * L)
                    V.tensor_tensor(hid_l[0:AD, 0:AJ, cs], o4[0:AD, :, 0, :], f(hid_h[0:AD, 0:AJ, cs]), ALU.subtract)
                    V.tensor_tensor(hid_l[AD:P, 0:AJ, cs], o4[AD:P, :, 1, :], f(hid_h[AD:P, 0:AJ, cs]), ALU.subtract).then_inc(s_ao, 1)
                    if c == 3:
                        dve.wait_ge(s_gt, l + 1)
                        V.tensor_copy(gT[:, 0, 0:(NP - 1) * MH], psum[:, 7, 0:(NP - 1) * MH])
                        V.tensor_copy(gT[0:L, 0, (NP - 1) * MH:NP * MH], psum[0:L, 7, (NP - 1) * MH:NP * MH])
                        V.tensor_copy(gT[:, 1, :], psum[:, 7, 64:64 + NC * MH]).then_inc(s_gtd, 1)
                    fill("a", c, 2)
                    gate_of(c, 2)
                    if c < 3:
                        (gates_maxima, gates_score_rows, gates_parts)[c]()

                ch = lambda b, half: psum[:, b, half * MH * L:(half + 1) * MH * L].rearrange("p (h t) -> p h t", h=MH)
                m2, r2 = (tmp[0][:, i * MH * L:(i + 1) * MH * L].rearrange("p (h t) -> p h t", h=MH) for i in range(2))
                hm = tmp[2][:, 0:MH * L].rearrange("p (h t) -> p h t", h=MH)

                def weighted(c):
                    w, q = int(c == SAMPLE), slice((c % 2) * L, (c % 2 + 1) * L)
                    dve.wait_ge(s_swp, NC * l + c + 1)
                    dve.wait_ge(s_ex, NC * l + c + 1)
                    ins = V.tensor_tensor(sw[q], ch(4, 0)[q], eexp[q], ALU.mult)
                    if c:
                        link(V.tensor_tensor(qw[:], z[:, 4:8, c * L:(c + 1) * L], ch(4, 1), ALU.mult))
                        dve.wait_ge(s_st, NC * l + c)
                        ins = V.tensor_tensor(nq[:], qw[:], cst[:, w, :, MD:MD + 1].to_broadcast([P, MH, L]), ALU.mult)
                    ins.then_inc(s_sw, 1)

                def low_part(c):
                    dve.wait_ge(s_hmh, NC * l + c + 1)
                    V.tensor_tensor(hid_l[:, MH:2 * MH, c * L:(c + 1) * L], hm, f(hid_h[:, MH:2 * MH, c * L:(c + 1) * L]),
                                    ALU.subtract).then_inc(s_hmd, 1)

                weighted(0)
                gate_of(NC, 0)
                fill("a", NC, 0)
                fill("p", 0, 0)
                fill("p", 0, 1)
                gate_of(NC, 1)
                for c in range(NC):
                    a, w = NC * l + c, int(c == SAMPLE)
                    dve.wait_ge(s_dsq, a + 1)
                    dve.wait_ge(s_em, a + 1)
                    V.tensor_tensor(dsq[:], dsq[:], ch(5, 0), ALU.max).then_inc(s_mx, 1)
                    if c > 1:
                        dve.wait_ge(s_st, a)
                    for h in (MH - 1, 0, 1, 2):
                        if h == MH - 1:
                            dve.wait_ge(s_nu, a + 1)
                            new = psum[:, 4, 0:MD + 1]
                        else:
                            if h == 0:
                                dve.wait_ge(s_u, a + 1)
                            new = psum[:, 7, h * (MD + 1):(h + 1) * (MD + 1)]
                        if c == 0:
                            ins = V.tensor_copy(cst[:, 0, h], new)
                        else:
                            ins = V.scalar_tensor_tensor(cst[:, w, h], cst[:, w, h], gT[:, 1, c * MH + h:c * MH + h + 1], new,
                                                         ALU.mult, ALU.add)
                        if h == MH - 1:
                            ins.then_inc(s_nn, 1)
                    ins.then_inc(s_st, 1)
                    if c:
                        low_part(c - 1)
                    fill("m", c, 0)
                    dve.wait_ge(s_ssm, a + 1)
                    dve.wait_ge(s_mx, a + 1)
                    V.scalar_tensor_tensor(m2, ch(6, 0), 1.0 / MD, dsq[:], ALU.mult, ALU.add).then_inc(s_s2, 1)
                    if c < SAMPLE:
                        weighted(c + 1)
                    dve.wait_ge(s_rs, a + 1)
                    link(V.scalar_tensor_tensor(r2, r2, -1.0, m2, ALU.mult, ALU.mult))
                    link(V.scalar_tensor_tensor(rstd[:], r2, 1.5, rstd[:], ALU.add, ALU.mult))
                    link(V.tensor_tensor(rstd[:], rstd[:], z[:, 12:16, c * L:(c + 1) * L], ALU.mult))
                    V.tensor_tensor(hm, z[:, 4:8, c * L:(c + 1) * L], rstd[:], ALU.mult).then_inc(s_hm, 1)
                    fill("m", c, 1)
                low_part(NC - 1)
                for w in range(2):
                    dve.wait_ge(s_ct, 2 * (l + 1))
                    V.tensor_copy(cout[:, w, :], psum[:, 6 + w, :])
                    V.tensor_copy(kout[0:MH, w, :], psum[0:MH, 4, w * P:(w + 1) * P]).then_inc(s_co, 1)
                fill("m", NC, 0)
                for s in range(S_WOM, S_MLP):
                    for m in range(2):
                        add_x(t0 + tile_of(s) + m, 2 * (s - S_WOM) + m)
                    split(g0 + s + 2)
                    for m in range(2):
                        norm_tile(2 * l + 1, 2 * (s - S_WOM) + m)

                tile_m, slot_m = t0 + S_MLP + 8, g0 + S_MLP
                hid0 = 8 * GROUPS * l
                rms_of(2 * l + 1)

                def mlp_split(j, q):
                    r = ((q + 2) % 4) // 2
                    pick = lambda w: w[:, (slot_m + q) % 2, :].rearrange("p (k c) -> p k c", k=KT)
                    dve.wait_ge(s_hi, slot_m + 3 + j)
                    V.tensor_tensor(pick(w_lo), stage[:, r, :].rearrange("p (k q c) -> p k q c", k=KT, q=2)[:, :, q % 2, :],
                                    f(pick(w_hi)), ALU.subtract).then_inc(s_lo, 1)

                def up_step(g, i, q):
                    j = 16 * g + 4 * i + q
                    n = hid0 + 8 * g + 4 * i + q + 1
                    dve.wait_ge(s_tile, tile_m + 1 + j)
                    V.tensor_tensor(two(tmp[0][:]), acc[(tile_m + q) % 2], two(rms[:]), ALU.mult).then_inc(s_evac, 1)
                    mlp_split(j, q)
                    dve.wait_ge(s_evac, tile_m + 1 + j)
                    V.scalar_tensor_tensor(tmp[1][:], tmp[0][:], 0.0, tmp[0][:], ALU.max, ALU.mult).then_inc(s_hh, 1)
                    dve.wait_ge(s_hidh, n)
                    V.tensor_tensor(hid_l[:, bass.ds(4 * i + q, 1), :], tmp[1][:].rearrange("p (o t) -> p o t", o=1),
                                    f(hid_h[:, bass.ds(4 * i + q, 1), :]), ALU.subtract).then_inc(s_hid, 1)

                with dve.Fori(0, GROUPS - 1) as g:
                    with dve.Fori(0, 2) as i:
                        for q in range(4):
                            up_step(g, i, q)
                    with dve.Fori(0, 2) as i:
                        for q in range(4):
                            j = 16 * g + 8 + 4 * i + q
                            dve.wait_ge(s_tile, tile_m + 1 + j)
                            xt = x[:, bass.ds(4 * i + q, 1), :].rearrange("p o (a t) -> p (o a) t", a=2)
                            V.tensor_tensor(xt, xt, acc[(tile_m + q) % 2], ALU.add).then_inc(s_evac, 1)
                            mlp_split(j, q)
                with dve.Fori(0, 2) as i:
                    for q in range(4):
                        up_step(GROUPS - 1, i, q)
                for k in range(KT):
                    add_x(t0 + TILES - KT + k, k)
                    split(g0 + SLOTS - KT + k + 2)
                    if l < DEPTH - 1:
                        norm_tile(2 * l + 2, k)

            dve.wait_ge(s_r0, 2 * DEPTH + 1)
            link(V.scalar_tensor_tensor(att_s[:, 5:10], att_s[:, 5:10], -1.0, att_s[:, 10:15], ALU.mult, ALU.mult))
            V.scalar_tensor_tensor(att_s[:, 0:5], att_s[:, 5:10], 1.5, att_s[:, 0:5], ALU.add, ALU.mult).then_inc(s_rms, 1)
            dve.wait_ge(s_rms, 2 * DEPTH + 1)
            zf = z[:, :, :].rearrange("p a t -> p (a t)")
            for t in range(5):
                m = P if t < 4 else DEC
                dve.wait_ge(s_yt, (1, 2, 3, 4, 9)[t])
                V.tensor_scalar(zf[0:m, t * DM:t * DM + 512], psum[0:m, 4 + t % 4, :], att_s[0:m, t:t + 1], None,
                                ALU.mult).then_inc(s_yed, 1)

        @block.tensor
        def _(pe):
            M = nc.tensor.matmul
            TR = nc.tensor.transpose
            zf = z[:, :, :].rearrange("p a t -> p (a t)")

            def products(t, lhs, k, first, last, hi_mov, lo_mov):
                ins = None
                for n, (w, mov) in enumerate(((w_hi, hi_mov), (w_hi, lo_mov), (w_lo, hi_mov))):
                    for a in range(2):
                        ins = M(acc[t % 2][:, a, :], lhs(w), mov[:, k, a * HALF:(a + 1) * HALF],
                                start=first and n == 0, stop=last and n == 2)
                return ins

            def sum_squares(n):
                pe.wait_ge(s_sum, n + 1)
                if n == 0:
                    pe.wait_ge(s_sqd, 1)
                    pe.wait_ge(s_x0, KT // 2)
                    pe.wait_ge(s_x0a, KT // 2)
                parts = [ssum[:]] if n else [ssum[:], z[:, 2, :]]
                for a in range(2):
                    for i, part in enumerate(parts):
                        ins = M(psum[:, 4 + a, 0:HALF], ones, part[:, a * HALF:(a + 1) * HALF], start=i == 0,
                                stop=i == len(parts) - 1)
                ins.then_inc(s_ss, 1)

            def unit(l, u):
                s, e = u // 8, u % 8
                g = SLOTS * l + s
                if e == 0:
                    pe.wait_ge(s_lo, g + 1)
                    if s == S_WOA:
                        pe.wait_ge(s_ao, NC * (l + 1))
                    if s == S_WOM:
                        pe.wait_ge(s_hmd, NC * (l + 1))
                if s < S_WOA:
                    t, k, first, last = TILES * l + s, e, e == 0, e == 7
                    if s == 0:
                        pe.wait_ge(s_xl, KT * 2 * l + k + 1)
                    lhs = lambda w: w[:, g % 2, k * P:(k + 1) * P]
                    mov = (xh, xl)
                    kk = k
                else:
                    m, k = e // 4, e % 4
                    t, first, last = TILES * l + tile_of(s) + m, k == 0, k == 3
                    lhs = lambda w: w[:, g % 2, k * 2 * P + m * P:k * 2 * P + (m + 1) * P]
                    mov = (hid_h, hid_l)
                    kk = k + (4 if s >= S_WOM else 0)
                if first and t >= 2:
                    pe.wait_ge(s_evac, t - 1)
                ins = products(t, lhs, kk, first, last, *mov)
                if last:
                    ins.then_inc(s_tile, 1)

            def fill(l, kind, c, i):
                for u in range(*fills[kind, c, i]):
                    unit(l, u)

            pe.wait_ge(s_const, 16)
            pe.wait_ge(s_xin[4], 16)
            for k in range(KT):
                ins = TR(psum[:, 7, k * DEC:(k + 1) * DEC], zf[0:DEC, 4 * DM + k * P:4 * DM + (k + 1) * P], ident[0:DEC, 0:DEC])
            ins.then_inc(s_xT, 1)
            for t in range(4):
                pe.wait_ge(s_xin[t], 16)
                if t == 3:
                    pe.wait_ge(s_xs, 1)
                    pe.wait_ge(s_par, 5 * 16)
                    TR(psum[:, 7, 0:56], zf[0:56, 5 * DM:5 * DM + P], ident[0:56, 0:56]).then_inc(s_xT, 1)
                for k in range(KT - 1):
                    ins = TR(psum[:, k, t * P:(t + 1) * P], zf[:, t * DM + k * P:t * DM + (k + 1) * P], ident)
                    if t == 3:
                        ins.then_inc(s_xT, 1)
            pe.wait_ge(s_gain, 2)
            for t in range(4):
                ins = TR(psum[:, 7, t * P:(t + 1) * P], zf[:, t * DM + (KT - 1) * P:(t + 1) * DM], ident)
            ins.then_inc(s_xT, 1)
            pe.wait_ge(s_x0, 2)
            pe.wait_ge(s_x0a, 2)

            for l in range(DEPTH):
                for u in range(8):
                    unit(l, u)
                sum_squares(2 * l)
                for u in range(8, 8 * S_MK):
                    unit(l, u)
                pe.wait_ge(s_rot, 5 * l + 1)
                pe.wait_ge(s_evac, TILES * l + S_AV + 1)
                pe.wait_ge(s_cl, 16 * 3 * (l + 1))
                pe.wait_ge(s_rms, 2 * l + 1)
                for n in range(8):
                    TR(psum[:, 4 + n // 4 * 2, (n % 4) * P:(n % 4 + 1) * P], vT[:, n * L:n * L + P], ident)
                for h in range(MH):
                    TR(psum[:, 5, h * P:(h + 1) * P], pT1[:, h * P:(h + 1) * P], ident)
                TR(psum[0:L, 7, 0:P], vT[:, SEQ:T], ident)
                TR(psum[:, 7, P:2 * P], kT[:, SEQ - WIN:SEQ], ident)
                TR(psum[0:DEC, 7, 2 * P:3 * P], kT[:, SEQ:T], ident)
                TR(psum[:, 7, 3 * P:4 * P], kraw[:], ident).then_inc(s_set, 1)
                fill(l, "s", 0, 0)
                pe.wait_ge(s_seta, l + 1)
                pe.wait_ge(s_setd, l + 1)
                pe.wait_ge(s_rot, 5 * (l + 1))

                for c in range(NC):
                    a, nk = NC * l + c, keys(c)
                    for j in range(AJ):
                        out = psum[:, 4 + j // 2, (j % 2) * (WIN + L):(j % 2) * (WIN + L) + nk]
                        q = qbd[j // 2][:, j % 2, c].rearrange("p g q -> p (g q)")
                        if c == SAMPLE:
                            M(out[:, 0:WIN], q, kcT[:], start=True, stop=True)
                            ins = M(out[:, WIN:nk], q, kT[:, SEQ:T], start=True, stop=True)
                        else:
                            ins = M(out, q, kT[:, (c + 1) * L - nk:(c + 1) * L], start=True, stop=True)
                    ins.then_inc(s_sc, 1)
                    fill(l, "a", c, 0)
                    pe.wait_ge(s_pn, a + 1)
                    if c == 4:
                        pe.wait_ge(s_gtd, l + 1)
                    if a:
                        pe.wait_ge(s_ao, a)
                    if n_pt1(l, c):
                        pe.wait_ge(s_pt1, n_pt1(l, c))
                    if n_pt2(l, c):
                        pe.wait_ge(s_pt2, n_pt2(l, c))
                    old = nk // P * P
                    for j in range(AJ):
                        if old:
                            ins = TR(psum[:, 6, j * P:(j + 1) * P], prob[:, j, 0:P], ident)
                        if nk != WIN:
                            ins = TR(psum[0:L, 7, j * P:(j + 1) * P], prob[:, j, old:nk], ident)
                    ins.then_inc(s_T, 1)
                    fill(l, "a", c, 1)
                    if old:
                        pe.wait_ge(s_pt1, n_pt1(l, c) + 1)
                        older = vcache[:] if c == SAMPLE else vwin[:, max(c - 2, 0), :]
                        ins = M(psum[:, 6, :], older, pT1[:], start=True, stop=nk == WIN)
                    if nk != WIN:
                        pe.wait_ge(s_pt2, n_pt2(l, c) + 1)
                        ins = M(psum[:, 6, :], vwin[0:L, c, :], pT2[:], start=not old, stop=True)
                    ins.then_inc(s_pv, 1)
                    if c == 3:
                        pe.wait_ge(s_g4, l + 1)
                        for p in range(NP):
                            r = L if p == NP - 1 else P
                            TR(psum[0:r, 7, p * MH:(p + 1) * MH], row(5)[:, p * P:p * P + r], ident[0:MH, 0:MH])
                        M(psum[:, 7, 64:64 + NC * MH], ones[0:MH, :], g9[0:MH, 48:48 + NC * MH], start=True, stop=True).then_inc(s_gt, 1)
                    fill(l, "a", c, 2)

                sel = lambda i: rconst[:, R_SEL + i * P:R_SEL + (i + 1) * P]
                head = lambda i, h: slice(i * MH * L + h * L, i * MH * L + (h + 1) * L)

                def scores(c):
                    p0 = c // 2 * P
                    cs = slice(c * L, (c + 1) * L)
                    if c:
                        pe.wait_ge(s_mx, NC * l + c)
                    M(psum[:, 5, 0:MH * L], rconst[:, R_ID:R_ID + P], rconst[:, R_NEG:R_NEG + MH * L], start=True, stop=False)
                    M(psum[:, 5, 0:MH * L], acl[:, p0:p0 + P], rconst[:, R_ROW:R_ROW + MH * L], start=False, stop=False)
                    for h in range(MH):
                        ins = M(psum[:, 5, head(0, h)], sel(h), ncr[:, cs], start=False, stop=h == MH - 1)
                    ins.then_inc(s_e, 1)
                    if c:
                        pe.wait_ge(s_nn, NC * l + c)
                    r = L if c == SAMPLE else P
                    for h in range(MH):
                        ins = M(psum[0:r, 4, head(0, h)], z[:, h, p0:p0 + r], z[:, 4 + h, cs], start=True, stop=True)
                    if c:
                        for h in range(MH):
                            ins = M(psum[:, 4, head(1, h)], sel(h), bcr[:, cs], start=True, stop=True)
                    ins.then_inc(s_swp, 1)

                def token_major(p, tile, signal):
                    r = L if p == NP - 1 else P
                    for h in range(MH):
                        ins = TR(psum[0:r, 7, h * MD:(h + 1) * MD], z[:, tile + h, p * P:p * P + r], ident)
                    ins.then_inc(signal, 1)

                pe.wait_ge(s_evac, TILES * l + S_MO)
                pe.wait_ge(s_rcon, 1)
                scores(0)
                token_major(0, 0, s_tk)
                fill(l, "a", NC, 0)
                fill(l, "p", 0, 0)
                pe.wait_ge(s_kev, NP * l + 1)
                pe.wait_ge(s_evac, TILES * l + S_WOA)
                token_major(0, 8, s_tv)
                fill(l, "p", 0, 1)
                pe.wait_ge(s_ao, NC * (l + 1))
                for c in range(NC):
                    a, w, pair = NC * l + c, int(c == SAMPLE), NP * l + c // 2
                    cs, q = slice(c * L, (c + 1) * L), slice((c % 2) * L, (c % 2 + 1) * L)
                    pe.wait_ge(s_sw, a + 1)
                    pe.wait_ge(s_vev, pair + 1)
                    if c:
                        pe.wait_ge(s_st, a)
                        pe.wait_ge(s_s2, a)
                    for h in range(MH):
                        M(psum[:, 6, head(0, h)], vtok[q, h], sw[q, h], start=True, stop=c == 0)
                        if c:
                            M(psum[:, 6, head(0, h)], cst[:, w, h, 0:MD], qw[:, h], start=False, stop=True)
                    for h in range(MH):
                        ins = M(psum[:, 5, head(0, h)], sel(MH + h), bcr[:, cs], start=True, stop=True)
                    ins.then_inc(s_em, 1)
                    if c:
                        pe.wait_ge(s_dn, (NC - 1) * l + c)
                    den = nq[:] if c else sw[q]
                    M(psum[:, 6, MH * L:2 * MH * L], ones[0:P if c else L, :], den.rearrange("p h t -> p (h t)"),
                      start=True, stop=True).then_inc(s_nd, 1)
                    pe.wait_ge(s_kev, pair + 1)
                    pe.wait_ge(s_wv, pair + 1)
                    M(psum[:, 4, 0:MD + 1], ktok[q, MH - 1], wsv[q, MH - 1], start=True, stop=True).then_inc(s_nu, 1)
                    for h in range(MH - 1):
                        ins = M(psum[:, 7, h * (MD + 1):(h + 1) * (MD + 1)], ktok[q, h], wsv[q, h], start=True, stop=True)
                    ins.then_inc(s_u, 1)
                    fill(l, "m", c, 0)
                    pe.wait_ge(s_hsq, a + 1)
                    M(psum[:, 6, 0:MH * L], ones, hsq[:].rearrange("p h t -> p (h t)"), start=True, stop=True).then_inc(s_ssm, 1)
                    if c < SAMPLE:
                        scores(c + 1)
                        if c % 2:
                            pe.wait_ge(s_st, a + 1)
                            token_major((c + 1) // 2, 8, s_tv)
                    fill(l, "m", c, 1)
                    if c < SAMPLE and c % 2:
                        pe.wait_ge(s_vev, pair + 2)
                        token_major((c + 1) // 2, 0, s_tk)
                pe.wait_ge(s_st, NC * (l + 1))
                pe.wait_ge(s_s2, NC * (l + 1))
                for w in range(2):
                    for h in range(MH):
                        TR(psum[:, 6 + w, h * P:(h + 1) * P], cst[:, w, h, 0:MD], ident)
                    TR(psum[0:MH, 4, w * P:(w + 1) * P], cst[:, w, :, MD], ident).then_inc(s_ct, 1)
                fill(l, "m", NC, 0)
                for u in range(8 * S_WOM, 8 * S_MLP):
                    unit(l, u)

                tile_m, slot_m, hid0 = TILES * l + S_MLP + 8, SLOTS * l + S_MLP, 8 * GROUPS * l

                def mlp_slot(g, down, i, q, first_slot=False):
                    j = 16 * g + 8 * down + 4 * i + q
                    pe.wait_ge(s_lo, slot_m + 1 + j)
                    pe.wait_ge(s_evac, tile_m - 1 + j)
                    for k in range(KT):
                        if first_slot:
                            pe.wait_ge(s_xl, KT * (2 * l + 1) + k + 1)
                        if down and q == 0:
                            pe.wait_ge(s_hid, hid0 + 8 * g + k + 1)
                        lhs = lambda w: w[:, (slot_m + q) % 2, k * P:(k + 1) * P]
                        mov = (hid_h, hid_l) if down else (xh, xl)
                        ins = products(tile_m + q, lhs, k, k == 0, k == KT - 1, *mov)
                    ins.then_inc(s_tile, 1)

                for j in range(KT):
                    mlp_slot(0, 0, j // 4, j % 4, j == 0)
                    if j == 0:
                        pe.wait_ge(s_co, 2 * (l + 1))
                        sum_squares(2 * l + 1)
                with pe.Fori(0, 2) as i:
                    for q in range(4):
                        mlp_slot(0, 1, i, q)
                with pe.Fori(1, GROUPS) as g:
                    for down in range(2):
                        with pe.Fori(0, 2) as i:
                            for q in range(4):
                                mlp_slot(g, down, i, q)

            def turn(t, half, bank):
                m = P if t < 4 else DEC
                for k in range(4):
                    ins = TR(psum[0:m, bank, k * P:(k + 1) * P], xg[:, half * 4 + k, t * P:t * P + m], ident)
                ins.then_inc(s_yt, 1)

            pe.wait_ge(s_xg, 4)
            for t in range(4):
                turn(t, 0, 4 + t)
            pe.wait_ge(s_xg, KT)
            pe.wait_ge(s_evac, TILES * DEPTH)
            turn(0, 1, 0)
            turn(1, 1, 1)
            pe.wait_ge(s_sum, 2 * DEPTH + 1)
            for t in range(4):
                M(psum[:, 3, t:t + 1], ssum[:, t * P:(t + 1) * P], ones[:, 0:1], start=True, stop=True)
            for q in range(2):
                ins = M(psum[q * DEC:(q + 1) * DEC, 3, 4:5], ssum[:, SEQ:T], ones[:, 0:1], start=True, stop=True)
            ins.then_inc(s_ss, 1)
            turn(2, 1, 2)
            pe.wait_ge(s_r0, 2 * DEPTH + 1)
            turn(3, 1, 3)
            pe.wait_ge(s_yed, 1)
            turn(4, 0, 4)
            pe.wait_ge(s_yea, 1)
            turn(4, 1, 0)


def norm_rows(g):
    return g.rearrange("l (k p) -> (l k) p", p=P)


_INS = ["x_prompt", "x_sample", "cache_k", "cache_v", "state_C", "state_n", "state_m", "norm1_g", "w_in", "gate_b",
        "attn_sink", "mnorm_g", "w_out", "norm2_g", "w_up", "w_down", "final_g"]
_OUTS = [(1, SEQ, DM), (1, DEC, DM)] + [(DEPTH, 1, WIN, AG, AD)] * 2 + [
    (DEPTH, 1, MH, MD, MD), (DEPTH, 1, MH, MD), (DEPTH, 1, MH)] + [(DEPTH, 1, DEC, AG, AD)] * 2 + [
    (DEPTH, 1, MH, MD, MD), (DEPTH, 1, MH, MD), (DEPTH, 1, MH)]


def kernel(**inputs):
    import numpy as _np
    import concourse.bacc as _bacc
    from concourse.bass_utils import run_bass_kernel_spmd as _run

    nc = _bacc.Bacc("TRN2", target_bir_lowering=False, num_devices=1)
    arrays = {f"in_{name}": _np.ascontiguousarray(inputs[name]) for name in _INS}
    arrays["in_const"] = constants()
    ins = [nc.dram_tensor(name, a.shape, F32, kind="ExternalInput").ap() for name, a in arrays.items()]
    outs = [nc.dram_tensor(f"out_{i}", shape, F32, kind="ExternalOutput").ap() for i, shape in enumerate(_OUTS)]
    hymba_step(nc, ins, outs)
    r = _run(nc, [arrays], core_ids=[0])
    return tuple(r.results[0][f"out_{i}"] for i in range(len(_OUTS)))
```
